# Optimizing a Trainium2 kernel written in Bass

```python
import math
import jax, jax.numpy as jnp
from jax import lax
import numpy as np

D_MODEL = 1024
BATCH = 1
SEQ = 512
DEPTH = 1
DEC_BATCH = 8
DEC_SEQ = 1
PAST_LEN = 4096
PAGE_SIZE = 128

D_MIX = D_MODEL
C_CONV = D_MIX // 2
C_SSM = D_MIX - C_CONV
CONV_WIDTH = 31
SSM_GROUP = 16
SSM_GROUPS = C_SSM // SSM_GROUP
SSM_STATE = 64
PEER_HEADS = 8
N_KEYS = 128
N_EXPERTS = N_KEYS * N_KEYS
PEER_TOPK = 16
D_KEY = 128
PEER_BLOCK = 128
EPS = 1e-6
DT_MIN = 1e-3
DT_MAX = 1e-1

kernel_name = "hybrid_conv_s5_peer_adaln_step"

def rms_norm(x, g):
    x32 = x.astype(jnp.float32)
    y = x32 * lax.rsqrt(jnp.mean(x32 * x32, axis=-1, keepdims=True) + EPS)
    return (y * g.astype(jnp.float32)).astype(x.dtype)

def layer_norm(x, g, b):
    x32 = x.astype(jnp.float32)
    xc = x32 - jnp.mean(x32, axis=-1, keepdims=True)
    y = xc * lax.rsqrt(jnp.mean(xc * xc, axis=-1, keepdims=True) + EPS)
    return (y * g.astype(jnp.float32) + b.astype(jnp.float32)).astype(x.dtype)

def ada_mod(c, w, b):
    return jax.nn.silu(c) @ w + b

def modulate(h, shift, scale):
    return h * (1.0 + scale[:, None, :]) + shift[:, None, :]

def causal_depthwise_conv(h, buf, w, b):
    full = jnp.concatenate([buf.astype(h.dtype), h], axis=1)
    out = lax.conv_general_dilated(
        full, w[:, None, :].astype(h.dtype), window_strides=(1,), padding='VALID',
        dimension_numbers=('NWC', 'WIO', 'NWC'), feature_group_count=h.shape[-1])
    return out + b.astype(h.dtype), full[:, -(CONV_WIDTH - 1):]

def ssm_discretize(lam_re, lam_im, log_dt, b_re, b_im):
    lr = lam_re.astype(jnp.float32)
    li = lam_im.astype(jnp.float32)
    dt = jnp.exp(log_dt.astype(jnp.float32))[:, None]
    mag = jnp.exp(lr * dt)
    ang = li * dt
    ar = mag * jnp.cos(ang)
    ai = mag * jnp.sin(ang)
    den = lr * lr + li * li
    cr = ((ar - 1.0) * lr + ai * li) / den
    ci = (ai * lr - (ar - 1.0) * li) / den
    br = b_re.astype(jnp.float32)
    bi = b_im.astype(jnp.float32)
    bbar_re = cr[..., None] * br - ci[..., None] * bi
    bbar_im = cr[..., None] * bi + ci[..., None] * br
    return ar, ai, bbar_re, bbar_im

def _ssm_combine(e1, e2):
    a1r, a1i, b1r, b1i = e1
    a2r, a2i, b2r, b2i = e2
    return (a1r * a2r - a1i * a2i,
            a1r * a2i + a1i * a2r,
            a2r * b1r - a2i * b1i + b2r,
            a2r * b1i + a2i * b1r + b2i)

def s5_mixer(u, h0_re, h0_im, lam_re, lam_im, log_dt, b_re, b_im, c_re, c_im, d_skip, w_glu):
    bsz, seqlen, _ = u.shape
    u32 = u.astype(jnp.float32)
    ug = u32.reshape(bsz, seqlen, SSM_GROUPS, SSM_GROUP)
    ar, ai, bbr, bbi = ssm_discretize(lam_re, lam_im, log_dt, b_re, b_im)
    xr = jnp.einsum('blgp,gnp->blgn', ug, bbr)
    xi = jnp.einsum('blgp,gnp->blgn', ug, bbi)
    h0r = h0_re.astype(jnp.float32)
    h0i = h0_im.astype(jnp.float32)
    xr = xr.at[:, 0].add(ar * h0r - ai * h0i)
    xi = xi.at[:, 0].add(ar * h0i + ai * h0r)
    arb = jnp.broadcast_to(ar, xr.shape)
    aib = jnp.broadcast_to(ai, xr.shape)
    _, _, hr, hi = lax.associative_scan(_ssm_combine, (arb, aib, xr, xi), axis=1)
    y = (jnp.einsum('blgn,gpn->blgp', hr, c_re.astype(jnp.float32))
         - jnp.einsum('blgn,gpn->blgp', hi, c_im.astype(jnp.float32)))
    y = y.reshape(bsz, seqlen, C_SSM) + d_skip.astype(jnp.float32) * u32
    z = jax.nn.gelu(y)
    out = z * jax.nn.sigmoid(z @ w_glu.astype(jnp.float32))
    return out.astype(u.dtype), hr[:, -1], hi[:, -1]

def peer_ffn(h, w_q, keys, u_tab, v_tab):
    bsz, seqlen, dm = h.shape
    t = bsz * seqlen
    x = h.reshape(t, dm)
    q = (x @ w_q).astype(jnp.float32).reshape(t, PEER_HEADS, 2, D_KEY // 2)
    s = jnp.einsum('thsk,hsnk->thsn', q, keys.astype(jnp.float32))
    s1, i1 = lax.top_k(s[:, :, 0], PEER_TOPK)
    s2, i2 = lax.top_k(s[:, :, 1], PEER_TOPK)
    cand_s = (s1[..., :, None] + s2[..., None, :]).reshape(t, PEER_HEADS, PEER_TOPK * PEER_TOPK)
    cand_i = (i1[..., :, None] * N_KEYS + i2[..., None, :]).reshape(t, PEER_HEADS, PEER_TOPK * PEER_TOPK)
    top_s, pos = lax.top_k(cand_s, PEER_TOPK)
    idx = jnp.take_along_axis(cand_i, pos, axis=-1)
    g = jax.nn.softmax(top_s, axis=-1)
    nsel = PEER_HEADS * PEER_TOPK
    idx = idx.reshape(t, nsel)
    g = g.reshape(t, nsel).astype(h.dtype)
    pad = (-t) % PEER_BLOCK
    nb = (t + pad) // PEER_BLOCK
    xp = jnp.pad(x, ((0, pad), (0, 0))).reshape(nb, PEER_BLOCK, dm)
    ip = jnp.pad(idx, ((0, pad), (0, 0))).reshape(nb, PEER_BLOCK, nsel)
    gp = jnp.pad(g, ((0, pad), (0, 0))).reshape(nb, PEER_BLOCK, nsel)

    def block(args):
        xb, ib, gb = args
        ub = jnp.take(u_tab, ib, axis=0)
        vb = jnp.take(v_tab, ib, axis=0)
        act = jax.nn.gelu(jnp.einsum('tkd,td->tk', ub, xb))
        return jnp.einsum('tk,tkd->td', gb * act, vb)

    out = lax.map(block, (xp, ip, gp))
    return out.reshape(nb * PEER_BLOCK, dm)[:t].reshape(bsz, seqlen, dm)

def trunk_layer(x, c, conv_buf, h0_re, h0_im, lp):
    (norm1_g, norm2_g, w_ada, b_ada, w_in, conv_w, conv_b, conv_ln_g, conv_ln_b,
     lam_re, lam_im, log_dt, b_re, b_im, c_re, c_im, d_skip, w_glu, w_out,
     peer_w_q, peer_keys, peer_u, peer_v) = lp
    sh1, sc1, g1, sh2, sc2, g2 = jnp.split(ada_mod(c, w_ada, b_ada), 6, axis=-1)
    h = modulate(rms_norm(x, norm1_g), sh1, sc1)
    z = h @ w_in
    a = z[..., :C_CONV]
    gate = z[..., C_CONV:2 * C_CONV]
    u = z[..., 2 * C_CONV:]
    hc = a * jax.nn.sigmoid(gate)
    hc, new_buf = causal_depthwise_conv(hc, conv_buf, conv_w, conv_b)
    hc = jax.nn.silu(layer_norm(hc, conv_ln_g, conv_ln_b))
    hs, hT_re, hT_im = s5_mixer(u, h0_re, h0_im, lam_re, lam_im, log_dt, b_re, b_im,
                                c_re, c_im, d_skip, w_glu)
    mix = jnp.concatenate([hc, hs.astype(hc.dtype)], axis=-1) @ w_out
    x = x + g1[:, None, :] * mix
    h2 = modulate(rms_norm(x, norm2_g), sh2, sc2)
    x = x + g2[:, None, :] * peer_ffn(h2, peer_w_q, peer_keys, peer_u, peer_v)
    return x, new_buf, hT_re, hT_im

def setup_inputs(seed: int = 0) -> dict:
    key = jax.random.key(seed)
    ks = list(jax.random.split(key, 40))
    f32 = jnp.float32

    def nrm(k, shape, scale):
        return jax.random.normal(k, shape, f32) * scale

    n_idx = jnp.arange(SSM_STATE, dtype=f32)
    lam_re = -0.5 + nrm(ks[0], (DEPTH, SSM_GROUPS, SSM_STATE), 0.01)
    lam_im = math.pi * n_idx[None, None, :] + nrm(ks[1], (DEPTH, SSM_GROUPS, SSM_STATE), 0.01)
    log_dt = jax.random.uniform(ks[2], (DEPTH, SSM_GROUPS), f32, math.log(DT_MIN), math.log(DT_MAX))
    return {
        "x_prompt": nrm(ks[3], (BATCH, SEQ, D_MODEL), 1.0),
        "x_sample": nrm(ks[4], (DEC_BATCH, DEC_SEQ, D_MODEL), 1.0),
        "state_conv": nrm(ks[5], (DEPTH, DEC_BATCH, CONV_WIDTH - 1, C_CONV), 0.5),
        "state_ssm_re": nrm(ks[6], (DEPTH, DEC_BATCH, SSM_GROUPS, SSM_STATE), 0.1),
        "state_ssm_im": nrm(ks[7], (DEPTH, DEC_BATCH, SSM_GROUPS, SSM_STATE), 0.1),
        "c_prompt": nrm(ks[8], (BATCH, D_MODEL), 1.0),
        "c_sample": nrm(ks[9], (DEC_BATCH, D_MODEL), 1.0),
        "norm1_g": 1.0 + nrm(ks[10], (DEPTH, D_MODEL), 0.02),
        "norm2_g": 1.0 + nrm(ks[11], (DEPTH, D_MODEL), 0.02),
        "w_ada": nrm(ks[12], (DEPTH, D_MODEL, 6 * D_MODEL), 0.5 * D_MODEL ** -0.5),
        "b_ada": nrm(ks[13], (DEPTH, 6 * D_MODEL), 0.01),
        "w_in": nrm(ks[14], (DEPTH, D_MODEL, 2 * C_CONV + C_SSM), D_MODEL ** -0.5),
        "conv_w": nrm(ks[15], (DEPTH, CONV_WIDTH, C_CONV), CONV_WIDTH ** -0.5),
        "conv_b": nrm(ks[16], (DEPTH, C_CONV), 0.01),
        "conv_ln_g": 1.0 + nrm(ks[17], (DEPTH, C_CONV), 0.02),
        "conv_ln_b": nrm(ks[18], (DEPTH, C_CONV), 0.01),
        "ssm_lambda_re": lam_re,
        "ssm_lambda_im": lam_im,
        "ssm_log_dt": log_dt,
        "ssm_b_re": nrm(ks[19], (DEPTH, SSM_GROUPS, SSM_STATE, SSM_GROUP), (2 * SSM_GROUP) ** -0.5),
        "ssm_b_im": nrm(ks[20], (DEPTH, SSM_GROUPS, SSM_STATE, SSM_GROUP), (2 * SSM_GROUP) ** -0.5),
        "ssm_c_re": nrm(ks[21], (DEPTH, SSM_GROUPS, SSM_GROUP, SSM_STATE), SSM_STATE ** -0.5),
        "ssm_c_im": nrm(ks[22], (DEPTH, SSM_GROUPS, SSM_GROUP, SSM_STATE), SSM_STATE ** -0.5),
        "ssm_d": nrm(ks[23], (DEPTH, C_SSM), 1.0),
        "ssm_w_glu": nrm(ks[24], (DEPTH, C_SSM, C_SSM), C_SSM ** -0.5),
        "w_out": nrm(ks[25], (DEPTH, D_MIX, D_MODEL), D_MIX ** -0.5),
        "peer_w_q": nrm(ks[26], (DEPTH, D_MODEL, PEER_HEADS * D_KEY), D_MODEL ** -0.5),
        "peer_keys": nrm(ks[27], (DEPTH, PEER_HEADS, 2, N_KEYS, D_KEY // 2), (D_KEY // 2) ** -0.5),
        "peer_u": nrm(ks[28], (DEPTH, N_EXPERTS, D_MODEL), D_MODEL ** -0.5),
        "peer_v": nrm(ks[29], (DEPTH, N_EXPERTS, D_MODEL), PEER_HEADS ** -0.5),
        "final_norm_g": 1.0 + nrm(ks[30], (D_MODEL,), 0.02),
        "w_ada_final": nrm(ks[31], (D_MODEL, 2 * D_MODEL), 0.5 * D_MODEL ** -0.5),
        "b_ada_final": nrm(ks[32], (2 * D_MODEL,), 0.01),
    }

def reference(x_prompt, x_sample, state_conv, state_ssm_re, state_ssm_im, c_prompt, c_sample,
              norm1_g, norm2_g, w_ada, b_ada, w_in, conv_w, conv_b, conv_ln_g, conv_ln_b,
              ssm_lambda_re, ssm_lambda_im, ssm_log_dt, ssm_b_re, ssm_b_im, ssm_c_re, ssm_c_im,
              ssm_d, ssm_w_glu, w_out, peer_w_q, peer_keys, peer_u, peer_v,
              final_norm_g, w_ada_final, b_ada_final):
    def run(x, c, conv_bufs, h_re, h_im):
        new_conv, new_re, new_im = [], [], []
        for l in range(DEPTH):
            lp = (norm1_g[l], norm2_g[l], w_ada[l], b_ada[l], w_in[l], conv_w[l], conv_b[l],
                  conv_ln_g[l], conv_ln_b[l], ssm_lambda_re[l], ssm_lambda_im[l], ssm_log_dt[l],
                  ssm_b_re[l], ssm_b_im[l], ssm_c_re[l], ssm_c_im[l], ssm_d[l], ssm_w_glu[l],
                  w_out[l], peer_w_q[l], peer_keys[l], peer_u[l], peer_v[l])
            x, nb, nr, ni = trunk_layer(x, c, conv_bufs[l], h_re[l], h_im[l], lp)
            new_conv.append(nb)
            new_re.append(nr)
            new_im.append(ni)
        shift, scale = jnp.split(ada_mod(c, w_ada_final, b_ada_final), 2, axis=-1)
        y = modulate(rms_norm(x, final_norm_g), shift, scale)
        return y, jnp.stack(new_conv), jnp.stack(new_re), jnp.stack(new_im)

    bp = x_prompt.shape[0]
    zero_conv = jnp.zeros((DEPTH, bp, CONV_WIDTH - 1, C_CONV), x_prompt.dtype)
    zero_h = jnp.zeros((DEPTH, bp, SSM_GROUPS, SSM_STATE), jnp.float32)
    y_prompt, conv_p, re_p, im_p = run(x_prompt, c_prompt, zero_conv, zero_h, zero_h)
    y_sample, conv_s, re_s, im_s = run(x_sample, c_sample, state_conv, state_ssm_re, state_ssm_im)
    return (y_prompt, y_sample, conv_p, conv_s, re_p, im_p, re_s, im_s)


_drawn_inputs = setup_inputs


def setup_inputs(seed=0):
    import zlib

    import numpy as np

    out = dict(_drawn_inputs(seed))
    spreads = {}
    factors = {'norm1_g': 2.803,
     'norm2_g': 7.044,
     'conv_b': 8.0,
     'conv_ln_g': 8.0,
     'conv_ln_b': 26.388,
     'ssm_lambda_re': 13.249,
     'ssm_c_re': 7.624,
     'ssm_c_im': 7.022,
     'final_norm_g': 7.666,
     'b_ada_final': 4.18}
    for name, (base, spread) in spreads.items():
        noise = np.random.default_rng([zlib.crc32(name.encode()), seed]).standard_normal(out[name].shape)
        drawn = base * np.exp(spread * noise) if base else spread * noise
        out[name] = __import__('jax').numpy.asarray(drawn.astype(out[name].dtype))
    for name, factor in factors.items():
        out[name] = (out[name] * factor).astype(out[name].dtype)
    return out
```

```python
from contextlib import ExitStack

import concourse.bass as bass
from concourse import mybir

F32 = mybir.dt.float32
F32R = mybir.dt.float32r
U32 = mybir.dt.uint32
I32 = mybir.dt.int32
ALU = mybir.AluOpType
ACT = mybir.ActivationFunctionType
AX = mybir.AxisListType

P = 128
D = 1024
KD = D // P
TP, TS = 512, 8
T = TP + TS
L = 8
NC = TP // L
HALVES = ((0, TP // 2), (TP // 2, T))
CC = 512
CT = CC // P
CW = 31
SG, SQ, SN = 32, 16, 64
ST = SG * SN // P
HEADS, NK, TOPK, DK = 8, 128, 16, 64
NSEL = HEADS * TOPK
TT = 104
NTT = T // TT
EPS = 1e-6
NRAW = 4
RAW = 1024
JB = 8
NB = NK // JB
A1 = 64
TOK = 8
GBLK = 16
HR = 2
NSMALL = 13
NMOD = 64
SH1, SC1, G1, SH2, SC2, G2, SHF, SCF = (8 * i for i in range(8))
INV2PI = 0.15915494309189535
TWO_PI_HI = 6.28125
TWO_PI_LO = 2 * 3.141592653589793 - 6.28125
MAGIC = 12582912.0
LOG2E = 1.4426950408889634
LN2_HI = 0.693359375
LN2_LO = -2.12194440e-4
PI_IN = 3.1415925
NEG = -3.0e38

PAIR = 16

STREAM = ([("ada", f) for f in range(PAIR)]
          + [("in", f) for f in (8, 9, 10, 11, 0, 4, 1, 5, 2, 6, 3, 7)]
          + [("ada", f) for f in range(PAIR, 2 * PAIR)]
          + [("glu", f) for f in range(4)]
          + [("ada", f) for f in range(2 * PAIR, 3 * PAIR)]
          + [("out", f) for f in range(8)]
          + [("ada", f) for f in range(3 * PAIR, 4 * PAIR)]
          + [("q", f) for f in range(8)])
NPRE = len(STREAM)
assert NPRE % NRAW == 0
FIRST = {}
ADA = [STREAM.index(("ada", PAIR * p)) for p in range(4)]
for _n, (_kind, _f) in enumerate(STREAM):
    FIRST.setdefault(_kind, _n)



def after(eng, sem, value):
    if isinstance(value, int) and value <= 0:
        return
    eng.wait_ge(sem, value)


def build(nc, dr, out):
    with ExitStack() as base:
        def sb(stack, name, shape, dt=F32):
            return stack.enter_context(nc.sbuf_tensor(name, shape, dt))

        def sem(name):
            return base.enter_context(nc.semaphore(name))

        hd = nc.dram_tensor("act_spill", [NK, P, T], F32, kind="Internal").ap()
        gpd = nc.dram_tensor("gate_spill", [NB, P, TP // GBLK, JB * GBLK], F32, kind="Internal").ap()
        gsd = nc.dram_tensor("gate_sample_spill", [NB, P, JB * TS], F32, kind="Internal").ap()
        ud = nc.dram_tensor("u_shuffle", [SG, SQ, L, NC], F32, kind="Internal").ap()
        usd = nc.dram_tensor("u_sample_shuffle", [SG, SQ, TS], F32, kind="Internal").ap()
        yd = nc.dram_tensor("y_shuffle", [SG, SQ, L, NC], F32, kind="Internal").ap()
        ysd = nc.dram_tensor("y_sample_shuffle", [SG, SQ, TS], F32, kind="Internal").ap()

        x = sb(base, "x_res", [P, KD, T])
        mods = sb(base, "mods", [P, NMOD, 1 + TS])
        gsc = sb(base, "gsc", [P, 3, KD, 1 + TS])
        bada = sb(base, "bada_sb", [P, NMOD])
        ngain = sb(base, "ngain_sb", [P, 3, KD])
        ones = sb(base, "ones", [P, P])
        ident = sb(base, "ident", [P, P])
        iota = sb(base, "iota", [P, P])
        rstd = sb(base, "rstd", [P, T])
        sq = sb(base, "sq", [P, 2, T])
        smalls = sb(base, "smalls", [P, KD, TS])
        sil = sb(base, "sil", [P, KD, 1 + TS])
        adaR = sb(base, "adaR", [32 + 1 + TS, RAW])
        raw = sb(base, "raw", [P, NRAW, RAW])

        ps = base.enter_context(nc.psum_tensor("ps", [P, 8, 512], F32))

        with ExitStack() as s5:
            h1 = sb(s5, "h1", [P, KD, T])
            mixin = sb(s5, "mixin", [P, KD, T])
            uT = sb(s5, "uT", [P, CT, T])
            FO = sb(s5, "FO", [P, 2, ST, L, SQ])
            ET = sb(s5, "ET", [P, 2, ST, P])
            Tm = sb(s5, "Tm", [P, SG, P])
            U = sb(s5, "U", [P, SG, NC + 2 * TS])
            S = sb(s5, "S", [P, 2, ST, NC + TS])
            ssp = sb(s5, "ssp", [P, 2, ST])
            hc = sb(s5, "hc", [P, CT, CW - 1 + TP])
            stc = sb(s5, "stc_sb", [P, CT, TS, CW])
            cw = sb(s5, "cw_sb", [P, CT, CW])
            cvec = sb(s5, "cvec_sb", [P, 4, CT])
            cT = sb(s5, "cT_sb", [P, KD, 1 + TS])
            par = sb(s5, "par_sb", [P, 3, ST])
            bm = sb(s5, "bm_sb", [P, 2, ST, SQ])
            cm = sb(s5, "cm_sb", [P, 2, ST, SQ])
            h0 = sb(s5, "h0_sb", [P, 2, ST, TS])
            Bb = sb(s5, "Bb", [P, 2, ST, SQ])
            Cbd = sb(s5, "Cbd", [P, 2, ST, 2, SQ])
            PW = sb(s5, "PW", [P, 2, ST, L + 1])
            PR = sb(s5, "PR", [P, 2, ST, L + 1])
            K = sb(s5, "K", [P, 40, ST])
            ki = sb(s5, "ki", [P, ST], I32)
            ssn = sb(s5, "ssn", [P, 2, ST, TS])
            with ExitStack() as xs:
                XI = sb(xs, "XI", [P, ST, 2 * L - 1, SQ])
            with ExitStack() as vs:
                V = sb(vs, "V", [P, 2, ST, NC + 2 * TS])
                wt = sb(vs, "wt", [P, ST, NC])
        flat = mixin[:, :, :].rearrange("p k t -> p (k t)")
        XR = flat[:, 0:ST * (2 * L - 1) * SQ].rearrange("p (t m q) -> p t m q", t=ST, q=SQ)
        R = flat[:, 0:2 * ST * NC].rearrange("p (a t c) -> p a t c", a=2, t=ST)
        W2 = flat[:, 2 * ST * NC:4 * ST * NC].rearrange("p (a t c) -> p a t c", a=2, t=ST)
        W2f = flat[:, 2 * ST * NC:4 * ST * NC].rearrange("p (a n) -> p a n", a=2)
        xt = hc[:, :, :].rearrange("p a n -> p (a n)")[:, 0:ST * L * SQ].rearrange(
            "p (t m q) -> p t m q", t=ST, q=SQ)
        Ysb = ET[:, :, :, :].rearrange("p a t n -> p (a t n)")[:, 0:SG * (NC + TS)].rearrange(
            "p (g c) -> p g c", g=SG)
        yT = h1[:, 0:CT, :]
        cv = h1[:, CT:2 * CT, :]
        MQ = (2 * L - 1) * SQ
        Kt = h1[:, 0:2, :].rearrange("p k t -> p (k t)")[:, 0:ST // 4 * MQ].rearrange("p (n m) -> p n m", m=MQ)

        with ExitStack() as tk:
            hl = sb(tk, "hl", [P, 2, 2, RAW], F32R)
            actr = sb(tk, "actr", [P, HR, T])
            with ExitStack() as tp:
                h2 = sb(tp, "h2", [P, 2, KD, T], F32R)
                ohA = sb(tp, "ohA", [P, 4, P], F32R)
                ohB = sb(tp, "ohB", [P, 4, 2, P], F32R)
                sc = sb(tp, "sc", [P, NTT, 2 * HEADS, NK])
                with ExitStack() as qs:
                    h2f = sb(qs, "h2f", [P, KD, T])
                    qT = sb(qs, "qT", [P, HEADS, T])
                    keys = sb(qs, "keys_sb", [P, HEADS, NK])
                with ExitStack() as ts_:
                    wk = sb(ts_, "wk", [P, 2 * NK])
                    v16 = sb(ts_, "v16", [P, HEADS, 2, TOPK])
                    i16 = sb(ts_, "i16", [P, HEADS, 2, TOPK], U32)
                    i16f = sb(ts_, "i16f", [P, HEADS, 2, TOPK])
                    cand = sb(ts_, "cand", [P, HEADS, TOPK, TOPK])
                    pos = sb(ts_, "pos", [P, NSEL], U32)
                    rr = sb(ts_, "rr", [P, 2, NSEL], U32)
                    rf = sb(ts_, "rf", [P, 2, NSEL])
                    eq = sb(ts_, "eq", [P, NSEL, TOPK])
                    selv = sb(ts_, "selv", [P, NTT, 3, NSEL])
                    rs = sb(ts_, "rs", [P, 2, NTT * HEADS])
                    selT = sb(ts_, "selT", [P, 3, T])
                    gp = sb(ts_, "gp", [P, 2, T], F32R)
                    stage = sb(ts_, "stage", [P, 2, NK, GBLK])
                    stages = sb(ts_, "stages", [P, NK, TS])
            with ExitStack() as cs:
                WHL = sb(cs, "WHL", [P, 2, 2, JB, T], F32R)
                wf = sb(cs, "wf", [P, 2, T])
                gbp = sb(cs, "gbp", [P, 2, TP // GBLK, JB, GBLK])
                gbs = sb(cs, "gbs", [P, 2, JB, TS])
                hring = sb(cs, "hring", [P, 4, T])
        yo = gbp[:, :, :, :, :].rearrange("p a k j t -> p (a k j t)")[:, 0:KD * T].rearrange(
            "p (k t) -> p k t", k=KD)

        s_small = sem("small_inputs_loaded")
        s_xl = sem("x_loaded")
        s_raw = [sem(f"weight_tile_loaded_{i}") for i in range(NRAW)]
        s_const = sem("constants_written")
        s_sil = sem("silu_c_ready")
        s_sq = sem("square_ready")
        s_squ = sem("square_used")
        s_stat = sem("column_sums_ready")
        s_rec = sem("reciprocal_ready")
        s_rstd = sem("rstd_ready")
        s_hs = sem("normed_scaled")
        s_h = sem("normed_shifted")
        s_mod = sem("modulation_tile_summed")
        s_ade = sem("modulation_rows_copied")
        s_adt = sem("modulations_transposed")
        s_mods = sem("modulations_ready")
        s_win = sem("input_projection_ready")
        s_uev = sem("u_copied")
        s_sig = sem("gate_sigmoid_ready")
        s_hc = sem("glu_rows_ready")
        s_ush = sem("u_stored")
        s_ul = sem("u_chunks_loaded")
        s_v = sem("vector_chain")
        s_p = sem("pool_chain")
        s_a = sem("scalar_chain")
        s_trig_in = sem("angles_ready")
        s_trig = sem("sin_cos_ready")
        s_Xr = sem("chunk_input_factors_ready")
        s_Fr = sem("chunk_output_factors_ready")
        s_prep = sem("chunk_matrix_products")
        s_prepe = sem("chunk_matrices_copied")
        s_V = sem("chunk_inputs_ready")
        s_Ve = sem("chunk_inputs_copied")
        s_S = sem("chunk_states_ready")
        s_Y = sem("chunk_outputs_ready")
        s_Ye = sem("chunk_outputs_copied")
        s_ysh = sem("y_stored")
        s_yl = sem("y_loaded")
        s_yd = sem("y_with_skip_ready")
        s_z = sem("gelu_y_ready")
        s_glu = sem("glu_product_ready")
        s_gsig = sem("glu_sigmoid_ready")
        s_hsm = sem("s5_rows_ready")
        s_cv = sem("conv_steps")
        s_cvd = sem("conv_centred")
        s_cn = sem("conv_normed")
        s_hcm = sem("conv_rows_ready")
        s_mix = sem("mix_product_ready")
        s_x1 = sem("residual_updated")
        s_xs = sem("samples_gated_product")
        s_keys = sem("keys_loaded")
        s_q = sem("query_product_ready")
        s_qe = sem("queries_copied")
        s_sc = sem("scores_ready")
        s_h2s = sem("h2_split_hi")
        s_h2l = sem("h2_split_lo")
        s_top = sem("selection_ready")
        s_exi = sem("softmax_exponents_in")
        s_exo = sem("softmax_exponents_out")
        s_selp = sem("selection_transposed")
        s_sele = sem("selection_copied")
        s_gh = sem("gates_split")
        s_hi = sem("weight_tile_hi")
        s_lo = sem("weight_tile_lo")
        s_pe = sem("peer_step_done")
        s_act = sem("activation_ready")
        s_hst = [sem(f"activation_stored_{i}") for i in range(HR)]
        s_oh = sem("one_hots_ready")
        s_tok = sem("token_gated")
        s_gev = sem("gates_copied")
        s_gst = [sem(f"gates_stored_{i}") for i in range(2)]
        s_gss = sem("sample_gates_stored")
        s_gl = [sem(f"gate_batch_loaded_{i}") for i in range(2)]
        s_hl = [sem(f"activation_loaded_{i}") for i in range(4)]
        s_w = sem("weighted_activation")
        s_wh = sem("weighted_activation_hi")
        s_wl = sem("weighted_activation_lo")
        s_out = sem("y_stored_out")
        s_os = sem("states_stored")
        s_fin = sem("final_rows_ready")


        counted, USED = {}, []
        for kind, _ in STREAM:
            counted[kind] = counted.get(kind, 0) + 1
            USED.append(({"ada": s_mod, "in": s_win, "glu": s_glu, "out": s_mix, "q": s_q}[kind], counted[kind]))

        block = base.enter_context(nc.Block())

        def natural(rows):
            return rows.rearrange("p (c i) -> p i c", i=L)

        SQ_BEFORE = {"rms1": 0, "conv": KD, "rms2": KD + CT, "final": 2 * KD + CT}
        SQU_BEFORE = {"rms1": 0, "conv": KD - 1, "rms2": KD + CT - 2, "final": 2 * KD + CT - 3}
        STAT = {"rms1": 1, "mean": 2, "conv": 3, "rms2": 4, "final": 5}
        RSTD = {"rms1": 1, "conv": 2, "rms2": 3, "final": 4}
        APPLY = {"rms1": 0, "rms2": 1, "final": 2}

        @block.sync
        def _(sp):
            for name, t in (("cT", cT[:]), ("par", par[:]), ("bm", bm[:]), ("cm", cm[:]), ("h0", h0[:]),
                            ("cw", cw[:]), ("cvec", cvec[:]), ("bada", bada[:]), ("ngain", ngain[:])):
                sp.dma_start(t, dr[name]).then_inc(s_small, 16)
            for c in range(CT):
                sp.dma_start(stc[:, c, :, 0:CW - 1], dr["stc"][:, c]).then_inc(s_small, 16)

            def load(n):
                kind, f = STREAM[n]
                if n >= NRAW:
                    sp.wait_ge(*USED[n - NRAW])
                w = 512 if kind == "glu" else RAW
                sp.dma_start(raw[:, n % NRAW, 0:w], dr["w_" + kind][f]).then_inc(s_raw[n % NRAW], 16)

            load(0)
            load(1)
            for k in range(KD):
                sp.dma_start(x[:, k, :], dr["x"][:, k]).then_inc(s_xl, 16)
            for n in range(2, NPRE):
                load(n)
            sp.wait_ge(s_os, 16 * (CT + 3))
            sp.wait_ge(s_x1, KD)
            sp.dma_start(keys[:], dr["keys"]).then_inc(s_keys, 16)
            for m in range(NRAW):
                sp.wait_ge(*USED[NPRE - NRAW + m])
                sp.dma_start(raw[:, m, :], dr["u"][m]).then_inc(s_raw[m], 16)

            def first_product(it, first, nxt, gates):
                for s in range(4):
                    m = it * 4 + (first + s)
                    sp.wait_ge(s_lo, m + 1)
                    if nxt == "u":
                        src = dr["u"][bass.ds(m + NRAW, 1)].rearrange("o p n -> p (o n)")
                    else:
                        src = dr["v"][s]
                    sp.dma_start(raw[:, s, :], src).then_inc(s_raw[s], 16)
                    sp.wait_ge(s_act, m + (NTT + 1))
                    sp.dma_start(hd[bass.ds(m, 1)].rearrange("o p n -> p (o n)"), actr[:, s % HR, :])\
                        .then_inc(s_hst[s % HR], 16)
                    if gates and s % 2:
                        sp.wait_ge(s_gev, it * 8 + (6 + (s + 1) * 2))
                        sp.dma_start(gpd[:, :, bass.ds(it * 2 + s // 2, 1), :].rearrange("b p k n -> p b (k n)"),
                                     stage[:, s // 2, :, :].rearrange("p (b j) t -> p b (j t)", b=NB))\
                            .then_inc(s_gst[s // 2], 16)

            with sp.Fori(0, A1 // 4) as it:
                first_product(it, 0, "u", False)
            with sp.Fori(0, (NK - A1) // 4 - 1) as it:
                first_product(it, A1, "u", True)
            first_product((NK - A1) // 4 - 1, A1, "v", True)
            sp.wait_ge(s_gev, 6 + (NK - A1 + 1) * 2)
            sp.dma_start(gsd.rearrange("b p n -> p b n"),
                         stages[:].rearrange("p (b j) t -> p b (j t)", b=NB)).then_inc(s_gss, 16)
            for s in range(HR):
                sp.wait_ge(s_hst[s], 16 * NK // HR)
            for s in range(2):
                sp.wait_ge(s_gst[s], 16 * (TP // GBLK) // 2)
            sp.wait_ge(s_gss, 16)

            def load_gates(b, slot):
                sp.dma_start(gbp[:, slot].rearrange("p k j t -> p (k j t)"),
                             gpd[bass.ds(b, 1)].rearrange("o p k n -> p (o k n)")).then_inc(s_gl[slot], 16)
                sp.dma_start(gbs[:, slot].rearrange("p j t -> p (j t)"),
                             gsd[bass.ds(b, 1)].rearrange("o p n -> p (o n)")).then_inc(s_gl[slot], 16)

            def load_act(j, slot):
                sp.dma_start(hring[:, slot, :], hd[bass.ds(j, 1)].rearrange("o p n -> p (o n)")).then_inc(s_hl[slot], 16)

            load_gates(0, 0)
            for j in range(4):
                load_act(j, j)
            load_gates(1, 1)
            for j in range(4, JB + 4):
                sp.wait_ge(s_w, j - 3)
                load_act(j, j % 4)

            def second_product(b2, odd, i2, s, more_v=True, more_h=True):
                mm = b2 * 16 + (i2 * 4 + (odd * 8 + s))
                if more_v:
                    sp.wait_ge(s_lo, mm + (NK + 1))
                    sp.dma_start(raw[:, s, :], dr["v"][bass.ds(mm + NRAW, 1)].rearrange("o p n -> p (o n)"))\
                        .then_inc(s_raw[s], 16)
                if more_h:
                    sp.wait_ge(s_w, mm + (JB + 1))
                    load_act(mm + 12, s)

            with sp.Fori(0, NB // 2 - 1) as b2:
                for odd in range(2):
                    sp.wait_ge(s_w, b2 * 16 + JB * (odd + 1))
                    load_gates(b2 * 2 + (odd + 2), odd)
                    with sp.Fori(0, 2) as i2:
                        for s in range(4):
                            second_product(b2, odd, i2, s)
            for mm in range(NK - 16, NK - 4):
                second_product(NB // 2 - 1, mm % 16 // 8, mm % 8 // 4, mm % 4, True, mm + 12 < NK)
            sp.wait_ge(s_hs, 3 * (KD + 1))
            for k in range(KD):
                sp.wait_ge(s_h, 2 * KD + k + 1)
                sp.dma_start(out["y"][:, k], yo[:, k, :]).then_inc(s_out, 16)
            sp.wait_ge(s_out, 16 * KD)

        @block.gpsimd
        def _(pool):
            n = [0]

            def link(ins):
                n[0] += 1
                ins.then_inc(s_p, 1)
                pool.wait_ge(s_p, n[0])

            pool.memset(ones[:], 1.0)
            pool.memset(adaR[:], 0.0)
            pool.memset(ident[:], 0.0)
            pool.memset(XR[:, :, L:2 * L - 1, :], 0.0)
            pool.memset(XI[:, :, L:2 * L - 1, :], 0.0)
            pool.memset(Cbd[:], 0.0)
            pool.memset(U[:, :, NC:NC + 2 * TS], 0.0)
            pool.memset(S[:, :, :, 0:1], 0.0)
            link(pool.iota(iota[:], pattern=[[1, P]], base=0, channel_multiplier=0,
                           allow_small_or_imprecise_dtypes=True))
            pool.affine_select(out=ident[:], in_=ident[:], compare_op=ALU.not_equal, fill=1.0,
                               base=0, pattern=[[-1, P]], channel_multiplier=1).then_inc(s_const, 1)
            for t in range(CT):
                pool.wait_ge(s_uev, t + 1)
                pool.dma_start(ud.rearrange("(t g) q i c -> t (g q) (i c)", t=CT)[t], uT[:, t, 0:TP]).then_inc(s_ush, 16)
                pool.dma_start(usd.rearrange("(t g) q s -> t (g q) s", t=CT)[t], uT[:, t, TP:T]).then_inc(s_ush, 16)
            pool.wait_ge(s_ush, 16 * 2 * CT)
            pool.wait_ge(s_const, 1)
            for i in range(L):
                pool.dma_start(U[i * SQ:(i + 1) * SQ, :, 0:NC],
                               ud[:, :, i, :].rearrange("g q c -> q g c")).then_inc(s_ul, 16)
            pool.dma_start(U[0:SQ, :, NC:NC + TS], usd.rearrange("g q s -> q g s")).then_inc(s_ul, 16)
            pool.dma_start(U[P - SQ:P, :, NC + TS:NC + 2 * TS], usd.rearrange("g q s -> q g s")).then_inc(s_ul, 16)
            pool.wait_ge(s_hc, CT)
            pool.dma_start(out["conv_p"], hc[:, :, TP:TP + CW - 1]).then_inc(s_os, 16)
            for c in range(CT):
                pool.dma_start(out["conv_s"][:, c], stc[:, c, :, 1:CW]).then_inc(s_os, 16)
            pool.wait_ge(s_Ye, 6)
            for i in range(L):
                pool.dma_start(yd[:, :, i, :].rearrange("g q c -> q g c"),
                               Ysb[i * SQ:(i + 1) * SQ, :, 0:NC]).then_inc(s_ysh, 16)
            pool.dma_start(ysd.rearrange("g q s -> q g s"), Ysb[0:SQ, :, NC:NC + TS]).then_inc(s_ysh, 16)
            pool.wait_ge(s_ysh, 16 * (L + 1))
            for t in range(CT):
                pool.dma_start(yT[:, t, 0:TP], yd.rearrange("(t g) q i c -> t (g q) (i c)", t=CT)[t]).then_inc(s_yl, 16)
                pool.dma_start(yT[:, t, TP:T], ysd.rearrange("(t g) q s -> t (g q) s", t=CT)[t]).then_inc(s_yl, 16)
            pool.wait_ge(s_S, 2)
            pool.dma_start(out["ssm_p"], ssp[:]).then_inc(s_os, 16)
            pool.dma_start(out["ssm_s"], ssn[:]).then_inc(s_os, 16)
            pool.wait_ge(s_yl, 16 * 2 * CT)
            pool.wait_ge(s_small, 16 * NSMALL)
            for t in range(CT):
                link(pool.tensor_scalar(uT[:, t, :], uT[:, t, :], cvec[:, 3, t:t + 1], 1.0, ALU.mult, ALU.mult))
                pool.tensor_tensor(yT[:, t, :], yT[:, t, :], uT[:, t, :], ALU.add).then_inc(s_yd, 1)
            for t in range(CT):
                pool.wait_ge(s_gsig, t + 1)
                pool.tensor_tensor(mixin[:, CT + t, :], yT[:, t, :], uT[:, t, :], ALU.mult).then_inc(s_hsm, 1)

            def low_part(s, m):
                pool.wait_ge(s_hi, m + 1)
                pool.tensor_tensor(hl[:, s % 2, 1, :], raw[:, s, :], hl[:, s % 2, 0, :].bitcast(F32),
                                   ALU.subtract).then_inc(s_lo, 1)

            with pool.Fori(0, 2 * NK // 4) as it:
                for s in range(4):
                    low_part(s, it * 4 + s)

        @block.scalar
        def _(act):
            act.wait_ge(s_small, 16 * NSMALL)
            act.activation(sil[:], cT[:], ACT.Silu).then_inc(s_sil, 1)
            act.wait_ge(s_trig_in, 1)
            act.activation(K[:, 12:14, :], K[:, 10:12, :], ACT.Sin).then_inc(s_trig, 1)

            def modulation_rows(pair):
                act.wait_ge(s_mod, PAIR * (pair + 1))
                after(act, s_adt, pair)
                if pair == 0:
                    act.wait_ge(s_const, 1)
                for c in range(2):
                    last = act.activation(adaR[32 * c:32 * c + 1 + TS, :], ps[32 * c:32 * c + 1 + TS, 6:8, :].rearrange(
                        "p a n -> p (a n)"), ACT.Copy)
                last.then_inc(s_ade, 1)

            def squares(norm, rows, count):
                for k in range(count):
                    if k >= 2:
                        act.wait_ge(s_squ, SQU_BEFORE[norm] + k - 1)
                    act.activation(sq[:, k % 2, :], rows[:, k, :], ACT.Square).then_inc(s_sq, 1)

            def root(norm):
                act.wait_ge(s_rec, RSTD[norm])
                act.activation(rstd[:], rstd[:], ACT.Sqrt).then_inc(s_rstd, 1)

            def shifts(norm, dst, first):
                for k in range(KD):
                    act.wait_ge(s_hs, APPLY[norm] * (KD + 1) + k + 1)
                    act.activation(dst[:, k, 0:TP], dst[:, k, 0:TP], ACT.Identity,
                                   bias=mods[:, first + k, 0:1]).then_inc(s_h, 1)

            act.wait_ge(s_xl, 16 * KD)
            squares("rms1", x, KD)
            modulation_rows(0)
            root("rms1")
            shifts("rms1", h1, SH1)
            for t in range(CT):
                act.wait_ge(s_win, t + 1)
                for h, (a, b) in enumerate(HALVES):
                    last = act.activation(uT[:, t, a:b], ps[:, 2 * (t % 2) + h, 0:b - a], ACT.Copy)
                last.then_inc(s_uev, 1)
            for t in range(CT):
                act.wait_ge(s_win, CT + 2 * t + 2)
                after(act, s_hc, t)
                for h, (a, b) in enumerate(HALVES):
                    last = act.activation(sq[:, 0, a:b], ps[:, 2 + h, 0:b - a], ACT.Sigmoid)
                last.then_inc(s_sig, 1)
            for e in range(20):
                act.wait_ge(s_prep, e + 1)
                src = ps[:, 4 + e % 2, :]
                if e < 4:
                    dst, src = Kt[:, e, :], src[:, 0:MQ]
                elif e < 12:
                    dst = ET[:, (e - 4) // 4, 4 * (e % 4):4 * (e % 4) + 4, :].rearrange("p t n -> p (t n)")
                else:
                    n4, ih = divmod(e - 12, 2)
                    dst = Tm[:, 8 * n4:8 * n4 + 8, 64 * ih:64 * ih + 64].rearrange("p g (i q) -> p i g q", q=SQ)
                    src = src.rearrange("p (i g q) -> p i g q", i=4, g=8)
                act.activation(dst, src, ACT.Copy).then_inc(s_prepe, 1)
            act.wait_ge(s_V, 1)
            for a in range(2):
                for b in range(3):
                    t0, t1 = 6 * b, min(6 * b + 6, ST)
                    act.activation(V[:, a, t0:t1, :].rearrange("p t c -> p (t c)"),
                                   ps[:, 3 * a + b, 0:(t1 - t0) * (NC + 2 * TS)], ACT.Copy).then_inc(s_Ve, 1)
            modulation_rows(1)
            act.wait_ge(s_Y, 1)
            for g in range(2):
                for b in range(3):
                    t0, t1 = 7 * b, min(7 * b + 7, ST)
                    act.activation(Ysb.rearrange("p (t g) c -> p t g c", g=2)[:, t0:t1, g, :],
                                   ps[:, 3 * g + b, 0:(t1 - t0) * (NC + TS)].rearrange("p (t c) -> p t c", c=NC + TS),
                                   ACT.Copy).then_inc(s_Ye, 1)
            for t in range(CT):
                act.wait_ge(s_yd, t + 1)
                act.activation(yT[:, t, :], yT[:, t, :], ACT.Gelu_apprx_tanh).then_inc(s_z, 1)
            for t in range(CT):
                act.wait_ge(s_glu, t + 1)
                for h, (a, b) in enumerate(HALVES):
                    last = act.activation(uT[:, t, a:b], ps[:, 2 * (t % 2) + h, 0:b - a], ACT.Sigmoid)
                last.then_inc(s_gsig, 1)
            modulation_rows(2)
            act.wait_ge(s_cvd, 1)
            squares("conv", cv, CT)
            root("conv")
            act.wait_ge(s_cn, 1)
            for t in range(CT):
                act.activation(mixin[:, t, 0:TP].rearrange("p (i c) -> p i c", i=L), natural(cv[:, t, 0:TP]), ACT.Silu,
                               scale=cvec[:, 1, t:t + 1], bias=cvec[:, 2, t:t + 1])
                act.activation(mixin[:, t, TP:T], cv[:, t, TP:T], ACT.Silu,
                               scale=cvec[:, 1, t:t + 1], bias=cvec[:, 2, t:t + 1]).then_inc(s_hcm, 1)
            for k in range(KD):
                act.wait_ge(s_x1, k + 1)
                if k >= 2:
                    act.wait_ge(s_squ, SQU_BEFORE["rms2"] + k - 1)
                act.activation(sq[:, k % 2, :], x[:, k, :], ACT.Square).then_inc(s_sq, 1)
            root("rms2")
            modulation_rows(3)
            shifts("rms2", h2f, SH2)
            for k in range(KD):
                if k == 0:
                    act.wait_ge(s_hs, 2 * (KD + 1))
                    act.wait_ge(s_h, 2 * KD)
                act.activation(h2[:, 0, k, :], h2f[:, k, :], ACT.Copy).then_inc(s_h2s, 1)
            for k in range(KD):
                act.wait_ge(s_q, k + 1)
                for h, (a, b) in enumerate(HALVES):
                    last = act.activation(qT[:, k, a:b], ps[:, 2 * (k % 2) + h, 0:b - a], ACT.Copy)
                last.then_inc(s_qe, 1)
            for t in range(NTT):
                act.wait_ge(s_sc, t + 1)
                for q in range(4):
                    last = act.activation(sc[0:TT, t, 4 * q:4 * q + 4, :].rearrange("p a n -> p (a n)"),
                                          ps[0:TT, 4 * (1 - t % 2) + q, :], ACT.Copy)
                last.then_inc(s_act, 1)

            NP4 = NPRE // 4
            for m in range(2):
                act.wait_ge(s_raw[m], 16 * (NP4 + 1))
                act.activation(hl[:, m, 0, :], raw[:, m, :], ACT.Copy).then_inc(s_hi, 1)

            def activations(s, it, first):
                m = it * 4 + (first + s)
                act.wait_ge(s_raw[(s + 2) % 4], (it + (NP4 + first // 4 + 1 + (s + 2) // 4)) * 16)
                act.wait_ge(s_pe, m + 1)
                act.activation(hl[:, s % 2, 0, :], raw[:, (s + 2) % 4, :], ACT.Copy).then_inc(s_hi, 1)
                after(act, s_hst[s % HR], it * 32 + (first // 2 + s // 2) * 16)
                for h, (a, b) in enumerate(HALVES):
                    last = act.activation(actr[:, s % HR, a:b], ps[:, 2 * (s % 2) + h, 0:b - a], ACT.Gelu_apprx_tanh)
                last.then_inc(s_act, 1)

            def copy_gates(s, it):
                if s % 2 == 0:
                    after(act, s_gst[s // 2], it * 16)
                for q in range(2):
                    act.wait_ge(s_tok, it * 32 + (8 * s + 4 * q + 4))
                    t0 = 8 * (s % 2) + 4 * q
                    act.activation(stage[:, s // 2, :, t0:t0 + 4].rearrange("p j t -> p t j"),
                                   ps[:, 4 + 2 * (s % 2) + q, :].rearrange("p (t j) -> p t j", t=4),
                                   ACT.Copy).then_inc(s_gev, 1)

            for s in range(4):
                activations(s, 0, 0)
            with act.Fori(1, A1 // 4) as it:
                for s in range(4):
                    activations(s, it, 0)
            act.wait_ge(s_exi, 1)
            act.activation(selv[0:TT, :, 2, :], eq[0:TT].rearrange("p a b -> p (a b)")[:, 0:NTT * NSEL].rearrange(
                "p (t n) -> p t n", t=NTT), ACT.Exp).then_inc(s_exo, 1)
            act.wait_ge(s_selp, 1)
            for kind in range(3):
                act.activation(selT[:, kind, 0:4 * TT], ps[:, 4 + kind, 0:4 * TT], ACT.Copy).then_inc(s_gev, 1)
                act.activation(selT[:, kind, 4 * TT:T], ps[:, 7, kind * TT:(kind + 1) * TT], ACT.Copy).then_inc(s_gev, 1)
            act.wait_ge(s_gev, 6)
            act.activation(gp[:, 0, :], selT[:, 2, :], ACT.Copy).then_inc(s_gh, 1)
            for s in range(4):
                activations(s, 0, A1)
                copy_gates(s, 0)
            with act.Fori(1, (NK - A1) // 4) as it:
                for s in range(4):
                    activations(s, it, A1)
                    copy_gates(s, it)
            for q in range(2):
                act.wait_ge(s_tok, TP + 4 * q + 4)
                act.activation(stages[:, :, 4 * q:4 * q + 4].rearrange("p j t -> p t j"),
                               ps[:, 4 + q, :].rearrange("p (t j) -> p t j", t=4), ACT.Copy).then_inc(s_gev, 1)

            def weighted_hi(j_in, slot, j, b_done):
                act.wait_ge(s_w, j + 1)
                if b_done is not None:
                    act.wait_ge(s_pe, b_done)
                act.activation(WHL[:, slot, 0, j_in, :], wf[:, j_in % 2, :], ACT.Copy).then_inc(s_wh, 1)

            for j in range(JB):
                weighted_hi(j, 0, j, NK if j == 0 else None)

            def second(b2, odd, i2, s, more_v=True, more_w=True):
                mm = b2 * 16 + (i2 * 4 + (odd * 8 + s))
                if more_w:
                    act.wait_ge(s_w, mm + 9)
                    if s == 0:
                        act.wait_ge(s_pe, b2 * 16 + (NK + 8 * odd))
                    act.activation(WHL[:, 1 - odd, 0, i2 * 4 + s, :], wf[:, s % 2, :], ACT.Copy).then_inc(s_wh, 1)
                if more_v:
                    act.wait_ge(s_raw[(s + 2) % 4], b2 * 64 + (i2 + (NP4 + NK // 4 + 2 * odd + 1 + (s + 2) // 4)) * 16)
                    act.wait_ge(s_pe, mm + (NK + 1))
                    act.activation(hl[:, s % 2, 0, :], raw[:, (s + 2) % 4, :], ACT.Copy).then_inc(s_hi, 1)

            with act.Fori(0, NB // 2 - 1) as b2:
                for odd in range(2):
                    for i2 in range(2):
                        for s in range(4):
                            second(b2, odd, i2, s)
            for mm in range(NK - 16, NK - 2):
                second(NB // 2 - 1, mm % 16 // 8, mm % 8 // 4, mm % 4, True, mm + 8 < NK)
            act.wait_ge(s_x1, KD + NK)
            squares("final", x, KD)
            root("final")
            shifts("final", yo, SHF)

        @block.vector
        def _(dve):
            n = [0]

            def link(ins):
                n[0] += 1
                ins.then_inc(s_v, 1)
                dve.wait_ge(s_v, n[0])

            def tt(o, a, b, op):
                link(dve.tensor_tensor(o, a, b, op))

            def cmul(o, a, b, t):
                dve.tensor_tensor(o[0], a[0], b[0], ALU.mult)
                tt(t, a[1], b[1], ALU.mult)
                tt(o[0], o[0], t, ALU.subtract)
                dve.tensor_tensor(o[1], a[0], b[1], ALU.mult)
                tt(t, a[1], b[0], ALU.mult)
                tt(o[1], o[1], t, ALU.add)

            def k(i):
                return K[:, i, :]

            def exp_exact(dst, src, t, r, p):
                link(dve.tensor_scalar(t, src, LOG2E, MAGIC, ALU.mult, ALU.add))
                link(dve.tensor_scalar(t, t, MAGIC, None, ALU.subtract))
                link(dve.tensor_scalar(t, t, 127.0, -126.0, ALU.min, ALU.max))
                link(dve.scalar_tensor_tensor(r, t, -LN2_HI, src, ALU.mult, ALU.add))
                link(dve.scalar_tensor_tensor(r, t, -LN2_LO, r, ALU.mult, ALU.add))
                link(dve.tensor_scalar(p, r, 1.0 / 5040, None, ALU.mult))
                for c in (1 / 720, 1 / 120, 1 / 24, 1 / 6, 0.5, 1.0):
                    link(dve.scalar_tensor_tensor(p, p, c, r, ALU.add, ALU.mult))
                link(dve.tensor_scalar(t, t, 127.0, None, ALU.add))
                link(dve.tensor_copy(ki[:], t))
                link(dve.tensor_scalar(ki[:], ki[:], 23, None, ALU.logical_shift_left))
                link(dve.scalar_tensor_tensor(dst, p, 1.0, ki[:].bitcast(F32), ALU.add, ALU.mult))

            dve.wait_ge(s_small, 16 * NSMALL)
            lr, li, ldt = par[:, 0, :], par[:, 1, :], par[:, 2, :]
            DT, X1, X8, MAG, MAG8, ANG = k(0), k(1), k(2), k(3), k(4), k(5)
            exp_exact(DT, ldt, k(6), k(7), k(8))
            tt(X1, lr, DT, ALU.mult)
            tt(ANG, li, DT, ALU.mult)
            link(dve.tensor_scalar(X8, X1, float(L), None, ALU.mult))
            exp_exact(MAG, X1, k(6), k(7), k(8))
            exp_exact(MAG8, X8, k(6), k(7), k(8))
            link(dve.tensor_scalar(k(6), ANG, INV2PI, MAGIC, ALU.mult, ALU.add))
            link(dve.tensor_scalar(k(6), k(6), MAGIC, None, ALU.subtract))
            link(dve.scalar_tensor_tensor(k(7), k(6), -TWO_PI_HI, ANG, ALU.mult, ALU.add))
            link(dve.scalar_tensor_tensor(k(10), k(6), -TWO_PI_LO, k(7), ALU.mult, ALU.add))
            link(dve.tensor_scalar(k(11), k(10), 0.5 * 3.141592653589793, None, ALU.add))
            link(dve.tensor_scalar(k(6), k(11), PI_IN, -2 * 3.141592653589793, ALU.is_gt, ALU.mult))
            tt(k(11), k(11), k(6), ALU.add)
            dve.tensor_scalar(K[:, 10:12, :], K[:, 10:12, :], PI_IN, -PI_IN, ALU.min, ALU.max).then_inc(s_trig_in, 1)
            dve.wait_ge(s_trig, 1)
            SIN, COS = k(12), k(13)
            dve.memset(PW[:, 0, :, 0:1], 1.0)
            dve.memset(PW[:, 1, :, 0:1], 0.0)
            tt(PW[:, 0, :, 1], MAG, COS, ALU.mult)
            tt(PW[:, 1, :, 1], MAG, SIN, ALU.mult)
            for m in (1, 2, 4):
                def wide(a):
                    return PW[:, a, :, m:m + 1].broadcast_to([P, ST, m])
                tmp = K[:, 14:14 + m, :].rearrange("p m t -> p t m")
                cmul([PW[:, a, :, m + 1:2 * m + 1] for a in (0, 1)], [wide(0), wide(1)],
                     [PW[:, a, :, 1:m + 1] for a in (0, 1)], tmp)
            for r in range(L + 1):
                last = dve.tensor_copy(PR[:, :, :, r], PW[:, :, :, L - r])
            link(last)
            AM, DEN, CR, CI = k(14), k(15), k(16), k(17)
            dve.tensor_scalar(AM, PW[:, 0, :, 1], -1.0, None, ALU.add)
            tt(DEN, lr, lr, ALU.mult)
            tt(k(18), li, li, ALU.mult)
            tt(DEN, DEN, k(18), ALU.add)
            link(dve.reciprocal(DEN, DEN))
            dve.tensor_tensor(CR, AM, lr, ALU.mult)
            tt(k(18), PW[:, 1, :, 1], li, ALU.mult)
            tt(CR, CR, k(18), ALU.add)
            dve.tensor_tensor(CI, PW[:, 1, :, 1], lr, ALU.mult)
            tt(k(18), AM, li, ALU.mult)
            tt(CI, CI, k(18), ALU.subtract)
            tt(CR, CR, DEN, ALU.mult)
            tt(CI, CI, DEN, ALU.mult)

            def per_state(a, n):
                return a.rearrange("p (t o) -> p t o", o=1).broadcast_to([P, ST, n])

            cmul([Bb[:, 0], Bb[:, 1]], [per_state(CR, SQ), per_state(CI, SQ)], [bm[:, 0], bm[:, 1]], xt[:, :, 0, :])
            dve.wait_ge(s_const, 1)

            def powers(src, first):
                return [src[:, a, :, first:first + L].rearrange("p t (m o) -> p t m o", o=1).broadcast_to([P, ST, L, SQ])
                        for a in (0, 1)]

            def over(m4):
                return [m4[:, a].rearrange("p t (o q) -> p t o q", o=1).broadcast_to([P, ST, L, SQ]) for a in (0, 1)]

            cmul([XR[:, :, 0:L, :], XI[:, :, 0:L, :]], powers(PR, 1), over(Bb), xt)
            for g2 in range(2):
                rows = slice(64 * g2, 64 * g2 + 64)
                dve.tensor_copy(Cbd[rows, 0, :, g2, :], cm[rows, 0])
                dve.tensor_scalar(Cbd[rows, 1, :, g2, :], cm[rows, 1], -1.0, None, ALU.mult).then_inc(s_Xr, 1)
            cmul([FO[:, 0], FO[:, 1]], powers(PW, 1), over(cm), xt)
            dve.tensor_scalar(FO[:, 1], FO[:, 1], -1.0, None, ALU.mult).then_inc(s_Fr, 1)
            cmul([k(20), k(21)], [COS, SIN], [COS, SIN], k(18))
            cmul([k(22), k(23)], [k(20), k(21)], [k(20), k(21)], k(18))
            cmul([k(20), k(21)], [k(22), k(23)], [k(22), k(23)], k(18))
            for i in range(5):
                q = (k(20 + 2 * i), k(21 + 2 * i))
                cmul([k(22 + 2 * i), k(23 + 2 * i)], q, q, k(18))
            dve.memset(hc[:, :, 0:CW - 1], 0.0)

            def modulations(pair):
                dve.wait_ge(s_adt, pair + 1)
                cols = ps[:, 6, 0:KD * (32 + 1 + TS)].rearrange("p (q s) -> p q s", q=KD)
                for c in range(2):
                    f0 = (2 * pair + c) * KD
                    last = dve.tensor_tensor(mods[:, f0:f0 + KD, :], cols[:, :, 32 * c:32 * c + 1 + TS],
                                             bada[:, f0:f0 + KD].rearrange("p (f o) -> p f o", o=1).broadcast_to(
                                                 [P, KD, 1 + TS]), ALU.add)
                last.then_inc(s_mods, 1)
                dve.wait_ge(s_mods, pair + 1)

            def gain(i, first):
                g = ngain[:, i].rearrange("p (f o) -> p f o", o=1).broadcast_to([P, KD, 1 + TS])
                link(dve.scalar_tensor_tensor(gsc[:, i], mods[:, first:first + KD, :], 1.0, g, ALU.add, ALU.mult))

            def variance(norm, width):
                dve.wait_ge(s_stat, STAT[norm])
                for h, (a, b) in enumerate(HALVES):
                    last = dve.tensor_scalar(rstd[:, a:b], ps[:, 4 + h, 0:b - a], 1.0 / width, EPS, ALU.mult, ALU.add)
                link(last)
                dve.reciprocal(rstd[:], rstd[:]).then_inc(s_rec, 1)
                dve.wait_ge(s_rstd, RSTD[norm])

            def apply_norm(norm, dst, first):
                i = APPLY[norm]
                for q in range(KD):
                    dve.scalar_tensor_tensor(dst[:, q, 0:TP], x[:, q, 0:TP], gsc[:, i, q, 0:1], rstd[:, 0:TP],
                                             ALU.mult, ALU.mult).then_inc(s_hs, 1)
                r = rstd[:, TP:T].rearrange("p (o s) -> p o s", o=1).broadcast_to([P, KD, TS])
                tt(smalls[:], x[:, :, TP:T], r, ALU.mult)
                tt(smalls[:], smalls[:], gsc[:, i, :, 1:1 + TS], ALU.mult)
                dve.tensor_tensor(dst[:, :, TP:T], smalls[:], mods[:, first:first + KD, 1:1 + TS], ALU.add)\
                    .then_inc(s_hs, 1)

            modulations(0)
            gain(0, SC1)
            variance("rms1", D)
            apply_norm("rms1", h1, SH1)

            for t in range(CT):
                dve.wait_ge(s_win, CT + 2 * t + 2)
                dve.wait_ge(s_sig, t + 1)
                rows = natural(hc[:, t, CW - 1:CW - 1 + TP])
                for h in range(2):
                    dve.tensor_tensor(rows[:, 4 * h:4 * h + 4, :],
                                      ps[:, h, 0:TP // 2].rearrange("p (i c) -> p i c", i=4),
                                      sq[:, 0, h * 256:h * 256 + 256].rearrange("p (i c) -> p i c", i=4), ALU.mult)
                dve.tensor_tensor(stc[:, t, :, CW - 1], ps[:, 1, TP // 2:TP // 2 + TS], sq[:, 0, TP:T],
                                  ALU.mult).then_inc(s_hc, 1)
            dve.wait_ge(s_hc, CT)

            dve.wait_ge(s_prep, 12)
            dve.memset(R[:, 0, :, 0:1], 1.0)
            link(dve.memset(R[:, 1, :, 0:1], 0.0))
            for i in range(6):
                m = 1 << i
                q = [per_state(k(20 + 2 * i + a), m) for a in (0, 1)]
                cmul([R[:, a, :, m:2 * m] for a in (0, 1)], q, [R[:, a, :, 0:m] for a in (0, 1)], wt[:, :, 0:m])
            dve.wait_ge(s_Ve, 6)
            vr, vi = V[:, 0, :, 0:NC], V[:, 1, :, 0:NC]
            dve.tensor_tensor(W2[:, 0], vr, R[:, 0], ALU.mult)
            tt(wt[:], vi, R[:, 1], ALU.mult)
            tt(W2[:, 0], W2[:, 0], wt[:], ALU.add)
            dve.tensor_tensor(W2[:, 1], vi, R[:, 0], ALU.mult)
            tt(wt[:], vr, R[:, 1], ALU.mult)
            tt(W2[:, 1], W2[:, 1], wt[:], ALU.subtract)
            link(dve.tensor_copy(wt[:], per_state(MAG8, NC)))
            link(dve.memset(wt[:, :, 0:1], 0.0))
            wtf = wt[:, :, :].rearrange("p t c -> p (t c)")
            for a in range(2):
                link(dve.tensor_tensor_scan(W2f[:, a, :], wtf, W2f[:, a, :], 0.0, ALU.mult, ALU.add))
            dve.tensor_tensor(V[:, 0, :, 0:NC], W2[:, 0], R[:, 0], ALU.mult)
            tt(wt[:], W2[:, 1], R[:, 1], ALU.mult)
            dve.tensor_tensor(S[:, 0, :, 1:NC], V[:, 0, :, 0:NC - 1], wt[:, :, 0:NC - 1], ALU.subtract)
            tt(ssp[:, 0, :], V[:, 0, :, NC - 1], wt[:, :, NC - 1], ALU.subtract)
            dve.tensor_tensor(V[:, 1, :, 0:NC], W2[:, 0], R[:, 1], ALU.mult)
            tt(wt[:], W2[:, 1], R[:, 0], ALU.mult)
            tt(S[:, 1, :, 1:NC], V[:, 1, :, 0:NC - 1], wt[:, :, 0:NC - 1], ALU.add)
            dve.tensor_tensor(ssp[:, 1, :], V[:, 1, :, NC - 1], wt[:, :, NC - 1], ALU.add)
            dve.tensor_copy(S[:, :, :, NC:NC + TS], h0[:]).then_inc(s_S, 1)
            a1 = [PW[:, a, :, 1:2].broadcast_to([P, ST, TS]) for a in (0, 1)]
            cmul([ssn[:, 0], ssn[:, 1]], a1, [h0[:, 0], h0[:, 1]], wt[:, :, 0:TS])
            dve.tensor_tensor(ssn[:], ssn[:], V[:, :, :, NC + TS:NC + 2 * TS], ALU.add).then_inc(s_S, 1)

            for t in range(CT):
                dve.tensor_scalar(cv[:, t, 0:TP], hc[:, t, 0:TP], cw[:, t, 0:1], cvec[:, 0, t:t + 1],
                                  ALU.mult, ALU.add).then_inc(s_cv, 1)
            for w in range(1, CW):
                for t in range(CT):
                    dve.wait_ge(s_cv, CT * (w - 1) + t + 1)
                    dve.scalar_tensor_tensor(cv[:, t, 0:TP], hc[:, t, w:w + TP], cw[:, t, w:w + 1], cv[:, t, 0:TP],
                                             ALU.mult, ALU.add).then_inc(s_cv, 1)
            prod = wt[:, :, :].rearrange("p t c -> p (t c)")[:, 0:CT * TS * CW].rearrange(
                "p (t s w) -> p t s w", t=CT, s=TS)
            dve.wait_ge(s_S, 2)
            for t in range(CT):
                last = dve.tensor_tensor(prod[:, t], stc[:, t],
                                         cw[:, t, :].rearrange("p (o w) -> p o w", o=1).broadcast_to([P, TS, CW]), ALU.mult)
            link(last)
            link(dve.tensor_reduce(cv[:, :, TP:T], prod, AX.X, ALU.add))
            dve.tensor_tensor(cv[:, :, TP:T], cv[:, :, TP:T],
                              cvec[:, 0, :].rearrange("p (t o) -> p t o", o=1).broadcast_to([P, CT, TS]),
                              ALU.add).then_inc(s_cv, 1)

            modulations(1)

            dve.wait_ge(s_stat, STAT["mean"])
            for h, (a, b) in enumerate(HALVES):
                mean = ps[:, 4 + h, 0:b - a].rearrange("p (o n) -> p o n", o=1).broadcast_to([P, CT, b - a])
                last = dve.scalar_tensor_tensor(cv[:, :, a:b], mean, -1.0 / CC, cv[:, :, a:b], ALU.mult, ALU.add)
            last.then_inc(s_cvd, 1)
            dve.wait_ge(s_cvd, 1)
            variance("conv", CC)
            dve.tensor_tensor(cv[:], cv[:], rstd[:].rearrange("p (o n) -> p o n", o=1).broadcast_to([P, CT, T]),
                              ALU.mult).then_inc(s_cn, 1)
            modulations(2)
            gain(1, SC2)

            def residual(f, first_gate, done):
                q, gate, bank = x[:, f, :], mods[:, first_gate + f, :], 2 * (f % 2)
                dve.tensor_tensor(smalls[:, f, :], ps[:, bank + 1, 256:256 + TS], gate[:, 1:1 + TS],
                                  ALU.mult).then_inc(s_xs, 1)
                for h in range(2):
                    dve.scalar_tensor_tensor(q[:, h * 256:h * 256 + 256], ps[:, bank + h, 0:256], gate[:, 0:1],
                                             q[:, h * 256:h * 256 + 256], ALU.mult, ALU.add)
                dve.wait_ge(s_xs, done)
                dve.tensor_tensor(q[:, TP:T], q[:, TP:T], smalls[:, f, :], ALU.add).then_inc(s_x1, 1)

            for q in range(KD):
                dve.wait_ge(s_mix, q + 1)
                residual(q, G1, q + 1)
            variance("rms2", D)
            dve.wait_ge(s_os, 16 * (CT + 3))
            apply_norm("rms2", h2f, SH2)
            for q in range(KD):
                dve.wait_ge(s_h2s, q + 1)
                dve.tensor_tensor(h2[:, 1, q, :], h2f[:, q, :], h2[:, 0, q, :].bitcast(F32), ALU.subtract).then_inc(s_h2l, 1)

            modulations(3)
            gain(2, SCF)

            A = slice(0, TT)
            dve.wait_ge(s_h2l, KD)
            dve.wait_ge(s_act, NTT)
            for t in range(NTT):
                def top16(vals, idx, src, width):
                    link(dve.max(vals[:, 0:8], src))
                    dve.max_index(idx[:, 0:8], vals[:, 0:8], src)
                    link(dve.match_replace(wk[A, 0:width], vals[:, 0:8], src, NEG))
                    link(dve.max(vals[:, 8:16], wk[A, 0:width]))
                    link(dve.max_index(idx[:, 8:16], vals[:, 8:16], wk[A, 0:width]))

                for h in range(HEADS):
                    for s in range(2):
                        top16(v16[A, h, s, :], i16[A, h, s, :], sc[A, t, s * HEADS + h, :], NK)
                dve.tensor_copy(i16f[A], i16[A])
                for h in range(HEADS):
                    last = dve.tensor_tensor(cand[A, h],
                                             v16[A, h, 0, :].rearrange("p (a o) -> p a o", o=1).broadcast_to([TT, TOPK, TOPK]),
                                             v16[A, h, 1, :].rearrange("p (o a) -> p o a", o=1).broadcast_to([TT, TOPK, TOPK]),
                                             ALU.add)
                link(last)
                for h in range(HEADS):
                    top16(selv[A, t, 2, h * TOPK:(h + 1) * TOPK], pos[A, h * TOPK:(h + 1) * TOPK],
                          cand[A, h].rearrange("p a b -> p (a b)"), TOPK * TOPK)
                dve.tensor_scalar(rr[A, 0, :], pos[A, :], 4, None, ALU.logical_shift_right)
                link(dve.tensor_scalar(rr[A, 1, :], pos[A, :], 15, None, ALU.bitwise_and))
                link(dve.tensor_copy(rf[A], rr[A]))
                for s in range(2):
                    tt(eq[A], rf[A, s, :].rearrange("p (n o) -> p n o", o=1).broadcast_to([TT, NSEL, TOPK]),
                       iota[A, 0:TOPK].rearrange("p (o r) -> p o r", o=1).broadcast_to([TT, NSEL, TOPK]), ALU.is_equal)
                    eq4 = eq[A].rearrange("p (h n) r -> p h n r", h=HEADS)
                    tt(eq4, eq4, i16f[A, :, s, :].rearrange("p h (o r) -> p h o r", o=1).broadcast_to(
                        [TT, HEADS, TOPK, TOPK]), ALU.mult)
                    link(dve.tensor_reduce(selv[A, t, s, :], eq[A], AX.X, ALU.add))
            sc4 = selv[A, :, 2, :].rearrange("p t (h n) -> p t h n", h=HEADS)
            ex = eq[A].rearrange("p a b -> p (a b)")[:, 0:NTT * NSEL].rearrange("p (t h n) -> p t h n", t=NTT, h=HEADS)
            dve.tensor_tensor(ex, sc4, selv[A, :, 2, :].rearrange("p t (h n) -> p t h n", h=HEADS)[:, :, :, 0:1]
                              .broadcast_to([TT, NTT, HEADS, TOPK]), ALU.subtract).then_inc(s_exi, 1)
            dve.wait_ge(s_exo, 1)
            sums = rs[A, 0, :].rearrange("p (t h) -> p t h", t=NTT)
            link(dve.tensor_reduce(sums, sc4, AX.X, ALU.add))
            link(dve.reciprocal(rs[A, 1, :], rs[A, 0, :]))
            dve.tensor_tensor(sc4, sc4, rs[A, 1, :].rearrange("p (t h o) -> p t h o", t=NTT, o=1).broadcast_to(
                [TT, NTT, HEADS, TOPK]), ALU.mult).then_inc(s_top, 1)

            dve.wait_ge(s_gh, 1)
            dve.tensor_tensor(gp[:, 1, :], selT[:, 2, :], gp[:, 0, :].bitcast(F32), ALU.subtract).then_inc(s_gh, 1)
            dve.wait_ge(s_gh, 2)
            gpf = gp[:, :, :].bitcast(F32)

            def one_hots(it, s):
                tok = it * 4 + s
                after(dve, s_tok, tok - 3)
                if isinstance(tok, int):
                    col = slice(tok, tok + 1)
                else:
                    col = bass.ds(tok, 1)
                dve.tensor_scalar(ohA[:, s, :], iota[:], selT[:, 0, col], None, ALU.is_equal)
                for q in range(2):
                    last = dve.tensor_scalar(ohB[:, s, q, :], iota[:], selT[:, 1, col], gpf[:, q, col],
                                             ALU.is_equal, ALU.mult)
                last.then_inc(s_oh, 1)

            for s in range(4):
                one_hots(0, s)
            with dve.Fori(1, T // 4) as it:
                for s in range(4):
                    one_hots(it, s)

            def weigh(jj, slot, hslot, gloads, hloads, j):
                dve.wait_ge(s_gl[slot], gloads)
                dve.wait_ge(s_hl[hslot], hloads)
                after(dve, s_wl, j - 1)
                w = wf[:, hslot % 2, :]
                h = hring[:, hslot, :]
                dve.tensor_tensor(w[:, 0:TP].rearrange("p (k t) -> p k t", t=GBLK),
                                  h[:, 0:TP].rearrange("p (k t) -> p k t", t=GBLK),
                                  gbp[:, slot, :, jj, :], ALU.mult)
                dve.tensor_tensor(w[:, TP:T], h[:, TP:T], gbs[:, slot, jj, :], ALU.mult).then_inc(s_w, 1)

            def low(jj, slot, j):
                dve.wait_ge(s_wh, j + 1)
                dve.tensor_tensor(WHL[:, slot, 1, jj, :], wf[:, jj % 2, :], WHL[:, slot, 0, jj, :].bitcast(F32),
                                  ALU.subtract).then_inc(s_wl, 1)

            dve.wait_ge(s_pe, NK)
            for j in range(JB):
                weigh(j, 0, j % 4, 32, 16 * (j // 4 + 1), j)
                if j:
                    low(j - 1, 0, j - 1)
            low(JB - 1, 0, JB - 1)

            def add_out(q, steps):
                dve.wait_ge(s_pe, steps)
                residual(q, G2, steps + (KD - NK))

            def second(b2, odd, jj, first, more_w=True):
                j = b2 * 16 + (odd * 8 + jj + 8)
                if more_w:
                    weigh(jj, 1 - odd, jj % 4, b2 * 32 + (32 if odd == 0 else 64),
                          (b2 * 4 + (2 * odd + 2 + jj // 4 + 1)) * 16, j)
                if not first:
                    add_out((jj - 1) % 8, b2 * 16 + (NK + odd * 8 + jj))
                if more_w:
                    low(jj, 1 - odd, j)

            for odd in range(2):
                for jj in range(JB):
                    second(0, odd, jj, odd == 0 and jj == 0)
            last_b2 = NB // 2 - 1
            with dve.Fori(1, last_b2) as b2:
                for odd in range(2):
                    for jj in range(JB):
                        second(b2, odd, jj, False)
            for odd in range(2):
                for jj in range(JB):
                    second(last_b2, odd, jj, False, odd == 0)
            add_out(KD - 1, 2 * NK)
            variance("final", D)
            apply_norm("final", yo, SHF)

        @block.tensor
        def _(pe):
            def tile(n_):
                pe.wait_ge(s_raw[n_ % NRAW], 16 * (n_ // NRAW + 1))

            def modulation_rows(pair, tiles=range(PAIR)):
                for i in tiles:
                    n_ = ADA[pair] + i
                    c, q = divmod(i, KD)
                    tile(n_)
                    if i == 0:
                        after(pe, s_mods, pair)
                    for h in range(2):
                        last = pe.matmul(ps[32 * c:32 * c + 1 + TS, 6 + h, :], sil[:, q, :],
                                         raw[:, n_ % NRAW, h * 512:(h + 1) * 512], start=q == 0, stop=q == KD - 1)
                    last.then_inc(s_mod, 1)

            def modulation_columns(pair):
                pe.wait_ge(s_ade, pair + 1)
                w = 32 + 1 + TS
                for q in range(KD):
                    last = pe.transpose(ps[:, 6, q * w:(q + 1) * w], adaR[:, q * P:(q + 1) * P], ident[0:w, 0:w])
                last.then_inc(s_adt, 1)

            def dense(n_, rows, count, bank, sem_):
                tile(n_)
                for q in range(count):
                    for h, (a, b) in enumerate(HALVES):
                        last = pe.matmul(ps[:, bank + h, 0:b - a], raw[:, n_ % NRAW, q * P:(q + 1) * P], rows[:, q, a:b],
                                         start=q == 0, stop=q == count - 1)
                last.then_inc(sem_, 1)

            def column_sums(rows_of, count, ready, summed):
                for q in range(count):
                    if ready is not None:
                        pe.wait_ge(s_sq, ready + q + 1)
                    r = rows_of(q)
                    for h, (a, b) in enumerate(HALVES):
                        last = pe.matmul(ps[:, 4 + h, 0:b - a], ones[:], r[:, a:b], start=q == 0, stop=q == count - 1)
                    if q < count - 1 and summed:
                        last.then_inc(s_squ, 1)
                last.then_inc(s_stat, 1)

            def sq_rows(q):
                return sq[:, q % 2, :]

            pe.wait_ge(s_sil, 1)
            modulation_rows(0, range(KD))
            pe.wait_ge(s_const, 1)
            column_sums(sq_rows, KD, SQ_BEFORE["rms1"], True)
            modulation_rows(0, range(KD, PAIR))
            modulation_columns(0)
            pe.wait_ge(s_h, KD)
            pe.wait_ge(s_hs, KD + 1)
            for w in range(12):
                if w in (2, 3, 4, 5):
                    pe.wait_ge(s_uev, w - 1)
                elif w >= 6:
                    pe.wait_ge(s_hc, (w - 4) // 2)
                dense(FIRST["in"] + w, h1, KD, 2 * (w % 2), s_win)
            pe.wait_ge(s_Xr, 2)
            X = (XR, XI)
            for e in range(20):
                if e >= 2:
                    pe.wait_ge(s_prepe, e - 1)
                bank = 4 + e % 2
                if e < 4:
                    for j in range(4):
                        for a in range(2):
                            last = pe.matmul(ps[32 * j:32 * j + 32, bank, 0:MQ],
                                             Cbd[:, a, 4 * e + j].rearrange("p g q -> p (g q)"),
                                             X[a][:, 4 * e + j].rearrange("p m q -> p (m q)"), start=a == 0, stop=a == 1)
                elif e < 12:
                    for j in range(4):
                        last = pe.transpose(ps[:, bank, j * P:(j + 1) * P],
                                            X[(e - 4) // 4][:, 4 * (e % 4) + j, 0:L, :].rearrange("p m q -> p (m q)"), ident[:])
                else:
                    n4, ih = divmod(e - 12, 2)
                    for j in range(4):
                        m = L - 1 - (4 * ih + j)
                        last = pe.transpose(ps[:, bank, j * P:(j + 1) * P], Kt[:, n4, m * SQ:m * SQ + P], ident[:])
                last.then_inc(s_prep, 1)
            pe.wait_ge(s_prepe, 20)
            pe.wait_ge(s_hc, CT)
            pe.wait_ge(s_ul, 16 * (L + 2))
            for t in range(ST):
                for g in range(2):
                    for a in range(2):
                        c = (t % 6) * (NC + 2 * TS)
                        last = pe.matmul(ps[64 * g:64 * g + 64, 3 * a + t // 6, c:c + NC + 2 * TS],
                                         ET[:, a, t, 64 * g:64 * g + 64], U[:, 2 * t + g, :], start=True, stop=True)
            last.then_inc(s_V, 1)
            modulation_rows(1)
            pe.wait_ge(s_S, 1)
            pe.wait_ge(s_Fr, 1)
            pe.wait_ge(s_Ve, 6)
            for t in range(ST):
                for g in range(2):
                    c = (t % 7) * (NC + TS)
                    o = ps[:, 3 * g + t // 7, c:c + NC + TS]
                    rows = slice(64 * g, 64 * g + 64)
                    pe.matmul(o, Tm[:, 2 * t + g, :], U[:, 2 * t + g, 0:NC + TS], start=True, stop=False)
                    for a in range(2):
                        last = pe.matmul(o, FO[rows, a, t].rearrange("p i q -> p (i q)"), S[rows, a, t],
                                         start=False, stop=a == 1)
            last.then_inc(s_Y, 1)
            modulation_columns(1)
            pe.wait_ge(s_z, CT)
            pe.wait_ge(s_Ye, 6)
            for w in range(CT):
                if w >= 2:
                    pe.wait_ge(s_gsig, w - 1)
                dense(FIRST["glu"] + w, yT, CT, 2 * (w % 2), s_glu)
            modulation_rows(2)
            pe.wait_ge(s_cv, CT * CW + 1)
            column_sums(lambda q: cv[:, q, :], CT, None, False)
            column_sums(sq_rows, CT, SQ_BEFORE["conv"], True)
            modulation_columns(2)
            pe.wait_ge(s_hsm, CT)
            pe.wait_ge(s_hcm, CT)
            for w in range(KD):
                if w >= 2:
                    pe.wait_ge(s_x1, w - 1)
                dense(FIRST["out"] + w, mixin, KD, 2 * (w % 2), s_mix)
            modulation_rows(3, range(KD))
            column_sums(sq_rows, KD, SQ_BEFORE["rms2"], True)
            modulation_rows(3, range(KD, PAIR))
            modulation_columns(3)
            pe.wait_ge(s_h, 2 * KD)
            pe.wait_ge(s_hs, 2 * (KD + 1))
            for w in range(KD):
                if w >= 2:
                    pe.wait_ge(s_qe, w - 1)
                dense(FIRST["q"] + w, h2f, KD, 2 * (w % 2), s_q)
            pe.wait_ge(s_keys, 16)
            pe.wait_ge(s_qe, KD)
            pe.wait_ge(s_mods, 4)
            for t in range(NTT):
                if t >= 2:
                    pe.wait_ge(s_act, t - 1)
                for h in range(HEADS):
                    for s in range(2):
                        i = s * HEADS + h
                        last = pe.matmul(ps[0:TT, 4 * (1 - t % 2) + i // 4, (i % 4) * NK:(i % 4 + 1) * NK],
                                         qT[64 * s:64 * s + 64, h, t * TT:(t + 1) * TT],
                                         keys[64 * s:64 * s + 64, h, :], start=True, stop=True)
                last.then_inc(s_sc, 1)

            PASSES = ((0, 0), (0, 1), (1, 0))

            def token(step, w, tok):
                if w % 4 == 0:
                    pe.wait_ge(s_gev, step * 2 + (4 + w // 4))
                pe.wait_ge(s_oh, tok + 1)
                slot = w % 4
                o = ps[:, 4 + 2 * (PAR[0]) + w // 4, (w % 4) * NK:(w % 4 + 1) * NK]
                pe.matmul(o, ohA[:, slot, :], ohB[:, slot, 0, :], start=True, stop=False)
                pe.matmul(o, ohA[:, slot, :], ohB[:, slot, 1, :], start=False, stop=True).then_inc(s_tok, 1)

            PAR = [0]

            def first_product(s, m, step=None):
                pe.wait_ge(s_lo, m + 1)
                pe.wait_ge(s_act, m + (NTT - 1))
                PAR[0] = s
                for q in range(KD):
                    for w, r in PASSES:
                        for h, (a, b) in enumerate(HALVES):
                            last = pe.matmul(ps[:, 2 * s + h, 0:b - a], hl[:, s, w, q * P:(q + 1) * P], h2[:, r, q, a:b],
                                             start=q == 0 and (w, r) == (0, 0), stop=q == KD - 1 and (w, r) == (1, 0))
                    if step is not None and q < KD - 1:
                        token(step, q, step * TOK + q)
                last.then_inc(s_pe, 1)
                if step is not None:
                    token(step, TOK - 1, step * TOK + TOK - 1)

            pe.wait_ge(s_h2l, KD)
            with pe.Fori(0, A1 // 2) as it:
                for s in range(2):
                    first_product(s, it * 2 + s)
            pe.wait_ge(s_top, 1)
            pe.wait_ge(s_act, NTT)
            for kind in range(3):
                for t in range(NTT):
                    o = ps[:, 4 + kind, t * TT:(t + 1) * TT] if t < 4 else ps[:, 7, kind * TT:(kind + 1) * TT]
                    last = pe.transpose(o, selv[0:TT, t, kind, :], ident[0:TT, 0:TT])
            last.then_inc(s_selp, 1)
            with pe.Fori(0, (NK - A1) // 2) as it:
                for s in range(2):
                    first_product(s, it * 2 + (A1 + s), it * 2 + s)
            PAR[0] = 0
            for w in range(TOK):
                token(NK - A1, w, TP + w)

            def second_product(odd, s, mm):
                pe.wait_ge(s_wl, b2 * 16 + 8 * (odd + 1))
                pe.wait_ge(s_lo, mm + (NK + 1))
                pe.wait_ge(s_x1, mm + (KD - 1))
                for j in range(JB):
                    for w, r in PASSES:
                        for h, (a, b) in enumerate(HALVES):
                            last = pe.matmul(ps[:, 2 * s + h, 0:b - a], hl[:, s, w, j * P:(j + 1) * P],
                                             WHL[:, odd, r, j, a:b],
                                             start=j == 0 and (w, r) == (0, 0), stop=j == JB - 1 and (w, r) == (1, 0))
                last.then_inc(s_pe, 1)

            pe.wait_ge(s_act, NTT + NK)
            with pe.Fori(0, NB // 2) as b2:
                for odd in range(2):
                    with pe.Fori(0, JB // 2) as i2:
                        for s in range(2):
                            second_product(odd, s, b2 * 16 + i2 * 2 + (odd * 8 + s))
            column_sums(sq_rows, KD, SQ_BEFORE["final"], True)


_OUTS = {"y": (P, KD, T), "conv_p": (P, CT, CW - 1), "conv_s": (P, CT, TS, CW - 1),
         "ssm_p": (P, 2, ST), "ssm_s": (P, 2, ST, TS)}


def layout(i):
    import numpy as np

    def cols(prompt, sample):
        chunked = prompt.reshape(NC, L, D).transpose(1, 0, 2).reshape(TP, D)
        return np.concatenate([chunked, sample], 0).T.reshape(KD, P, T).transpose(1, 0, 2)

    def tiles(w):
        k, n = w.shape
        return w.reshape(k // P, P, n // P, P).transpose(2, 1, 0, 3).reshape(n // P, P, k)

    def slabs(w):
        k, n = w.shape
        return w.reshape(k // P, P, n // RAW, RAW).transpose(2, 0, 1, 3).reshape(-1, P, RAW)

    def per_partition(v):
        return v.reshape(-1, P).T

    def states(v):
        return v.reshape(ST, P, -1).transpose(1, 0, 2)

    a = {
        "x": cols(i["x_prompt"][0], i["x_sample"][:, 0]),
        "cT": np.concatenate([i["c_prompt"], i["c_sample"]], 0).T.reshape(KD, P, 1 + TS).transpose(1, 0, 2),
        "par": np.stack([per_partition(i["ssm_lambda_re"][0].reshape(-1)), per_partition(i["ssm_lambda_im"][0].reshape(-1)),
                         per_partition(np.repeat(i["ssm_log_dt"][0], SN))], 1),
        "bm": np.stack([states(i["ssm_b_re"][0]), states(i["ssm_b_im"][0])], 1),
        "cm": np.stack([states(i["ssm_c_re"][0].transpose(0, 2, 1)), states(i["ssm_c_im"][0].transpose(0, 2, 1))], 1),
        "h0": np.stack([states(i[n][0].reshape(TS, SG * SN).T) for n in ("state_ssm_re", "state_ssm_im")], 1),
        "stc": i["state_conv"][0].transpose(2, 0, 1).reshape(CT, P, TS, CW - 1).transpose(1, 0, 2, 3),
        "cw": i["conv_w"][0].T.reshape(CT, P, CW).transpose(1, 0, 2),
        "cvec": np.stack([per_partition(i[n][0]) for n in ("conv_b", "conv_ln_g", "conv_ln_b", "ssm_d")], 1),
        "bada": np.concatenate([per_partition(i["b_ada"][0]), per_partition(i["b_ada_final"])], 1),
        "ngain": np.stack([per_partition(v) for v in (i["norm1_g"][0], i["norm2_g"][0], i["final_norm_g"])], 1),
        "w_ada": np.concatenate([slabs(i["w_ada"][0]), slabs(i["w_ada_final"])], 0),
        "w_in": tiles(i["w_in"][0]),
        "w_glu": tiles(i["ssm_w_glu"][0]),
        "w_out": tiles(i["w_out"][0]),
        "w_q": tiles(i["peer_w_q"][0]),
        "keys": i["peer_keys"][0].transpose(1, 3, 0, 2).reshape(P, HEADS, NK),
        "u": i["peer_u"][0].reshape(P, NK, KD, P).transpose(1, 3, 2, 0).reshape(NK, P, RAW),
        "v": i["peer_v"][0].reshape(P, NB, JB, KD, P).transpose(1, 3, 0, 2, 4).reshape(NB * KD, P, RAW),
    }
    return {n: np.ascontiguousarray(v) for n, v in a.items()}


def kernel(**inputs):
    import numpy as np
    import concourse.bacc as bacc
    from concourse.bass_utils import run_bass_kernel_spmd

    inputs = {n: np.asarray(v) for n, v in inputs.items()}
    nc = bacc.Bacc("TRN2", target_bir_lowering=False, num_devices=1)
    arrays = layout(inputs)
    dr = {n: nc.dram_tensor(f"in_{n}", a.shape, F32, kind="ExternalInput").ap() for n, a in arrays.items()}
    out = {n: nc.dram_tensor(f"out_{n}", s, F32, kind="ExternalOutput").ap() for n, s in _OUTS.items()}
    build(nc, dr, out)
    r = run_bass_kernel_spmd(nc, [{f"in_{n}": a for n, a in arrays.items()}], core_ids=[0]).results[0]
    y = r["out_y"].transpose(1, 0, 2).reshape(D, T).T
    y_prompt = y[:TP].reshape(L, NC, D).transpose(1, 0, 2).reshape(1, TP, D)
    conv_p = r["out_conv_p"].transpose(2, 1, 0).reshape(1, 1, CW - 1, CC)
    conv_s = r["out_conv_s"].transpose(2, 3, 1, 0).reshape(1, TS, CW - 1, CC)
    ssm_p = r["out_ssm_p"].transpose(1, 2, 0).reshape(2, 1, 1, SG, SN)
    ssm_s = r["out_ssm_s"].transpose(1, 3, 2, 0).reshape(2, 1, TS, SG, SN)
    c = np.ascontiguousarray
    return (c(y_prompt), c(y[TP:].reshape(TS, 1, D)), c(conv_p), c(conv_s), c(ssm_p[0]), c(ssm_p[1]), c(ssm_s[0]), c(ssm_s[1]))
```

```python
from contextlib import ExitStack

import concourse.bass as bass
from concourse import mybir

F32 = mybir.dt.float32
F32R = mybir.dt.float32r
U32 = mybir.dt.uint32
I32 = mybir.dt.int32
ALU = mybir.AluOpType
ACT = mybir.ActivationFunctionType
AX = mybir.AxisListType

P = 128
D = 1024
KD = D // P
TP, TS = 512, 8
T = TP + TS
L = 8
NC = TP // L
HALVES = ((0, TP // 2), (TP // 2, T))
CC = 512
CT = CC // P
CW = 31
SG, SQ, SN = 32, 16, 64
ST = SG * SN // P
HEADS, NK, TOPK, DK = 8, 128, 16, 64
NSEL = HEADS * TOPK
TT = 104
NTT = T // TT
EPS = 1e-6
NRAW = 4
RAW = 1024
JB = 8
NB = NK // JB
A3 = 8
A1 = NK - TP // 8 - A3
TOK = 8
GBLK = 16
HR = 2
NSMALL = 12
NMOD = 64
SH1, SC1, G1, SH2, SC2, G2, SHF, SCF = (8 * i for i in range(8))
INV2PI = 0.15915494309189535
TWO_PI_HI = 6.28125
TWO_PI_LO = 2 * 3.141592653589793 - 6.28125
MAGIC = 12582912.0
LOG2E = 1.4426950408889634
LN2_HI = 0.693359375
LN2_LO = -2.12194440e-4
PI_IN = 3.1415925
NEG = -3.0e38

PAIR = 16

STREAM = ([("ada", f) for f in range(PAIR)]
          + [("in", f) for f in (8, 9, 10, 11, 0, 4, 1, 5, 2, 6, 3, 7)]
          + [("ada", f) for f in range(PAIR, 2 * PAIR)]
          + [("glu", f) for f in range(4)]
          + [("ada", f) for f in range(2 * PAIR, 3 * PAIR)]
          + [("ada", f) for f in range(3 * PAIR, 3 * PAIR + 8)]
          + [("out", f) for f in range(8)]
          + [("ada", f) for f in range(3 * PAIR + 8, 4 * PAIR)]
          + [("q", f) for f in range(8)])
NPRE = len(STREAM)
assert NPRE % NRAW == 0
FIRST = {}
for _n, (_kind, _f) in enumerate(STREAM):
    FIRST.setdefault(_kind, _n)



def after(eng, sem, value):
    if isinstance(value, int) and value <= 0:
        return
    eng.wait_ge(sem, value)


def build(nc, dr, out):
    with ExitStack() as base:
        def sb(stack, name, shape, dt=F32):
            return stack.enter_context(nc.sbuf_tensor(name, shape, dt))

        def sem(name):
            return base.enter_context(nc.semaphore(name))

        hd = nc.dram_tensor("act_spill", [NK, P, T], F32, kind="Internal").ap()
        gpd = nc.dram_tensor("gate_spill", [NB, P, TP // GBLK, JB * GBLK], F32, kind="Internal").ap()
        ud = nc.dram_tensor("u_shuffle", [SG, SQ, L, NC], F32, kind="Internal").ap()
        usd = nc.dram_tensor("u_sample_shuffle", [SG, SQ, TS], F32, kind="Internal").ap()

        x = sb(base, "x_res", [P, KD, T])
        mods = sb(base, "mods", [P, NMOD, 1 + TS])
        gsc = sb(base, "gsc", [P, 3, KD, 1 + TS])
        bada = sb(base, "bada_sb", [P, NMOD])
        ngain = sb(base, "ngain_sb", [P, 3, KD])
        ones = sb(base, "ones", [P, P])
        ident = sb(base, "ident", [P, P])
        iota = sb(base, "iota", [P, P])
        rstd = sb(base, "rstd", [P, T])
        sq = sb(base, "sq", [P, 2, T])
        smalls = sb(base, "smalls", [P, KD, TS])
        sil = sb(base, "sil", [P, KD, 1 + TS])
        adaR = sb(base, "adaR", [P, RAW])
        raw = sb(base, "raw", [P, NRAW, RAW])

        ps = base.enter_context(nc.psum_tensor("ps", [P, 8, 512], F32))

        with ExitStack() as s5:
            h1 = sb(s5, "h1", [P, KD, T])
            mixin = sb(s5, "mixin", [P, KD, T])
            uT = sb(s5, "uT", [P, CT, T])
            FO = sb(s5, "FO", [P, 2, ST, L, SQ])
            ET = sb(s5, "ET", [P, 2, ST, P])
            Tm = sb(s5, "Tm", [P, SG, P])
            U = sb(s5, "U", [P, SG, NC + 2 * TS])
            dskip = sb(s5, "dskip", [P, CT, P])
            S = sb(s5, "S", [P, 2, ST, NC + TS])
            ssp = sb(s5, "ssp", [P, 2, ST])
            hc = sb(s5, "hc", [P, CT, CW - 1 + TP])
            stc = sb(s5, "stc_sb", [P, CT, TS, CW])
            cw = sb(s5, "cw_sb", [P, CT, CW])
            cvec = sb(s5, "cvec_sb", [P, 4, CT])
            cT = sb(s5, "cT_sb", [P, KD, 1 + TS])
            par = sb(s5, "par_sb", [P, 3, ST])
            bm = sb(s5, "bm_sb", [P, 2, ST, SQ])
            cm = sb(s5, "cm_sb", [P, 2, ST, SQ])
            h0 = sb(s5, "h0_sb", [P, 2, ST, TS])
            Bb = sb(s5, "Bb", [P, 2, ST, SQ])
            Cbd = sb(s5, "Cbd", [P, 2, ST, 2, SQ])
            PW = sb(s5, "PW", [P, 2, ST, L + 1])
            PR = sb(s5, "PR", [P, 2, ST, L + 1])
            K = sb(s5, "K", [P, 40, ST])
            ki = sb(s5, "ki", [P, ST], I32)
            ssn = sb(s5, "ssn", [P, 2, ST, TS])
            with ExitStack() as xs:
                XI = sb(xs, "XI", [P, ST, 2 * L - 1, SQ])
            with ExitStack() as vs:
                V = sb(vs, "V", [P, 2, ST, NC + 2 * TS])
                wt = sb(vs, "wt", [P, ST, NC])
        flat = mixin[:, :, :].rearrange("p k t -> p (k t)")
        XR = flat[:, 0:ST * (2 * L - 1) * SQ].rearrange("p (t m q) -> p t m q", t=ST, q=SQ)
        R = flat[:, 0:2 * ST * NC].rearrange("p (a t c) -> p a t c", a=2, t=ST)
        W2 = flat[:, 2 * ST * NC:4 * ST * NC].rearrange("p (a t c) -> p a t c", a=2, t=ST)
        W2f = flat[:, 2 * ST * NC:4 * ST * NC].rearrange("p (a n) -> p a n", a=2)
        xt = hc[:, :, :].rearrange("p a n -> p (a n)")[:, 0:ST * L * SQ].rearrange(
            "p (t m q) -> p t m q", t=ST, q=SQ)
        Ysb = ET[0:NC + TS, :, :, :].rearrange("p a t n -> p (a t n)").rearrange(
            "p (t i m) -> p t i m", t=CT, i=L)
        yT = h1[:, 0:CT, :]
        cv = h1[:, CT:2 * CT, :]
        MQ = (2 * L - 1) * SQ
        Kt = h1[:, 0:2, :].rearrange("p k t -> p (k t)")[:, 0:ST // 4 * MQ].rearrange("p (n m) -> p n m", m=MQ)

        with ExitStack() as tk:
            hl = sb(tk, "hl", [P, 2, 2, RAW], F32R)
            actr = sb(tk, "actr", [P, HR, T])
            with ExitStack() as tp:
                h2 = sb(tp, "h2", [P, 2, KD, T], F32R)
                ohA = sb(tp, "ohA", [P, 4, P], F32R)
                ohB = sb(tp, "ohB", [P, 4, 2, P], F32R)
                with ExitStack() as ss:
                    sc = sb(ss, "sc", [P, NTT, 2 * HEADS, NK])
                    with ExitStack() as qs:
                        h2f = sb(qs, "h2f", [P, KD, T])
                        qT = sb(qs, "qT", [P, HEADS, T])
                        keys = sb(qs, "keys_sb", [P, HEADS, 2, NK])
                    with ExitStack() as ts_:
                        wk = sb(ts_, "wk", [P, 2 * NK])
                        v16 = sb(ts_, "v16", [P, HEADS, 2, TOPK])
                        i16 = sb(ts_, "i16", [P, HEADS, 2, TOPK], U32)
                        i16f = sb(ts_, "i16f", [P, HEADS, 2, TOPK])
                        cand = sb(ts_, "cand", [P, HEADS, TOPK, TOPK])
                        pos = sb(ts_, "pos", [P, NSEL], U32)
                        rr = sb(ts_, "rr", [P, 2, NSEL], U32)
                        rf = sb(ts_, "rf", [P, 2, NSEL])
                        eq = sb(ts_, "eq", [P, NSEL, TOPK])
                        selv = sb(ts_, "selv", [P, NTT, 3, NSEL])
                        rs = sb(ts_, "rs", [P, 2, NTT * HEADS])
                        selT = sb(ts_, "selT", [P, 3, T])
                        gp = sb(ts_, "gp", [P, 2, T], F32R)
                with ExitStack() as sg:
                    stage = sb(sg, "stage", [P, 2, 2, NK, GBLK])
            with ExitStack() as cs:
                WH1 = sb(cs, "WH1", [P, 2, JB, T], F32R)
                beside = sb(cs, "one_hots_place", [P, 4 * 3 * P])
                WH0 = sb(cs, "WH0", [P, 2, JB, T], F32R)
                hring = sb(cs, "hring", [P, 4, T])
                wf = sb(cs, "wf", [P, 2, T])
                gbp = sb(cs, "gbp", [P, 2, TP // GBLK, JB, GBLK])
        WHL = (WH0, WH1)
        yo = gbp[:, :, :, :, :].rearrange("p a k j t -> p (a k j t)")[:, 0:KD * T].rearrange(
            "p (k t) -> p k t", k=KD)

        stages = adaR[:, :].rearrange("p (j s) -> p j s", s=TS)

        s_small = sem("small_inputs_loaded")
        s_c = sem("c_loaded")
        s_xl = sem("x_loaded")
        s_raw = [sem(f"weight_tile_loaded_{i}") for i in range(NRAW)]
        s_const = sem("constants_written")
        s_sil = sem("silu_c_ready")
        s_sq = sem("square_ready")
        s_squ = sem("square_used")
        s_stat = sem("column_sums_ready")
        s_rec = sem("reciprocal_ready")
        s_rstd = sem("rstd_ready")
        s_hs = sem("normed_scaled")
        s_h = sem("normed_shifted")
        s_mod = sem("modulation_tile_summed")
        s_ade = sem("modulation_rows_copied")
        s_adt = sem("modulations_transposed")
        s_mods = sem("modulations_ready")
        s_win = sem("input_projection_ready")
        s_uev = sem("u_copied")
        s_sig = sem("gate_sigmoid_ready")
        s_hc = sem("glu_rows_ready")
        s_ush = sem("u_stored")
        s_ul = sem("u_chunks_loaded")
        s_v = sem("vector_chain")
        s_p = sem("pool_chain")
        s_a = sem("scalar_chain")
        s_trig_in = sem("angles_ready")
        s_trig = sem("sin_cos_ready")
        s_Xr = sem("chunk_input_factors_ready")
        s_Fr = sem("chunk_output_factors_ready")
        s_prep = sem("chunk_matrix_products")
        s_prepe = sem("chunk_matrices_copied")
        s_V = sem("chunk_inputs_ready")
        s_Ve = sem("chunk_inputs_copied")
        s_S = sem("chunk_states_ready")
        s_Y = sem("chunk_outputs_ready")
        s_Ye = sem("chunk_outputs_copied")
        s_dg = sem("skip_diagonals_written")
        s_yt = sem("y_with_skip_ready")
        s_z = sem("gelu_y_ready")
        s_glu = sem("glu_product_ready")
        s_gsig = sem("glu_sigmoid_ready")
        s_hsm = sem("s5_rows_ready")
        s_cv = sem("conv_steps")
        s_cvd = sem("conv_centred")
        s_cn = sem("conv_normed")
        s_hcm = sem("conv_rows_ready")
        s_mix = sem("mix_product_ready")
        s_x1 = sem("residual_updated")
        s_xs = sem("samples_gated_product")
        s_kz = sem("keys_zeroed")
        s_keys = sem("keys_loaded")
        s_q = sem("query_product_ready")
        s_qe = sem("queries_copied")
        s_sc = sem("scores_ready")
        s_h2s = sem("h2_split_hi")
        s_h2l = sem("h2_split_lo")
        s_top = sem("selection_ready")
        s_exi = sem("softmax_exponents_in")
        s_exo = sem("softmax_exponents_out")
        s_selp = sem("selection_transposed")
        s_sele = sem("selection_copied")
        s_gh = sem("gates_split")
        s_hi = sem("weight_tile_hi")
        s_lo = sem("weight_tile_lo")
        s_pe = sem("peer_step_done")
        s_act = sem("activation_ready")
        s_hst = [sem(f"activation_stored_{i}") for i in range(HR)]
        s_oh = sem("one_hots_ready")
        s_tok = sem("token_gated")
        s_gev = sem("gates_copied")
        s_gadd = sem("gate_parts_added")
        s_gst = [sem(f"gates_stored_{i}") for i in range(2)]
        s_gl = [sem(f"gate_batch_loaded_{i}") for i in range(2)]
        s_hl = [sem(f"activation_loaded_{i}") for i in range(4)]
        s_w = sem("weighted_activation")
        s_wh = sem("weighted_activation_hi")
        s_wl = sem("weighted_activation_lo")
        s_out = sem("y_stored_out")
        s_os = sem("states_stored")
        s_fin = sem("final_rows_ready")


        counted, USED = {}, []
        for kind, _ in STREAM:
            counted[kind] = counted.get(kind, 0) + 1
            USED.append(({"ada": s_mod, "in": s_win, "glu": s_glu, "out": s_mix, "q": s_q}[kind], counted[kind]))

        H_AT = {2: (4,), 3: (5, 6), 4: (7, 8), 5: (9, 10), 6: (11,)}
        W_AT = {2: (0,), 3: (1, 2), 4: (3, 4), 5: (5, 6), 6: (7,)}

        block = base.enter_context(nc.Block())

        def natural(rows):
            return rows.rearrange("p (c i) -> p i c", i=L)

        SQ_BEFORE = {"rms1": 0, "conv": KD, "rms2": KD + CT, "final": 2 * KD + CT}
        SQU_BEFORE = {"rms1": 0, "conv": KD - 1, "rms2": KD + CT - 2, "final": 2 * KD + CT - 3}
        STAT = {"rms1": 1, "mean": 2, "conv": 3, "rms2": 4, "final": 5}
        RSTD = {"rms1": 1, "conv": 2, "rms2": 3, "final": 4}
        APPLY = {"rms1": 0, "rms2": 1, "final": 2}

        @block.sync
        def _(sp):
            def load(n):
                kind, f = STREAM[n]
                if n >= NRAW:
                    sp.wait_ge(*USED[n - NRAW])
                w = 512 if kind == "glu" else RAW
                sp.dma_start(raw[:, n % NRAW, 0:w], dr["w_" + kind][f]).then_inc(s_raw[n % NRAW], 16)

            sp.dma_start(cT[:], dr["cT"]).then_inc(s_c, 16)
            load(0)
            for name, t in (("par", par[:]), ("bm", bm[:]), ("cm", cm[:]), ("h0", h0[:]),
                            ("cw", cw[:]), ("cvec", cvec[:]), ("bada", bada[:]), ("ngain", ngain[:])):
                sp.dma_start(t, dr[name]).then_inc(s_small, 16)
            for c in range(CT):
                sp.dma_start(stc[:, c, :, 0:CW - 1], dr["stc"][:, c]).then_inc(s_small, 16)

            load(1)
            for k in range(KD):
                sp.dma_start(x[:, k, :], dr["x"][:, k]).then_inc(s_xl, 16)
            for n in range(2, NPRE):
                load(n)
            sp.wait_ge(s_kz, 1)
            for half in range(2):
                rows = slice(DK * half, DK * half + DK)
                sp.dma_start(keys[rows, :, half, :], dr["keys"][rows]).then_inc(s_keys, 16)
            for m in range(NRAW):
                sp.wait_ge(*USED[NPRE - NRAW + m])
                sp.dma_start(raw[:, m, :], dr["u"][m]).then_inc(s_raw[m], 16)

            def first_product(it, first, nxt, gates):
                for s in range(4):
                    m = it * 4 + (first + s)
                    sp.wait_ge(s_lo, m + 1)
                    if nxt == "u":
                        src = dr["u"][bass.ds(m + NRAW, 1)].rearrange("o p n -> p (o n)")
                    else:
                        src = dr["v"][s]
                    sp.dma_start(raw[:, s, :], src).then_inc(s_raw[s], 16)
                    sp.wait_ge(s_act, m + (NTT + 1))
                    sp.dma_start(hd[bass.ds(m, 1)].rearrange("o p n -> p (o n)"), actr[:, s % HR, :])\
                        .then_inc(s_hst[s % HR], 16)
                    if gates and s % 2:
                        sp.wait_ge(s_gadd, it * 4 + (s + 1))
                        sp.dma_start(gpd[:, :, bass.ds(it * 2 + s // 2, 1), :].rearrange("b p k n -> p b (k n)"),
                                     stage[:, s // 2, 0, :, :].rearrange("p (b j) t -> p b (j t)", b=NB))\
                            .then_inc(s_gst[s // 2], 16)

            with sp.Fori(0, A1 // 4) as it:
                first_product(it, 0, "u", False)
            with sp.Fori(0, TP // TOK // 4) as it:
                first_product(it, A1, "u", True)

            def load_gates(b, slot):
                sp.dma_start(gbp[:, slot].rearrange("p k j t -> p (k j t)"),
                             gpd[bass.ds(b, 1)].rearrange("o p k n -> p (o k n)")).then_inc(s_gl[slot], 16)

            def load_act(j, slot):
                sp.dma_start(hring[:, slot, :], hd[bass.ds(j, 1)].rearrange("o p n -> p (o n)")).then_inc(s_hl[slot], 16)

            for k in range(A3):
                m, s = NK - A3 + k, k % 4
                sp.wait_ge(s_lo, m + 1)
                src = dr["u"][m + NRAW] if m + NRAW < NK else dr["v"][m + NRAW - NK]
                sp.dma_start(raw[:, s, :], src).then_inc(s_raw[s], 16)
                sp.wait_ge(s_act, m + (NTT + 1))
                sp.dma_start(hd[m], actr[:, s % HR, :]).then_inc(s_hst[s % HR], 16)
                if k == 0:
                    for i in range(HR):
                        sp.wait_ge(s_hst[i], 16 * (NK - A3) // HR)
                    for j in range(4):
                        load_act(j, j)
                    for i in range(2):
                        sp.wait_ge(s_gst[i], 16 * (TP // GBLK) // 2)
                    load_gates(0, 0)
                    sp.wait_ge(s_gadd, TP // TOK + 1)
                    load_gates(1, 1)
                else:
                    for j in H_AT.get(k, ()):
                        sp.wait_ge(s_w, j - 3)
                        load_act(j, j % 4)
            for s in range(HR):
                sp.wait_ge(s_hst[s], 16 * NK // HR)

            def second_product(b2, odd, i2, s, more_v=True, more_h=True):
                mm = b2 * 16 + (i2 * 4 + (odd * 8 + s))
                if more_v:
                    sp.wait_ge(s_lo, mm + (NK + 1))
                    sp.dma_start(raw[:, s, :], dr["v"][bass.ds(mm + NRAW, 1)].rearrange("o p n -> p (o n)"))\
                        .then_inc(s_raw[s], 16)
                if more_h:
                    sp.wait_ge(s_w, mm + (JB + 1))
                    load_act(mm + 12, s)

            with sp.Fori(0, NB // 2 - 1) as b2:
                for odd in range(2):
                    sp.wait_ge(s_w, b2 * 16 + JB * (odd + 1))
                    load_gates(b2 * 2 + (odd + 2), odd)
                    with sp.Fori(0, 2) as i2:
                        for s in range(4):
                            second_product(b2, odd, i2, s)
            for mm in range(NK - 16, NK - 4):
                second_product(NB // 2 - 1, mm % 16 // 8, mm % 8 // 4, mm % 4, True, mm + 12 < NK)
            sp.wait_ge(s_hs, 3 * (KD + 1))
            for k in range(KD):
                sp.wait_ge(s_h, 2 * KD + k + 1)
                sp.dma_start(out["y"][:, k], yo[:, k, :]).then_inc(s_out, 16)
            sp.wait_ge(s_out, 16 * KD)

        @block.gpsimd
        def _(pool):
            n = [0]

            def link(ins):
                n[0] += 1
                ins.then_inc(s_p, 1)
                pool.wait_ge(s_p, n[0])

            pool.memset(ones[:], 1.0)
            pool.memset(adaR[0:32 + 1 + TS, :], 0.0)
            pool.memset(ident[:], 0.0)
            pool.memset(XR[:, :, L:2 * L - 1, :], 0.0)
            pool.memset(XI[:, :, L:2 * L - 1, :], 0.0)
            pool.memset(Cbd[:], 0.0)
            pool.memset(U[:, :, NC:NC + 2 * TS], 0.0)
            pool.memset(S[:, :, :, 0:1], 0.0)
            link(pool.iota(iota[:], pattern=[[1, P]], base=0, channel_multiplier=0,
                           allow_small_or_imprecise_dtypes=True))
            pool.affine_select(out=ident[:], in_=ident[:], compare_op=ALU.not_equal, fill=1.0,
                               base=0, pattern=[[-1, P]], channel_multiplier=1).then_inc(s_const, 1)
            pool.wait_ge(s_small, 16 * NSMALL)
            pool.wait_ge(s_const, 1)
            for t in range(CT):
                pool.tensor_scalar(dskip[:, t, :], ident[:], cvec[:, 3, t:t + 1], 1.0, ALU.mult, ALU.mult).then_inc(s_dg, 1)
            for t in range(CT):
                pool.wait_ge(s_uev, t + 1)
                pool.dma_start(ud.rearrange("(t g) q i c -> t (g q) (i c)", t=CT)[t], uT[:, t, 0:TP]).then_inc(s_ush, 16)
                pool.dma_start(usd.rearrange("(t g) q s -> t (g q) s", t=CT)[t], uT[:, t, TP:T]).then_inc(s_ush, 16)
            pool.wait_ge(s_ush, 16 * 2 * CT)
            pool.wait_ge(s_const, 1)
            for i in range(L):
                pool.dma_start(U[i * SQ:(i + 1) * SQ, :, 0:NC],
                               ud[:, :, i, :].rearrange("g q c -> q g c")).then_inc(s_ul, 16)
            pool.dma_start(U[0:SQ, :, NC:NC + TS], usd.rearrange("g q s -> q g s")).then_inc(s_ul, 16)
            pool.dma_start(U[P - SQ:P, :, NC + TS:NC + 2 * TS], usd.rearrange("g q s -> q g s")).then_inc(s_ul, 16)
            pool.wait_ge(s_hc, CT)
            pool.dma_start(out["conv_p"], hc[:, :, TP:TP + CW - 1]).then_inc(s_os, 16)
            for c in range(CT):
                pool.dma_start(out["conv_s"][:, c], stc[:, c, :, 1:CW]).then_inc(s_os, 16)
            pool.wait_ge(s_S, 2)
            pool.dma_start(out["ssm_p"], ssp[:]).then_inc(s_os, 16)
            pool.dma_start(out["ssm_s"], ssn[:]).then_inc(s_os, 16)
            for t in range(CT):
                pool.wait_ge(s_gsig, t + 1)
                pool.tensor_tensor(mixin[:, CT + t, :], yT[:, t, :], uT[:, t, :], ALU.mult).then_inc(s_hsm, 1)

            pool.wait_ge(s_os, 16 * (CT + 3))
            pool.wait_ge(s_x1, KD)
            pool.memset(keys[:], 0.0).then_inc(s_kz, 1)

            def low_part(s, m):
                pool.wait_ge(s_hi, m + 1)
                pool.tensor_tensor(hl[:, s % 2, 1, :], raw[:, s, :], hl[:, s % 2, 0, :].bitcast(F32),
                                   ALU.subtract).then_inc(s_lo, 1)

            def add_gates(s, step, dst=None):
                t = slice(8 * (s % 2), 8 * (s % 2) + TOK)
                hi, lo = stage[:, s // 2, 0, :, t], stage[:, s // 2, 1, :, t]
                pool.wait_ge(s_gev, step * 4 + 10)
                pool.tensor_tensor(hi if dst is None else dst, hi, lo, ALU.add).then_inc(s_gadd, 1)

            for m in range(2):
                low_part(m, m)
            with pool.Fori(0, A1 // 4) as it:
                for s in range(4):
                    low_part((s + 2) % 4, it * 4 + (s + 2))
            with pool.Fori(0, TP // TOK // 4) as it:
                for s in range(4):
                    low_part((s + 2) % 4, it * 4 + (A1 + s + 2))
                    add_gates(s, it * 4 + s)
            low_part(2, NK - A3 + 2)
            add_gates(0, TP // TOK, stages)
            low_part(3, NK - A3 + 3)
            with pool.Fori((NK - A3 + 4) // 4, 2 * NK // 4) as it:
                for s in range(4):
                    low_part(s, it * 4 + s)

        @block.scalar
        def _(act):
            act.wait_ge(s_c, 16)
            act.activation(sil[:], cT[:], ACT.Silu).then_inc(s_sil, 1)
            act.wait_ge(s_trig_in, 1)
            act.activation(K[:, 12:14, :], K[:, 10:12, :], ACT.Sin).then_inc(s_trig, 1)

            def modulation_rows(pair):
                act.wait_ge(s_mod, PAIR * (pair + 1))
                after(act, s_adt, pair)
                if pair == 0:
                    act.wait_ge(s_const, 1)
                for c in range(2):
                    last = act.activation(adaR[32 * c:32 * c + 1 + TS, :], ps[32 * c:32 * c + 1 + TS, 6:8, :].rearrange(
                        "p a n -> p (a n)"), ACT.Copy)
                last.then_inc(s_ade, 1)

            def squares(norm, rows, count):
                for k in range(count):
                    if k >= 2:
                        act.wait_ge(s_squ, SQU_BEFORE[norm] + k - 1)
                    act.activation(sq[:, k % 2, :], rows[:, k, :], ACT.Square).then_inc(s_sq, 1)

            def root(norm):
                act.wait_ge(s_rec, RSTD[norm])
                act.activation(rstd[:], rstd[:], ACT.Sqrt).then_inc(s_rstd, 1)

            def shifts(norm, dst, first):
                for k in range(KD):
                    act.wait_ge(s_hs, APPLY[norm] * (KD + 1) + k + 1)
                    act.activation(dst[:, k, 0:TP], dst[:, k, 0:TP], ACT.Identity,
                                   bias=mods[:, first + k, 0:1]).then_inc(s_h, 1)

            act.wait_ge(s_xl, 16 * KD)
            squares("rms1", x, KD)
            root("rms1")
            modulation_rows(0)
            shifts("rms1", h1, SH1)
            for t in range(CT):
                act.wait_ge(s_win, t + 1)
                for h, (a, b) in enumerate(HALVES):
                    last = act.activation(uT[:, t, a:b], ps[:, 2 * (t % 2) + h, 0:b - a], ACT.Copy)
                last.then_inc(s_uev, 1)
            for t in range(CT):
                act.wait_ge(s_win, CT + 2 * t + 2)
                after(act, s_hc, t)
                for h, (a, b) in enumerate(HALVES):
                    last = act.activation(sq[:, 0, a:b], ps[:, 2 + h, 0:b - a], ACT.Sigmoid)
                last.then_inc(s_sig, 1)
            for e in range(20):
                act.wait_ge(s_prep, e + 1)
                src = ps[:, 4 + e % 2, :]
                if e < 4:
                    dst, src = Kt[:, e, :], src[:, 0:MQ]
                elif e < 12:
                    dst = ET[:, (e - 4) // 4, 4 * (e % 4):4 * (e % 4) + 4, :].rearrange("p t n -> p (t n)")
                else:
                    n4, ih = divmod(e - 12, 2)
                    dst = Tm[:, 8 * n4:8 * n4 + 8, 64 * ih:64 * ih + 64].rearrange("p g (i q) -> p i g q", q=SQ)
                    src = src.rearrange("p (i g q) -> p i g q", i=4, g=8)
                act.activation(dst, src, ACT.Copy).then_inc(s_prepe, 1)
            act.wait_ge(s_V, 1)
            for a in range(2):
                for b in range(3):
                    t0, t1 = 6 * b, min(6 * b + 6, ST)
                    act.activation(V[:, a, t0:t1, :].rearrange("p t c -> p (t c)"),
                                   ps[:, 3 * a + b, 0:(t1 - t0) * (NC + 2 * TS)], ACT.Copy).then_inc(s_Ve, 1)
            modulation_rows(1)
            for e in range(2 * CT):
                b, g2 = divmod(e, 2)
                if g2 == 0 or b == 0:
                    act.wait_ge(s_Y, 1 + g2)
                act.activation(Ysb[:, b].rearrange("p i (g h q) -> p g h i q", h=2, q=SQ)[:, :, g2],
                               ps[0:NC + TS, 4 * g2 + b, :].rearrange("p (g i q) -> p g i q", g=4, i=L),
                               ACT.Copy).then_inc(s_Ye, 1)
            for t in range(CT):
                act.wait_ge(s_yt, t + 1)
                for h in range(2):
                    act.activation(yT[:, t, h * 256:(h + 1) * 256].rearrange("p (i c) -> p i c", i=4),
                                   ps[:, 4 * h + t, 0:4 * (NC + TS)].rearrange("p (i c) -> p i c", i=4)[:, :, 0:NC],
                                   ACT.Gelu_apprx_tanh)
                act.activation(yT[:, t, TP:T], ps[:, t, NC:NC + TS], ACT.Gelu_apprx_tanh).then_inc(s_z, 1)
            for t in range(CT):
                act.wait_ge(s_glu, t + 1)
                for h, (a, b) in enumerate(HALVES):
                    last = act.activation(uT[:, t, a:b], ps[:, 2 * (t % 2) + h, 0:b - a], ACT.Sigmoid)
                last.then_inc(s_gsig, 1)
            modulation_rows(2)
            act.wait_ge(s_cvd, 1)
            squares("conv", cv, CT)
            root("conv")
            act.wait_ge(s_cn, 1)
            for t in range(CT):
                act.activation(mixin[:, t, 0:TP].rearrange("p (i c) -> p i c", i=L), natural(cv[:, t, 0:TP]), ACT.Silu,
                               scale=cvec[:, 1, t:t + 1], bias=cvec[:, 2, t:t + 1])
                act.activation(mixin[:, t, TP:T], cv[:, t, TP:T], ACT.Silu,
                               scale=cvec[:, 1, t:t + 1], bias=cvec[:, 2, t:t + 1]).then_inc(s_hcm, 1)
            for k in range(KD):
                act.wait_ge(s_x1, k + 1)
                if k >= 2:
                    act.wait_ge(s_squ, SQU_BEFORE["rms2"] + k - 1)
                act.activation(sq[:, k % 2, :], x[:, k, :], ACT.Square).then_inc(s_sq, 1)
            root("rms2")
            shifts("rms2", h2f, SH2)
            modulation_rows(3)
            for k in range(KD):
                if k == 0:
                    act.wait_ge(s_hs, 2 * (KD + 1))
                    act.wait_ge(s_h, 2 * KD)
                act.activation(h2[:, 0, k, :], h2f[:, k, :], ACT.Copy).then_inc(s_h2s, 1)
            for k in range(KD):
                act.wait_ge(s_q, k + 1)
                for h, (a, b) in enumerate(HALVES):
                    last = act.activation(qT[:, k, a:b], ps[:, 2 * (k % 2) + h, 0:b - a], ACT.Copy)
                last.then_inc(s_qe, 1)
            for t in range(NTT):
                act.wait_ge(s_sc, t + 1)
                for q in range(4):
                    last = act.activation(sc[0:TT, t, 4 * q:4 * q + 4, :].rearrange("p a n -> p (a n)"),
                                          ps[0:TT, 4 * (1 - t % 2) + q, :], ACT.Copy)
                last.then_inc(s_act, 1)

            NP4 = NPRE // 4
            for m in range(2):
                act.wait_ge(s_raw[m], 16 * (NP4 + 1))
                act.activation(hl[:, m, 0, :], raw[:, m, :], ACT.Copy).then_inc(s_hi, 1)

            def activations(s, it, first):
                m = it * 4 + (first + s)
                act.wait_ge(s_raw[(s + 2) % 4], (it + (NP4 + first // 4 + 1 + (s + 2) // 4)) * 16)
                act.wait_ge(s_pe, m + 1)
                act.activation(hl[:, s % 2, 0, :], raw[:, (s + 2) % 4, :], ACT.Copy).then_inc(s_hi, 1)
                after(act, s_hst[s % HR], it * 32 + (first // 2 + s // 2) * 16)
                for h, (a, b) in enumerate(HALVES):
                    last = act.activation(actr[:, s % HR, a:b], ps[:, 2 * (s % 2) + h, 0:b - a], ACT.Gelu_apprx_tanh)
                last.then_inc(s_act, 1)

            def copy_gates(s, it, banks):
                if s % 2 == 0 and 0 in banks:
                    after(act, s_gst[s // 2], it * 16)
                for q in banks:
                    act.wait_ge(s_tok, it * 32 + (8 * s + 2 * q + 2))
                    t0 = 8 * (s % 2) + 2 * q
                    act.activation(stage[:, s // 2, :, :, t0:t0 + 2].rearrange("p a j t -> p t a j"),
                                   ps[:, 4 + q, :].rearrange("p (t a j) -> p t a j", t=2, a=2),
                                   ACT.Copy).then_inc(s_gev, 1)

            for s in range(4):
                activations(s, 0, 0)
            with act.Fori(1, A1 // 4) as it:
                for s in range(4):
                    activations(s, it, 0)
            act.wait_ge(s_exi, 1)
            act.activation(selv[0:TT, :, 2, :], eq[0:TT].rearrange("p a b -> p (a b)")[:, 0:NTT * NSEL].rearrange(
                "p (t n) -> p t n", t=NTT), ACT.Exp).then_inc(s_exo, 1)
            act.wait_ge(s_selp, 1)
            for kind in range(3):
                act.activation(selT[:, kind, 0:4 * TT], ps[:, 4 + kind, 0:4 * TT], ACT.Copy).then_inc(s_gev, 1)
                act.activation(selT[:, kind, 4 * TT:T], ps[:, 7, kind * TT:(kind + 1) * TT], ACT.Copy).then_inc(s_gev, 1)
            act.wait_ge(s_gev, 6)
            act.activation(gp[:, 0, :], selT[:, 2, :], ACT.Copy).then_inc(s_gh, 1)
            for s in range(4):
                copy_gates(s, 0, (0, 1, 2))
                activations(s, 0, A1)
                copy_gates(s, 0, (3,))
            with act.Fori(1, TP // TOK // 4) as it:
                for s in range(4):
                    copy_gates(s, it, (0, 1, 2))
                    activations(s, it, A1)
                    copy_gates(s, it, (3,))

            def weighted_hi(j):
                act.wait_ge(s_w, j + 1)
                act.activation(WH0[:, 0, j, :], wf[:, j % 2, :], ACT.Copy).then_inc(s_wh, 1)

            for k in range(A3):
                activations(k % 4, TP // TOK // 4 + k // 4, A1)
                if k == 0:
                    copy_gates(0, TP // TOK // 4, range(4))
                for j in W_AT.get(k, ()):
                    weighted_hi(j)

            def second(b2, odd, i2, s, more_v=True, more_w=True):
                mm = b2 * 16 + (i2 * 4 + (odd * 8 + s))
                if more_w:
                    act.wait_ge(s_w, mm + 9)
                    if s == 0:
                        act.wait_ge(s_pe, b2 * 16 + (NK + 8 * odd))
                    act.activation(WHL[1 - odd][:, 0, i2 * 4 + s, :], wf[:, s % 2, :], ACT.Copy).then_inc(s_wh, 1)
                if more_v:
                    act.wait_ge(s_raw[(s + 2) % 4], b2 * 64 + (i2 + (NP4 + NK // 4 + 2 * odd + 1 + (s + 2) // 4)) * 16)
                    act.wait_ge(s_pe, mm + (NK + 1))
                    act.activation(hl[:, s % 2, 0, :], raw[:, (s + 2) % 4, :], ACT.Copy).then_inc(s_hi, 1)

            with act.Fori(0, NB // 2 - 1) as b2:
                for odd in range(2):
                    for i2 in range(2):
                        for s in range(4):
                            second(b2, odd, i2, s)
            for mm in range(NK - 16, NK - 2):
                second(NB // 2 - 1, mm % 16 // 8, mm % 8 // 4, mm % 4, True, mm + 8 < NK)
            act.wait_ge(s_x1, KD + NK)
            squares("final", x, KD)
            root("final")
            shifts("final", yo, SHF)

        @block.vector
        def _(dve):
            n = [0]

            def link(ins):
                n[0] += 1
                ins.then_inc(s_v, 1)
                dve.wait_ge(s_v, n[0])

            def tt(o, a, b, op):
                link(dve.tensor_tensor(o, a, b, op))

            def cmul(o, a, b, t):
                dve.tensor_tensor(o[0], a[0], b[0], ALU.mult)
                tt(t, a[1], b[1], ALU.mult)
                tt(o[0], o[0], t, ALU.subtract)
                dve.tensor_tensor(o[1], a[0], b[1], ALU.mult)
                tt(t, a[1], b[0], ALU.mult)
                tt(o[1], o[1], t, ALU.add)

            def k(i):
                return K[:, i, :]

            def exp_exact(dst, src, t, r, p):
                link(dve.tensor_scalar(t, src, LOG2E, MAGIC, ALU.mult, ALU.add))
                link(dve.tensor_scalar(t, t, MAGIC, None, ALU.subtract))
                link(dve.tensor_scalar(t, t, 127.0, -126.0, ALU.min, ALU.max))
                link(dve.scalar_tensor_tensor(r, t, -LN2_HI, src, ALU.mult, ALU.add))
                link(dve.scalar_tensor_tensor(r, t, -LN2_LO, r, ALU.mult, ALU.add))
                link(dve.tensor_scalar(p, r, 1.0 / 5040, None, ALU.mult))
                for c in (1 / 720, 1 / 120, 1 / 24, 1 / 6, 0.5, 1.0):
                    link(dve.scalar_tensor_tensor(p, p, c, r, ALU.add, ALU.mult))
                link(dve.tensor_scalar(t, t, 127.0, None, ALU.add))
                link(dve.tensor_copy(ki[:], t))
                link(dve.tensor_scalar(ki[:], ki[:], 23, None, ALU.logical_shift_left))
                link(dve.scalar_tensor_tensor(dst, p, 1.0, ki[:].bitcast(F32), ALU.add, ALU.mult))

            dve.wait_ge(s_small, 16 * NSMALL)
            lr, li, ldt = par[:, 0, :], par[:, 1, :], par[:, 2, :]
            DT, X1, X8, MAG, MAG8, ANG = k(0), k(1), k(2), k(3), k(4), k(5)
            exp_exact(DT, ldt, k(6), k(7), k(8))
            tt(X1, lr, DT, ALU.mult)
            tt(ANG, li, DT, ALU.mult)
            link(dve.tensor_scalar(X8, X1, float(L), None, ALU.mult))
            exp_exact(MAG, X1, k(6), k(7), k(8))
            exp_exact(MAG8, X8, k(6), k(7), k(8))
            link(dve.tensor_scalar(k(6), ANG, INV2PI, MAGIC, ALU.mult, ALU.add))
            link(dve.tensor_scalar(k(6), k(6), MAGIC, None, ALU.subtract))
            link(dve.scalar_tensor_tensor(k(7), k(6), -TWO_PI_HI, ANG, ALU.mult, ALU.add))
            link(dve.scalar_tensor_tensor(k(10), k(6), -TWO_PI_LO, k(7), ALU.mult, ALU.add))
            link(dve.tensor_scalar(k(11), k(10), 0.5 * 3.141592653589793, None, ALU.add))
            link(dve.tensor_scalar(k(6), k(11), PI_IN, -2 * 3.141592653589793, ALU.is_gt, ALU.mult))
            tt(k(11), k(11), k(6), ALU.add)
            dve.tensor_scalar(K[:, 10:12, :], K[:, 10:12, :], PI_IN, -PI_IN, ALU.min, ALU.max).then_inc(s_trig_in, 1)
            dve.wait_ge(s_trig, 1)
            SIN, COS = k(12), k(13)
            dve.memset(PW[:, 0, :, 0:1], 1.0)
            dve.memset(PW[:, 1, :, 0:1], 0.0)
            tt(PW[:, 0, :, 1], MAG, COS, ALU.mult)
            tt(PW[:, 1, :, 1], MAG, SIN, ALU.mult)
            for m in (1, 2, 4):
                def wide(a):
                    return PW[:, a, :, m:m + 1].broadcast_to([P, ST, m])
                tmp = K[:, 14:14 + m, :].rearrange("p m t -> p t m")
                cmul([PW[:, a, :, m + 1:2 * m + 1] for a in (0, 1)], [wide(0), wide(1)],
                     [PW[:, a, :, 1:m + 1] for a in (0, 1)], tmp)
            for r in range(L + 1):
                last = dve.tensor_copy(PR[:, :, :, r], PW[:, :, :, L - r])
            link(last)
            AM, DEN, CR, CI = k(14), k(15), k(16), k(17)
            dve.tensor_scalar(AM, PW[:, 0, :, 1], -1.0, None, ALU.add)
            tt(DEN, lr, lr, ALU.mult)
            tt(k(18), li, li, ALU.mult)
            tt(DEN, DEN, k(18), ALU.add)
            link(dve.reciprocal(DEN, DEN))
            dve.tensor_tensor(CR, AM, lr, ALU.mult)
            tt(k(18), PW[:, 1, :, 1], li, ALU.mult)
            tt(CR, CR, k(18), ALU.add)
            dve.tensor_tensor(CI, PW[:, 1, :, 1], lr, ALU.mult)
            tt(k(18), AM, li, ALU.mult)
            tt(CI, CI, k(18), ALU.subtract)
            tt(CR, CR, DEN, ALU.mult)
            tt(CI, CI, DEN, ALU.mult)

            def per_state(a, n):
                return a.rearrange("p (t o) -> p t o", o=1).broadcast_to([P, ST, n])

            cmul([Bb[:, 0], Bb[:, 1]], [per_state(CR, SQ), per_state(CI, SQ)], [bm[:, 0], bm[:, 1]], xt[:, :, 0, :])
            def modulations(pair):
                dve.wait_ge(s_adt, pair + 1)
                cols = ps[:, 6, 0:KD * (32 + 1 + TS)].rearrange("p (q s) -> p q s", q=KD)
                for c in range(2):
                    f0 = (2 * pair + c) * KD
                    last = dve.tensor_tensor(mods[:, f0:f0 + KD, :], cols[:, :, 32 * c:32 * c + 1 + TS],
                                             bada[:, f0:f0 + KD].rearrange("p (f o) -> p f o", o=1).broadcast_to(
                                                 [P, KD, 1 + TS]), ALU.add)
                last.then_inc(s_mods, 1)
                dve.wait_ge(s_mods, pair + 1)

            def gain(i, first):
                g = ngain[:, i].rearrange("p (f o) -> p f o", o=1).broadcast_to([P, KD, 1 + TS])
                link(dve.scalar_tensor_tensor(gsc[:, i], mods[:, first:first + KD, :], 1.0, g, ALU.add, ALU.mult))

            def variance(norm, width):
                dve.wait_ge(s_stat, STAT[norm])
                for h, (a, b) in enumerate(HALVES):
                    last = dve.tensor_scalar(rstd[:, a:b], ps[:, 4 + h, 0:b - a], 1.0 / width, EPS, ALU.mult, ALU.add)
                link(last)
                dve.reciprocal(rstd[:], rstd[:]).then_inc(s_rec, 1)
                dve.wait_ge(s_rstd, RSTD[norm])

            def apply_norm(norm, dst, first):
                i = APPLY[norm]
                for q in range(KD):
                    dve.scalar_tensor_tensor(dst[:, q, 0:TP], x[:, q, 0:TP], gsc[:, i, q, 0:1], rstd[:, 0:TP],
                                             ALU.mult, ALU.mult).then_inc(s_hs, 1)
                r = rstd[:, TP:T].rearrange("p (o s) -> p o s", o=1).broadcast_to([P, KD, TS])
                tt(smalls[:], x[:, :, TP:T], r, ALU.mult)
                tt(smalls[:], smalls[:], gsc[:, i, :, 1:1 + TS], ALU.mult)
                dve.tensor_tensor(dst[:, :, TP:T], smalls[:], mods[:, first:first + KD, 1:1 + TS], ALU.add)\
                    .then_inc(s_hs, 1)

            variance("rms1", D)
            modulations(0)
            gain(0, SC1)
            apply_norm("rms1", h1, SH1)

            dve.wait_ge(s_const, 1)

            def powers(src, first):
                return [src[:, a, :, first:first + L].rearrange("p t (m o) -> p t m o", o=1).broadcast_to([P, ST, L, SQ])
                        for a in (0, 1)]

            def over(m4):
                return [m4[:, a].rearrange("p t (o q) -> p t o q", o=1).broadcast_to([P, ST, L, SQ]) for a in (0, 1)]

            cmul([XR[:, :, 0:L, :], XI[:, :, 0:L, :]], powers(PR, 1), over(Bb), xt)
            for g2 in range(2):
                rows = slice(64 * g2, 64 * g2 + 64)
                dve.tensor_copy(Cbd[rows, 0, :, g2, :], cm[rows, 0])
                dve.tensor_scalar(Cbd[rows, 1, :, g2, :], cm[rows, 1], -1.0, None, ALU.mult).then_inc(s_Xr, 1)
            cmul([FO[:, 0], FO[:, 1]], powers(PW, 1), over(cm), xt)
            dve.tensor_scalar(FO[:, 1], FO[:, 1], -1.0, None, ALU.mult).then_inc(s_Fr, 1)
            cmul([k(20), k(21)], [COS, SIN], [COS, SIN], k(18))
            cmul([k(22), k(23)], [k(20), k(21)], [k(20), k(21)], k(18))
            cmul([k(20), k(21)], [k(22), k(23)], [k(22), k(23)], k(18))
            for i in range(5):
                q = (k(20 + 2 * i), k(21 + 2 * i))
                cmul([k(22 + 2 * i), k(23 + 2 * i)], q, q, k(18))
            dve.memset(hc[:, :, 0:CW - 1], 0.0)

            for t in range(CT):
                dve.wait_ge(s_win, CT + 2 * t + 2)
                dve.wait_ge(s_sig, t + 1)
                rows = natural(hc[:, t, CW - 1:CW - 1 + TP])
                for h in range(2):
                    dve.tensor_tensor(rows[:, 4 * h:4 * h + 4, :],
                                      ps[:, h, 0:TP // 2].rearrange("p (i c) -> p i c", i=4),
                                      sq[:, 0, h * 256:h * 256 + 256].rearrange("p (i c) -> p i c", i=4), ALU.mult)
                dve.tensor_tensor(stc[:, t, :, CW - 1], ps[:, 1, TP // 2:TP // 2 + TS], sq[:, 0, TP:T],
                                  ALU.mult).then_inc(s_hc, 1)
            dve.wait_ge(s_hc, CT)

            dve.wait_ge(s_prep, 12)
            dve.memset(R[:, 0, :, 0:1], 1.0)
            link(dve.memset(R[:, 1, :, 0:1], 0.0))
            for i in range(6):
                m = 1 << i
                q = [per_state(k(20 + 2 * i + a), m) for a in (0, 1)]
                cmul([R[:, a, :, m:2 * m] for a in (0, 1)], q, [R[:, a, :, 0:m] for a in (0, 1)], wt[:, :, 0:m])
            dve.wait_ge(s_Ve, 6)
            vr, vi = V[:, 0, :, 0:NC], V[:, 1, :, 0:NC]
            dve.tensor_tensor(W2[:, 0], vr, R[:, 0], ALU.mult)
            tt(wt[:], vi, R[:, 1], ALU.mult)
            tt(W2[:, 0], W2[:, 0], wt[:], ALU.add)
            dve.tensor_tensor(W2[:, 1], vi, R[:, 0], ALU.mult)
            tt(wt[:], vr, R[:, 1], ALU.mult)
            tt(W2[:, 1], W2[:, 1], wt[:], ALU.subtract)
            link(dve.tensor_copy(wt[:], per_state(MAG8, NC)))
            link(dve.memset(wt[:, :, 0:1], 0.0))
            wtf = wt[:, :, :].rearrange("p t c -> p (t c)")
            for a in range(2):
                link(dve.tensor_tensor_scan(W2f[:, a, :], wtf, W2f[:, a, :], 0.0, ALU.mult, ALU.add))
            dve.tensor_tensor(V[:, 0, :, 0:NC], W2[:, 0], R[:, 0], ALU.mult)
            tt(wt[:], W2[:, 1], R[:, 1], ALU.mult)
            dve.tensor_tensor(S[:, 0, :, 1:NC], V[:, 0, :, 0:NC - 1], wt[:, :, 0:NC - 1], ALU.subtract)
            tt(ssp[:, 0, :], V[:, 0, :, NC - 1], wt[:, :, NC - 1], ALU.subtract)
            dve.tensor_tensor(V[:, 1, :, 0:NC], W2[:, 0], R[:, 1], ALU.mult)
            tt(wt[:], W2[:, 1], R[:, 0], ALU.mult)
            tt(S[:, 1, :, 1:NC], V[:, 1, :, 0:NC - 1], wt[:, :, 0:NC - 1], ALU.add)
            dve.tensor_tensor(ssp[:, 1, :], V[:, 1, :, NC - 1], wt[:, :, NC - 1], ALU.add)
            dve.tensor_copy(S[:, :, :, NC:NC + TS], h0[:]).then_inc(s_S, 1)
            modulations(1)
            a1 = [PW[:, a, :, 1:2].broadcast_to([P, ST, TS]) for a in (0, 1)]
            cmul([ssn[:, 0], ssn[:, 1]], a1, [h0[:, 0], h0[:, 1]], wt[:, :, 0:TS])
            dve.tensor_tensor(ssn[:], ssn[:], V[:, :, :, NC + TS:NC + 2 * TS], ALU.add).then_inc(s_S, 1)

            for t in range(CT):
                dve.tensor_scalar(cv[:, t, 0:TP], hc[:, t, 0:TP], cw[:, t, 0:1], cvec[:, 0, t:t + 1],
                                  ALU.mult, ALU.add).then_inc(s_cv, 1)
            for w in range(1, CW):
                for t in range(CT):
                    dve.wait_ge(s_cv, CT * (w - 1) + t + 1)
                    dve.scalar_tensor_tensor(cv[:, t, 0:TP], hc[:, t, w:w + TP], cw[:, t, w:w + 1], cv[:, t, 0:TP],
                                             ALU.mult, ALU.add).then_inc(s_cv, 1)
            prod = wt[:, :, :].rearrange("p t c -> p (t c)")[:, 0:CT * TS * CW].rearrange(
                "p (t s w) -> p t s w", t=CT, s=TS)
            dve.wait_ge(s_S, 2)
            for t in range(CT):
                last = dve.tensor_tensor(prod[:, t], stc[:, t],
                                         cw[:, t, :].rearrange("p (o w) -> p o w", o=1).broadcast_to([P, TS, CW]), ALU.mult)
            link(last)
            link(dve.tensor_reduce(cv[:, :, TP:T], prod, AX.X, ALU.add))
            dve.tensor_tensor(cv[:, :, TP:T], cv[:, :, TP:T],
                              cvec[:, 0, :].rearrange("p (t o) -> p t o", o=1).broadcast_to([P, CT, TS]),
                              ALU.add).then_inc(s_cv, 1)

            modulations(2)
            gain(1, SC2)

            dve.wait_ge(s_stat, STAT["mean"])
            for h, (a, b) in enumerate(HALVES):
                mean = ps[:, 4 + h, 0:b - a].rearrange("p (o n) -> p o n", o=1).broadcast_to([P, CT, b - a])
                last = dve.scalar_tensor_tensor(cv[:, :, a:b], mean, -1.0 / CC, cv[:, :, a:b], ALU.mult, ALU.add)
            last.then_inc(s_cvd, 1)
            dve.wait_ge(s_cvd, 1)
            variance("conv", CC)
            dve.tensor_tensor(cv[:], cv[:], rstd[:].rearrange("p (o n) -> p o n", o=1).broadcast_to([P, CT, T]),
                              ALU.mult).then_inc(s_cn, 1)

            def residual(f, first_gate, done):
                q, gate, bank = x[:, f, :], mods[:, first_gate + f, :], 2 * (f % 2)
                dve.tensor_tensor(smalls[:, f, :], ps[:, bank + 1, 256:256 + TS], gate[:, 1:1 + TS],
                                  ALU.mult).then_inc(s_xs, 1)
                for h in range(2):
                    dve.scalar_tensor_tensor(q[:, h * 256:h * 256 + 256], ps[:, bank + h, 0:256], gate[:, 0:1],
                                             q[:, h * 256:h * 256 + 256], ALU.mult, ALU.add)
                dve.wait_ge(s_xs, done)
                dve.tensor_tensor(q[:, TP:T], q[:, TP:T], smalls[:, f, :], ALU.add).then_inc(s_x1, 1)

            for q in range(KD):
                dve.wait_ge(s_mix, q + 1)
                residual(q, G1, q + 1)
            variance("rms2", D)
            dve.wait_ge(s_os, 16 * (CT + 3))
            apply_norm("rms2", h2f, SH2)
            for q in range(KD):
                dve.wait_ge(s_h2s, q + 1)
                dve.tensor_tensor(h2[:, 1, q, :], h2f[:, q, :], h2[:, 0, q, :].bitcast(F32), ALU.subtract).then_inc(s_h2l, 1)

            modulations(3)
            gain(2, SCF)

            A = slice(0, TT)
            dve.wait_ge(s_h2l, KD)
            dve.wait_ge(s_act, NTT)
            for t in range(NTT):
                def top16(vals, idx, src, width):
                    link(dve.max(vals[:, 0:8], src))
                    dve.max_index(idx[:, 0:8], vals[:, 0:8], src)
                    link(dve.match_replace(wk[A, 0:width], vals[:, 0:8], src, NEG))
                    link(dve.max(vals[:, 8:16], wk[A, 0:width]))
                    link(dve.max_index(idx[:, 8:16], vals[:, 8:16], wk[A, 0:width]))

                for h in range(HEADS):
                    for s in range(2):
                        top16(v16[A, h, s, :], i16[A, h, s, :], sc[A, t, 2 * h + s, :], NK)
                dve.tensor_copy(i16f[A], i16[A])
                for h in range(HEADS):
                    last = dve.tensor_tensor(cand[A, h],
                                             v16[A, h, 0, :].rearrange("p (a o) -> p a o", o=1).broadcast_to([TT, TOPK, TOPK]),
                                             v16[A, h, 1, :].rearrange("p (o a) -> p o a", o=1).broadcast_to([TT, TOPK, TOPK]),
                                             ALU.add)
                link(last)
                for h in range(HEADS):
                    top16(selv[A, t, 2, h * TOPK:(h + 1) * TOPK], pos[A, h * TOPK:(h + 1) * TOPK],
                          cand[A, h].rearrange("p a b -> p (a b)"), TOPK * TOPK)
                dve.tensor_scalar(rr[A, 0, :], pos[A, :], 4, None, ALU.logical_shift_right)
                link(dve.tensor_scalar(rr[A, 1, :], pos[A, :], 15, None, ALU.bitwise_and))
                link(dve.tensor_copy(rf[A], rr[A]))
                for s in range(2):
                    tt(eq[A], rf[A, s, :].rearrange("p (n o) -> p n o", o=1).broadcast_to([TT, NSEL, TOPK]),
                       iota[A, 0:TOPK].rearrange("p (o r) -> p o r", o=1).broadcast_to([TT, NSEL, TOPK]), ALU.is_equal)
                    eq4 = eq[A].rearrange("p (h n) r -> p h n r", h=HEADS)
                    tt(eq4, eq4, i16f[A, :, s, :].rearrange("p h (o r) -> p h o r", o=1).broadcast_to(
                        [TT, HEADS, TOPK, TOPK]), ALU.mult)
                    link(dve.tensor_reduce(selv[A, t, s, :], eq[A], AX.X, ALU.add))
            sc4 = selv[A, :, 2, :].rearrange("p t (h n) -> p t h n", h=HEADS)
            ex = eq[A].rearrange("p a b -> p (a b)")[:, 0:NTT * NSEL].rearrange("p (t h n) -> p t h n", t=NTT, h=HEADS)
            dve.tensor_tensor(ex, sc4, selv[A, :, 2, :].rearrange("p t (h n) -> p t h n", h=HEADS)[:, :, :, 0:1]
                              .broadcast_to([TT, NTT, HEADS, TOPK]), ALU.subtract).then_inc(s_exi, 1)
            dve.wait_ge(s_exo, 1)
            sums = rs[A, 0, :].rearrange("p (t h) -> p t h", t=NTT)
            link(dve.tensor_reduce(sums, sc4, AX.X, ALU.add))
            link(dve.reciprocal(rs[A, 1, :], rs[A, 0, :]))
            dve.tensor_tensor(sc4, sc4, rs[A, 1, :].rearrange("p (t h o) -> p t h o", t=NTT, o=1).broadcast_to(
                [TT, NTT, HEADS, TOPK]), ALU.mult).then_inc(s_top, 1)

            dve.wait_ge(s_gh, 1)
            dve.tensor_tensor(gp[:, 1, :], selT[:, 2, :], gp[:, 0, :].bitcast(F32), ALU.subtract).then_inc(s_gh, 1)
            dve.wait_ge(s_gh, 2)
            gpf = gp[:, :, :].bitcast(F32)

            def one_hots(it, s):
                tok = it * 4 + s
                after(dve, s_tok, tok - 3)
                if isinstance(tok, int):
                    col = slice(tok, tok + 1)
                else:
                    col = bass.ds(tok, 1)
                dve.tensor_scalar(ohA[:, s, :], iota[:], selT[:, 0, col], None, ALU.is_equal)
                last = dve.scalar_tensor_tensor(
                    ohB[:, s], iota[:].rearrange("p (o n) -> p o n", o=1).broadcast_to([P, 2, P]), selT[:, 1, col],
                    gpf[:, :, col].broadcast_to([P, 2, P]), ALU.is_equal, ALU.mult)
                last.then_inc(s_oh, 1)

            for s in range(4):
                one_hots(0, s)
            with dve.Fori(1, T // 4) as it:
                for s in range(4):
                    one_hots(it, s)

            def weigh(jj, slot, hslot, gloads, hloads, j):
                dve.wait_ge(s_gl[slot], gloads)
                dve.wait_ge(s_hl[hslot], hloads)
                after(dve, s_wl, j - 1)
                w = wf[:, hslot % 2, :]
                h = hring[:, hslot, :]
                dve.tensor_tensor(w[:, 0:TP].rearrange("p (k t) -> p k t", t=GBLK),
                                  h[:, 0:TP].rearrange("p (k t) -> p k t", t=GBLK),
                                  gbp[:, slot, :, jj, :], ALU.mult)
                dve.tensor_tensor(w[:, TP:T], h[:, TP:T], stages[:, j, :] if isinstance(j, int) else
                                  stages[:, bass.ds(j, 1), :].rearrange("p o t -> p (o t)"), ALU.mult).then_inc(s_w, 1)

            def low(jj, slot, j):
                dve.wait_ge(s_wh, j + 1)
                dve.tensor_tensor(WHL[slot][:, 1, jj, :], wf[:, jj % 2, :], WHL[slot][:, 0, jj, :].bitcast(F32),
                                  ALU.subtract).then_inc(s_wl, 1)

            dve.wait_ge(s_gadd, TP // TOK + 1)
            for j in range(JB):
                weigh(j, 0, j % 4, 16, 16 * (j // 4 + 1), j)
                if j:
                    low(j - 1, 0, j - 1)
            low(JB - 1, 0, JB - 1)

            def add_out(q, steps):
                dve.wait_ge(s_pe, steps)
                residual(q, G2, steps + (KD - NK))

            def second(b2, odd, jj, first, more_w=True):
                j = b2 * 16 + (odd * 8 + jj + 8)
                if more_w:
                    weigh(jj, 1 - odd, jj % 4, b2 * 16 + (16 if odd == 0 else 32),
                          (b2 * 4 + (2 * odd + 2 + jj // 4 + 1)) * 16, j)
                if not first:
                    add_out((jj - 1) % 8, b2 * 16 + (NK + odd * 8 + jj))
                if more_w:
                    low(jj, 1 - odd, j)

            for odd in range(2):
                for jj in range(JB):
                    second(0, odd, jj, odd == 0 and jj == 0)
            last_b2 = NB // 2 - 1
            with dve.Fori(1, last_b2) as b2:
                for odd in range(2):
                    for jj in range(JB):
                        second(b2, odd, jj, False)
            for odd in range(2):
                for jj in range(JB):
                    second(last_b2, odd, jj, False, odd == 0)
            add_out(KD - 1, 2 * NK)
            variance("final", D)
            apply_norm("final", yo, SHF)

        @block.tensor
        def _(pe):
            def tile(n_):
                pe.wait_ge(s_raw[n_ % NRAW], 16 * (n_ // NRAW + 1))

            def modulation_rows(pair, tiles=range(PAIR)):
                for i in tiles:
                    n_ = STREAM.index(("ada", PAIR * pair + i))
                    c, q = divmod(i, KD)
                    tile(n_)
                    if i == 0:
                        after(pe, s_mods, pair)
                    for h in range(2):
                        last = pe.matmul(ps[32 * c:32 * c + 1 + TS, 6 + h, :], sil[:, q, :],
                                         raw[:, n_ % NRAW, h * 512:(h + 1) * 512], start=q == 0, stop=q == KD - 1)
                    last.then_inc(s_mod, 1)

            def modulation_columns(pair):
                pe.wait_ge(s_ade, pair + 1)
                w = 32 + 1 + TS
                for q in range(KD):
                    last = pe.transpose(ps[:, 6, q * w:(q + 1) * w], adaR[0:w, q * P:(q + 1) * P], ident[0:w, 0:w])
                last.then_inc(s_adt, 1)

            def dense(n_, rows, count, bank, sem_):
                tile(n_)
                for q in range(count):
                    for h, (a, b) in enumerate(HALVES):
                        last = pe.matmul(ps[:, bank + h, 0:b - a], raw[:, n_ % NRAW, q * P:(q + 1) * P], rows[:, q, a:b],
                                         start=q == 0, stop=q == count - 1)
                last.then_inc(sem_, 1)

            def column_sums(rows_of, count, ready, summed):
                for q in range(count):
                    if ready is not None:
                        pe.wait_ge(s_sq, ready + q + 1)
                    r = rows_of(q)
                    for h, (a, b) in enumerate(HALVES):
                        last = pe.matmul(ps[:, 4 + h, 0:b - a], ones[:], r[:, a:b], start=q == 0, stop=q == count - 1)
                    if q < count - 1 and summed:
                        last.then_inc(s_squ, 1)
                last.then_inc(s_stat, 1)

            def sq_rows(q):
                return sq[:, q % 2, :]

            pe.wait_ge(s_sil, 1)
            modulation_rows(0, range(KD))
            pe.wait_ge(s_const, 1)
            column_sums(sq_rows, KD, SQ_BEFORE["rms1"], True)
            modulation_rows(0, range(KD, PAIR))
            modulation_columns(0)
            pe.wait_ge(s_h, KD)
            pe.wait_ge(s_hs, KD + 1)
            for w in range(12):
                if w in (2, 3, 4, 5):
                    pe.wait_ge(s_uev, w - 1)
                elif w >= 6:
                    pe.wait_ge(s_hc, (w - 4) // 2)
                dense(FIRST["in"] + w, h1, KD, 2 * (w % 2), s_win)
            pe.wait_ge(s_Xr, 2)
            X = (XR, XI)
            for e in range(20):
                if e >= 2:
                    pe.wait_ge(s_prepe, e - 1)
                bank = 4 + e % 2
                if e < 4:
                    for j in range(4):
                        for a in range(2):
                            last = pe.matmul(ps[32 * j:32 * j + 32, bank, 0:MQ],
                                             Cbd[:, a, 4 * e + j].rearrange("p g q -> p (g q)"),
                                             X[a][:, 4 * e + j].rearrange("p m q -> p (m q)"), start=a == 0, stop=a == 1)
                elif e < 12:
                    for j in range(4):
                        last = pe.transpose(ps[:, bank, j * P:(j + 1) * P],
                                            X[(e - 4) // 4][:, 4 * (e % 4) + j, 0:L, :].rearrange("p m q -> p (m q)"), ident[:])
                else:
                    n4, ih = divmod(e - 12, 2)
                    for j in range(4):
                        m = L - 1 - (4 * ih + j)
                        last = pe.transpose(ps[:, bank, j * P:(j + 1) * P], Kt[:, n4, m * SQ:m * SQ + P], ident[:])
                last.then_inc(s_prep, 1)
            pe.wait_ge(s_prepe, 20)
            pe.wait_ge(s_hc, CT)
            pe.wait_ge(s_ul, 16 * (L + 2))
            for t in range(ST):
                for g in range(2):
                    for a in range(2):
                        c = (t % 6) * (NC + 2 * TS)
                        last = pe.matmul(ps[64 * g:64 * g + 64, 3 * a + t // 6, c:c + NC + 2 * TS],
                                         ET[:, a, t, 64 * g:64 * g + 64], U[:, 2 * t + g, :], start=True, stop=True)
            last.then_inc(s_V, 1)
            modulation_rows(1)
            modulation_columns(1)
            pe.wait_ge(s_S, 1)
            pe.wait_ge(s_Fr, 1)
            pe.wait_ge(s_Ve, 6)
            for g in range(2):
                rows = slice(64 * g, 64 * g + 64)
                if g == 1:
                    pe.wait_ge(s_mods, 2)
                for t in range(ST):
                    o = ps[0:NC + TS, 4 * g + t // 4, (t % 4) * P:(t % 4 + 1) * P]
                    pe.matmul(o, U[:, 2 * t + g, 0:NC + TS], Tm[:, 2 * t + g, :], start=True, stop=False)
                    for a in range(2):
                        last = pe.matmul(o, S[rows, a, t], FO[rows, a, t].rearrange("p i q -> p (i q)"),
                                         start=False, stop=a == 1)
                last.then_inc(s_Y, 1)
            pe.wait_ge(s_dg, CT)
            for t in range(CT):
                pe.wait_ge(s_Ye, 2 * t + 2)
                for h in range(2):
                    o = ps[:, 4 * h + t, 0:4 * (NC + TS)].rearrange("p (i c) -> p i c", i=4)
                    if h == 0:
                        pe.matmul(o[:, 0, NC:NC + TS], dskip[:, t, :], uT[:, t, TP:T], start=True, stop=False)
                        pe.matmul(o[:, 0, NC:NC + TS], Ysb[:, t, 0, :], ident[0:NC + TS, NC:NC + TS], start=False, stop=True)
                    pe.matmul(o[:, :, 0:NC], dskip[:, t, :], uT[:, t, h * 256:(h + 1) * 256], start=True, stop=False)
                    for i in range(4):
                        last = pe.matmul(o[:, i, 0:NC], Ysb[0:NC, t, 4 * h + i, :], ident[0:NC, 0:NC],
                                         start=False, stop=i == 3)
                last.then_inc(s_yt, 1)
            pe.wait_ge(s_z, CT)
            for w in range(CT):
                if w >= 2:
                    pe.wait_ge(s_gsig, w - 1)
                dense(FIRST["glu"] + w, yT, CT, 2 * (w % 2), s_glu)
            modulation_rows(2)
            modulation_columns(2)
            pe.wait_ge(s_cv, CT * CW + 1)
            column_sums(lambda q: cv[:, q, :], CT, None, False)
            column_sums(sq_rows, CT, SQ_BEFORE["conv"], True)
            modulation_rows(3, range(KD))
            pe.wait_ge(s_hsm, CT)
            pe.wait_ge(s_hcm, CT)
            for w in range(KD):
                if w >= 2:
                    pe.wait_ge(s_x1, w - 1)
                dense(FIRST["out"] + w, mixin, KD, 2 * (w % 2), s_mix)
            column_sums(sq_rows, KD, SQ_BEFORE["rms2"], True)
            modulation_rows(3, range(KD, PAIR))
            pe.wait_ge(s_h, 2 * KD)
            pe.wait_ge(s_hs, 2 * (KD + 1))
            for w in range(KD):
                if w >= 2:
                    pe.wait_ge(s_qe, w - 1)
                dense(FIRST["q"] + w, h2f, KD, 2 * (w % 2), s_q)
            modulation_columns(3)
            pe.wait_ge(s_keys, 32)
            pe.wait_ge(s_qe, KD)
            pe.wait_ge(s_mods, 4)
            for t in range(NTT):
                if t >= 2:
                    pe.wait_ge(s_act, t - 1)
                for h in range(HEADS):
                    last = pe.matmul(ps[0:TT, 4 * (1 - t % 2) + h // 2, (h % 2) * 2 * NK:(h % 2 + 1) * 2 * NK],
                                     qT[:, h, t * TT:(t + 1) * TT], keys[:, h].rearrange("p s n -> p (s n)"),
                                     start=True, stop=True)
                last.then_inc(s_sc, 1)

            PASSES = ((0, 0), (0, 1), (1, 0))

            def token(step, w, tok):
                if w % 2 == 0:
                    pe.wait_ge(s_gev, step * 4 + (3 + w // 2))
                pe.wait_ge(s_oh, tok + 1)
                pe.matmul(ps[:, 4 + w // 2, (w % 2) * 2 * NK:(w % 2 + 1) * 2 * NK], ohA[:, w % 4, :],
                          ohB[:, w % 4].rearrange("p a n -> p (a n)"), start=True, stop=True).then_inc(s_tok, 1)

            def first_product(s, m, step=None):
                pe.wait_ge(s_lo, m + 1)
                pe.wait_ge(s_act, m + (NTT - 1))
                for q in range(KD):
                    for w, r in PASSES:
                        for h, (a, b) in enumerate(HALVES):
                            last = pe.matmul(ps[:, 2 * s + h, 0:b - a], hl[:, s, w, q * P:(q + 1) * P], h2[:, r, q, a:b],
                                             start=q == 0 and (w, r) == (0, 0), stop=q == KD - 1 and (w, r) == (1, 0))
                    if step is not None and q < KD - 1:
                        token(step, q, step * TOK + q)
                last.then_inc(s_pe, 1)
                if step is not None:
                    token(step, TOK - 1, step * TOK + TOK - 1)

            pe.wait_ge(s_h2l, KD)
            with pe.Fori(0, A1 // 2) as it:
                for s in range(2):
                    first_product(s, it * 2 + s)
            pe.wait_ge(s_top, 1)
            pe.wait_ge(s_act, NTT)
            for kind in range(3):
                for t in range(NTT):
                    o = ps[:, 4 + kind, t * TT:(t + 1) * TT] if t < 4 else ps[:, 7, kind * TT:(kind + 1) * TT]
                    last = pe.transpose(o, selv[0:TT, t, kind, :], ident[0:TT, 0:TT])
            last.then_inc(s_selp, 1)
            with pe.Fori(0, TP // TOK // 2) as it:
                for s in range(2):
                    first_product(s, it * 2 + (A1 + s), it * 2 + s)
            first_product(0, NK - A3, TP // TOK)
            for m in range(NK - A3 + 1, NK):
                first_product(m % 2, m)

            def second_product(odd, s, mm):
                pe.wait_ge(s_wl, b2 * 16 + 8 * (odd + 1))
                pe.wait_ge(s_lo, mm + (NK + 1))
                pe.wait_ge(s_x1, mm + (KD - 1))
                for j in range(JB):
                    for w, r in PASSES:
                        for h, (a, b) in enumerate(HALVES):
                            last = pe.matmul(ps[:, 2 * s + h, 0:b - a], hl[:, s, w, j * P:(j + 1) * P],
                                             WHL[odd][:, r, j, a:b],
                                             start=j == 0 and (w, r) == (0, 0), stop=j == JB - 1 and (w, r) == (1, 0))
                last.then_inc(s_pe, 1)

            pe.wait_ge(s_act, NTT + NK)
            with pe.Fori(0, NB // 2) as b2:
                for odd in range(2):
                    with pe.Fori(0, JB // 2) as i2:
                        for s in range(2):
                            second_product(odd, s, b2 * 16 + i2 * 2 + (odd * 8 + s))
            column_sums(sq_rows, KD, SQ_BEFORE["final"], True)


_OUTS = {"y": (P, KD, T), "conv_p": (P, CT, CW - 1), "conv_s": (P, CT, TS, CW - 1),
         "ssm_p": (P, 2, ST), "ssm_s": (P, 2, ST, TS)}


def layout(i):
    import numpy as np

    def cols(prompt, sample):
        chunked = prompt.reshape(NC, L, D).transpose(1, 0, 2).reshape(TP, D)
        return np.concatenate([chunked, sample], 0).T.reshape(KD, P, T).transpose(1, 0, 2)

    def tiles(w):
        k, n = w.shape
        return w.reshape(k // P, P, n // P, P).transpose(2, 1, 0, 3).reshape(n // P, P, k)

    def slabs(w):
        k, n = w.shape
        return w.reshape(k // P, P, n // RAW, RAW).transpose(2, 0, 1, 3).reshape(-1, P, RAW)

    def per_partition(v):
        return v.reshape(-1, P).T

    def states(v):
        return v.reshape(ST, P, -1).transpose(1, 0, 2)

    a = {
        "x": cols(i["x_prompt"][0], i["x_sample"][:, 0]),
        "cT": np.concatenate([i["c_prompt"], i["c_sample"]], 0).T.reshape(KD, P, 1 + TS).transpose(1, 0, 2),
        "par": np.stack([per_partition(i["ssm_lambda_re"][0].reshape(-1)), per_partition(i["ssm_lambda_im"][0].reshape(-1)),
                         per_partition(np.repeat(i["ssm_log_dt"][0], SN))], 1),
        "bm": np.stack([states(i["ssm_b_re"][0]), states(i["ssm_b_im"][0])], 1),
        "cm": np.stack([states(i["ssm_c_re"][0].transpose(0, 2, 1)), states(i["ssm_c_im"][0].transpose(0, 2, 1))], 1),
        "h0": np.stack([states(i[n][0].reshape(TS, SG * SN).T) for n in ("state_ssm_re", "state_ssm_im")], 1),
        "stc": i["state_conv"][0].transpose(2, 0, 1).reshape(CT, P, TS, CW - 1).transpose(1, 0, 2, 3),
        "cw": i["conv_w"][0].T.reshape(CT, P, CW).transpose(1, 0, 2),
        "cvec": np.stack([per_partition(i[n][0]) for n in ("conv_b", "conv_ln_g", "conv_ln_b", "ssm_d")], 1),
        "bada": np.concatenate([per_partition(i["b_ada"][0]), per_partition(i["b_ada_final"])], 1),
        "ngain": np.stack([per_partition(v) for v in (i["norm1_g"][0], i["norm2_g"][0], i["final_norm_g"])], 1),
        "w_ada": np.concatenate([slabs(i["w_ada"][0]), slabs(i["w_ada_final"])], 0),
        "w_in": tiles(i["w_in"][0]),
        "w_glu": tiles(i["ssm_w_glu"][0]),
        "w_out": tiles(i["w_out"][0]),
        "w_q": tiles(i["peer_w_q"][0]),
        "keys": i["peer_keys"][0].transpose(1, 3, 0, 2).reshape(P, HEADS, NK),
        "u": i["peer_u"][0].reshape(P, NK, KD, P).transpose(1, 3, 2, 0).reshape(NK, P, RAW),
        "v": i["peer_v"][0].reshape(P, NB, JB, KD, P).transpose(1, 3, 0, 2, 4).reshape(NB * KD, P, RAW),
    }
    return {n: np.ascontiguousarray(v) for n, v in a.items()}


def kernel(**inputs):
    import numpy as np
    import concourse.bacc as bacc
    from concourse.bass_utils import run_bass_kernel_spmd

    inputs = {n: np.asarray(v) for n, v in inputs.items()}
    nc = bacc.Bacc("TRN2", target_bir_lowering=False, num_devices=1)
    arrays = layout(inputs)
    dr = {n: nc.dram_tensor(f"in_{n}", a.shape, F32, kind="ExternalInput").ap() for n, a in arrays.items()}
    out = {n: nc.dram_tensor(f"out_{n}", s, F32, kind="ExternalOutput").ap() for n, s in _OUTS.items()}
    build(nc, dr, out)
    r = run_bass_kernel_spmd(nc, [{f"in_{n}": a for n, a in arrays.items()}], core_ids=[0]).results[0]
    y = r["out_y"].transpose(1, 0, 2).reshape(D, T).T
    y_prompt = y[:TP].reshape(L, NC, D).transpose(1, 0, 2).reshape(1, TP, D)
    conv_p = r["out_conv_p"].transpose(2, 1, 0).reshape(1, 1, CW - 1, CC)
    conv_s = r["out_conv_s"].transpose(2, 3, 1, 0).reshape(1, TS, CW - 1, CC)
    ssm_p = r["out_ssm_p"].transpose(1, 2, 0).reshape(2, 1, 1, SG, SN)
    ssm_s = r["out_ssm_s"].transpose(1, 3, 2, 0).reshape(2, 1, TS, SG, SN)
    c = np.ascontiguousarray
    return (c(y_prompt), c(y[TP:].reshape(TS, 1, D)), c(conv_p), c(conv_s), c(ssm_p[0]), c(ssm_p[1]), c(ssm_s[0]), c(ssm_s[1]))
```

```python
from contextlib import ExitStack

import concourse.bass as bass
from concourse import mybir

F32 = mybir.dt.float32
F32R = mybir.dt.float32r
U32 = mybir.dt.uint32
I32 = mybir.dt.int32
ALU = mybir.AluOpType
ACT = mybir.ActivationFunctionType
AX = mybir.AxisListType

P = 128
D = 1024
KD = D // P
TP, TS = 512, 8
T = TP + TS
L = 8
NC = TP // L
HALVES = ((0, TP // 2), (TP // 2, T))
CC = 512
CT = CC // P
CW = 31
SG, SQ, SN = 32, 16, 64
ST = SG * SN // P
HEADS, NK, TOPK, DK = 8, 128, 16, 64
NSEL = HEADS * TOPK
RC = 4
NCAND = RC * TOPK + (TOPK - RC) * RC
TT = 104
NTT = T // TT
EPS = 1e-6
NRAW = 4
RAW = 1024
JB = 8
NB = NK // JB
A3 = 8
A1 = NK - TP // 8 - A3
TOK = 8
GBLK = 16
HR = 2
NSMALL = 12
NMOD = 64
SH1, SC1, G1, SH2, SC2, G2, SHF, SCF = (8 * i for i in range(8))
INV2PI = 0.15915494309189535
TWO_PI_HI = 6.28125
TWO_PI_LO = 2 * 3.141592653589793 - 6.28125
MAGIC = 12582912.0
LOG2E = 1.4426950408889634
LN2_HI = 0.693359375
LN2_LO = -2.12194440e-4
PI_IN = 3.1415925
NEG = -3.0e38

PAIR = 16

EARLY = 4
LATE = 8

STREAM = ([("ada", f) for f in range(PAIR)]
          + [("ada", f) for f in range(PAIR, PAIR + EARLY)]
          + [("in", f) for f in (8, 9, 10, 11, 0, 4, 1, 5, 2, 6, 3, 7)]
          + [("ada", f) for f in range(PAIR + EARLY, 2 * PAIR)]
          + [("glu", f) for f in range(4)]
          + [("ada", f) for f in range(2 * PAIR, 3 * PAIR)]
          + [("ada", f) for f in range(3 * PAIR, 3 * PAIR + LATE)]
          + [("out", f) for f in range(8)]
          + [("ada", f) for f in range(3 * PAIR + LATE, 4 * PAIR)]
          + [("q", f) for f in range(8)])
NPRE = len(STREAM)
SPLIT = [_n for _n, (_kind, _) in enumerate(STREAM) if _kind in ("in", "out", "q")]
NSP = len(SPLIT)
FSP = {_kind: [STREAM[_n][0] for _n in SPLIT].index(_kind) for _kind in ("in", "out", "q")}
assert NSP % 2 == 0
assert NPRE % NRAW == 0
FIRST = {}
for _n, (_kind, _f) in enumerate(STREAM):
    FIRST.setdefault(_kind, _n)


def after(eng, sem, value):
    if isinstance(value, int) and value <= 0:
        return
    eng.wait_ge(sem, value)


def build(nc, dr, out):
    with ExitStack() as base:
        def sb(stack, name, shape, dt=F32):
            return stack.enter_context(nc.sbuf_tensor(name, shape, dt))

        def sem(name):
            return base.enter_context(nc.semaphore(name))

        hd = nc.dram_tensor("act_spill", [NK, P, T], F32, kind="Internal").ap()
        gpd = nc.dram_tensor("gate_spill", [NB, P, TP // GBLK, JB * GBLK], F32, kind="Internal").ap()
        ud = nc.dram_tensor("u_shuffle", [SG, SQ, L, NC], F32, kind="Internal").ap()
        usd = nc.dram_tensor("u_sample_shuffle", [SG, SQ, TS], F32, kind="Internal").ap()

        x = sb(base, "x_res", [P, KD, T])
        mods = sb(base, "mods", [P, NMOD, 1 + TS])
        gsc = sb(base, "gsc", [P, 3, KD, 1 + TS])
        bada = sb(base, "bada_sb", [P, NMOD])
        ngain = sb(base, "ngain_sb", [P, 3, KD])
        ones = sb(base, "ones", [P, P])
        ident = sb(base, "ident", [P, P])
        iota = sb(base, "iota", [P, P])
        rstd = sb(base, "rstd", [P, T])
        sq = sb(base, "sq", [P, 2, T])
        smalls = sb(base, "smalls", [P, KD, TS])
        sil = sb(base, "sil", [P, KD, 1 + TS])
        adaR = sb(base, "adaR", [P, RAW])
        raw = sb(base, "raw", [P, NRAW, RAW])

        ps = base.enter_context(nc.psum_tensor("ps", [P, 8, 512], F32))

        with ExitStack() as s5:
            with ExitStack() as lo_:
                h1lo = sb(lo_, "h1_lo", [P, KD, T], F32R)
                mixlo = sb(lo_, "mixin_lo", [P, KD, T], F32R)
            h1 = sb(s5, "h1", [P, KD, T])
            mixin = sb(s5, "mixin", [P, KD, T])
            uT = sb(s5, "uT", [P, CT, T])
            FO = sb(s5, "FO", [P, 2, ST, L, SQ])
            with ExitStack() as sp_:
                hlm = sb(sp_, "hlm", [P, 2, 2, RAW], F32R)
                rhi = sb(sp_, "rows_hi", [P, KD, T], F32R)
            ET = sb(s5, "ET", [P, 2, ST, P])
            Tm = sb(s5, "Tm", [P, SG, P])
            dskip = sb(s5, "dskip", [P, CT, P])
            U = sb(s5, "U", [P, SG, NC + 2 * TS])
            S = sb(s5, "S", [P, 2, ST, NC + TS])
            ssp = sb(s5, "ssp", [P, 2, ST])
            hc = sb(s5, "hc", [P, CT, CW - 1 + TP])
            stc = sb(s5, "stc_sb", [P, CT, TS, CW])
            cw = sb(s5, "cw_sb", [P, CT, CW])
            cvec = sb(s5, "cvec_sb", [P, 4, CT])
            cT = sb(s5, "cT_sb", [P, KD, 1 + TS])
            par = sb(s5, "par_sb", [P, 3, ST])
            bm = sb(s5, "bm_sb", [P, 2, ST, SQ])
            cm = sb(s5, "cm_sb", [P, 2, ST, SQ])
            h0 = sb(s5, "h0_sb", [P, 2, ST, TS])
            Bb = sb(s5, "Bb", [P, 2, ST, SQ])
            Cbd = sb(s5, "Cbd", [P, 2, ST, 2, SQ])
            PW = sb(s5, "PW", [P, 2, ST, L + 1])
            PR = sb(s5, "PR", [P, 2, ST, L + 1])
            K = sb(s5, "K", [P, 40, ST])
            ki = sb(s5, "ki", [P, ST], I32)
            ssn = sb(s5, "ssn", [P, 2, ST, TS])
            with ExitStack() as xs:
                XI = sb(xs, "XI", [P, ST, 2 * L - 1, SQ])
            with ExitStack() as vs:
                V = sb(vs, "V", [P, 2, ST, NC + 2 * TS])
                wt = sb(vs, "wt", [P, ST, NC])
        flat = mixin[:, :, :].rearrange("p k t -> p (k t)")
        XR = flat[:, 0:ST * (2 * L - 1) * SQ].rearrange("p (t m q) -> p t m q", t=ST, q=SQ)
        R = flat[:, 0:2 * ST * NC].rearrange("p (a t c) -> p a t c", a=2, t=ST)
        W2 = flat[:, 2 * ST * NC:4 * ST * NC].rearrange("p (a t c) -> p a t c", a=2, t=ST)
        W2f = flat[:, 2 * ST * NC:4 * ST * NC].rearrange("p (a n) -> p a n", a=2)
        xt = hc[:, :, :].rearrange("p a n -> p (a n)")[:, 0:ST * L * SQ].rearrange(
            "p (t m q) -> p t m q", t=ST, q=SQ)
        Ysb = ET[0:NC + TS, :, :, :].rearrange("p a t n -> p (a t n)").rearrange(
            "p (t i m) -> p t i m", t=CT, i=L)
        yT = h1[:, 0:CT, :]
        cv = h1[:, CT:2 * CT, :]
        MQ = (2 * L - 1) * SQ
        Kt = h1[:, 0:2, :].rearrange("p k t -> p (k t)")[:, 0:ST // 4 * MQ].rearrange("p (n m) -> p n m", m=MQ)

        with ExitStack() as tk:
            hl = sb(tk, "hl", [P, 2, 2, RAW], F32R)
            actr = sb(tk, "actr", [P, HR, T])
            with ExitStack() as tp:
                h2 = sb(tp, "h2", [P, 2, KD, T], F32R)
                ohA = sb(tp, "ohA", [P, 4, P], F32R)
                ohB = sb(tp, "ohB", [P, 4, 2, P], F32R)
                with ExitStack() as ss:
                    sc = sb(ss, "sc", [P, NTT, 2 * HEADS, NK])
                    with ExitStack() as qs:
                        h2f = sb(qs, "h2f", [P, KD, T])
                        qT = sb(qs, "qT", [P, HEADS, T])
                        keys = sb(qs, "keys_sb", [P, HEADS, 2, NK])
                    with ExitStack() as ts_:
                        wk = sb(ts_, "wk", [P, 2 * NK])
                        v16 = sb(ts_, "v16", [P, HEADS, 2, TOPK])
                        i16 = sb(ts_, "i16", [P, HEADS, 2, TOPK], U32)
                        i16f = sb(ts_, "i16f", [P, HEADS, 2, TOPK])
                        cand = sb(ts_, "cand", [P, HEADS, NCAND])
                        pos = sb(ts_, "pos", [P, NSEL], U32)
                        rr = sb(ts_, "rr", [P, 4, NSEL], U32)
                        rf = sb(ts_, "rf", [P, 4, NSEL])
                        late = sb(ts_, "late", [P, NSEL])
                        eq = sb(ts_, "eq", [P, NSEL, TOPK])
                        selv = sb(ts_, "selv", [P, NTT, 3, NSEL])
                        rs = sb(ts_, "rs", [P, 2, NTT * HEADS])
                        selT = sb(ts_, "selT", [P, 3, T])
                        gp = sb(ts_, "gp", [P, 2, T], F32R)
                with ExitStack() as sg:
                    stage = sb(sg, "stage", [P, 2, 2, NK, GBLK])
            with ExitStack() as cs:
                WH1 = sb(cs, "WH1", [P, 2, JB, T], F32R)
                sb(cs, "one_hots_place", [P, 4 * 3 * P])
                WH0 = sb(cs, "WH0", [P, 2, JB, T], F32R)
                hring = sb(cs, "hring", [P, 4, T])
                wf = sb(cs, "wf", [P, 2, T])
                gbp = sb(cs, "gbp", [P, 2, TP // GBLK, JB, GBLK])
        WHL = (WH0, WH1)
        yo = gbp[:, :, :, :, :].rearrange("p a k j t -> p (a k j t)")[:, 0:KD * T].rearrange(
            "p (k t) -> p k t", k=KD)

        stages = adaR[:, :].rearrange("p (j s) -> p j s", s=TS)

        s_small = sem("small_inputs_loaded")
        s_c = sem("c_loaded")
        s_xl = sem("x_loaded")
        s_raw = [sem(f"weight_tile_loaded_{i}") for i in range(NRAW)]
        s_const = sem("constants_written")
        s_sil = sem("silu_c_ready")
        s_sq = sem("square_ready")
        s_squ = sem("square_used")
        s_stat = sem("column_sums_ready")
        s_rec = sem("reciprocal_ready")
        s_rstd = sem("rstd_ready")
        s_hs = sem("normed_scaled")
        s_h = sem("normed_shifted")
        s_mod = sem("modulation_tile_summed")
        s_ade = sem("modulation_rows_copied")
        s_adt = sem("modulations_transposed")
        s_mods = sem("modulations_ready")
        s_win = sem("input_projection_ready")
        s_uev = sem("u_copied")
        s_sig = sem("gate_sigmoid_ready")
        s_hc = sem("glu_rows_ready")
        s_ush = sem("u_stored")
        s_ul = sem("u_chunks_loaded")
        s_v = sem("vector_chain")
        s_p = sem("pool_chain")
        s_trig_in = sem("angles_ready")
        s_trig = sem("sin_cos_ready")
        s_Xr = sem("chunk_input_factors_ready")
        s_Fr = sem("chunk_output_factors_ready")
        s_prep = sem("chunk_matrix_products")
        s_prepe = sem("chunk_matrices_copied")
        s_V = sem("chunk_inputs_ready")
        s_Ve = sem("chunk_inputs_copied")
        s_S = sem("chunk_states_ready")
        s_Y = sem("chunk_outputs_ready")
        s_Ye = sem("chunk_outputs_copied")
        s_dg = sem("skip_diagonals_written")
        s_yt = sem("y_with_skip_ready")
        s_z = sem("gelu_y_ready")
        s_glu = sem("glu_product_ready")
        s_gsig = sem("glu_sigmoid_ready")
        s_hsm = sem("s5_rows_ready")
        s_cv = sem("conv_steps")
        s_cvd = sem("conv_centred")
        s_cn = sem("conv_normed")
        s_hcm = sem("conv_rows_ready")
        s_h1s = sem("h1_samples_split_hi")
        s_h1l = sem("h1_split_lo")
        s_rh = sem("rows_split_hi")
        s_rl = sem("rows_split_lo")
        s_mix = sem("mix_product_ready")
        s_x1 = sem("residual_updated")
        s_xs = sem("samples_gated_product")
        s_kz = sem("keys_zeroed")
        s_keys = sem("keys_loaded")
        s_q = sem("query_product_ready")
        s_qe = sem("queries_copied")
        s_sc = sem("scores_ready")
        s_h2s = sem("h2_split_hi")
        s_h2l = sem("h2_split_lo")
        s_top = sem("selection_ready")
        s_exi = sem("softmax_exponents_in")
        s_exo = sem("softmax_exponents_out")
        s_selp = sem("selection_transposed")
        s_gh = sem("gates_split")
        s_hi = sem("weight_tile_hi")
        s_lo = sem("weight_tile_lo")
        s_pe = sem("peer_step_done")
        s_act = sem("activation_ready")
        s_hst = [sem(f"activation_stored_{i}") for i in range(HR)]
        s_oh = sem("one_hots_ready")
        s_tok = sem("token_gated")
        s_gev = sem("gates_copied")
        s_gadd = sem("gate_parts_added")
        s_gst = [sem(f"gates_stored_{i}") for i in range(2)]
        s_gl = [sem(f"gate_batch_loaded_{i}") for i in range(2)]
        s_hl = [sem(f"activation_loaded_{i}") for i in range(4)]
        s_w = sem("weighted_activation")
        s_wh = sem("weighted_activation_hi")
        s_wl = sem("weighted_activation_lo")
        s_out = sem("y_stored_out")
        s_os = sem("states_stored")


        counted, USED = {}, []
        for kind, _ in STREAM:
            counted[kind] = counted.get(kind, 0) + 1
            if len(USED) in SPLIT:
                USED.append((s_lo, SPLIT.index(len(USED)) + 1))
            else:
                USED.append(({"ada": s_mod, "glu": s_glu}[kind], counted[kind]))

        def in_bank(w):
            return 2 * ((w + 2) % 3)

        H_AT = {3: (4, 5), 4: (6, 7), 5: (8, 9), 6: (10, 11)}
        W_AT = {3: (0, 1), 4: (2, 3), 5: (4, 5), 6: (6, 7)}

        block = base.enter_context(nc.Block())

        def natural(rows):
            return rows.rearrange("p (c i) -> p i c", i=L)

        SQ_BEFORE = {"rms1": 0, "conv": KD, "rms2": KD + CT, "final": 2 * KD + CT}
        SQU_BEFORE = {"rms1": 0, "conv": KD - 1, "rms2": KD + CT - 2, "final": 2 * KD + CT - 3}
        STAT = {"rms1": 1, "mean": 2, "conv": 3, "rms2": 4, "final": 5}
        RSTD = {"rms1": 1, "conv": 2, "rms2": 3, "final": 4}
        APPLY = {"rms1": 0, "rms2": 1, "final": 2}

        @block.sync
        def _(sp):
            def load(n):
                kind, f = STREAM[n]
                if n >= NRAW:
                    sp.wait_ge(*USED[n - NRAW])
                w = 512 if kind == "glu" else RAW
                sp.dma_start(raw[:, n % NRAW, 0:w], dr["w_" + kind][f]).then_inc(s_raw[n % NRAW], 16)

            sp.dma_start(cT[:], dr["cT"]).then_inc(s_c, 16)
            load(0)
            for name, t in (("par", par[:]), ("bm", bm[:]), ("cm", cm[:]), ("h0", h0[:]),
                            ("cw", cw[:]), ("cvec", cvec[:]), ("bada", bada[:]), ("ngain", ngain[:])):
                sp.dma_start(t, dr[name]).then_inc(s_small, 16)
            for c in range(CT):
                sp.dma_start(stc[:, c, :, 0:CW - 1], dr["stc"][:, c]).then_inc(s_small, 16)

            load(1)
            for k in range(KD):
                sp.dma_start(x[:, k, :], dr["x"][:, k]).then_inc(s_xl, 16)
            for n in range(2, NPRE):
                load(n)
            sp.wait_ge(s_kz, 1)
            for half in range(2):
                rows = slice(DK * half, DK * half + DK)
                sp.dma_start(keys[rows, :, half, :], dr["keys"][rows]).then_inc(s_keys, 16)
            for m in range(NRAW):
                sp.wait_ge(*USED[NPRE - NRAW + m])
                sp.dma_start(raw[:, m, :], dr["u"][m]).then_inc(s_raw[m], 16)

            def first_product(it, first, nxt, gates):
                for s in range(4):
                    m = it * 4 + (first + s)
                    sp.wait_ge(s_lo, m + (NSP + 1))
                    if nxt == "u":
                        src = dr["u"][bass.ds(m + NRAW, 1)].rearrange("o p n -> p (o n)")
                    else:
                        src = dr["v"][s]
                    sp.dma_start(raw[:, s, :], src).then_inc(s_raw[s], 16)
                    sp.wait_ge(s_act, m + (NTT + 1))
                    sp.dma_start(hd[bass.ds(m, 1)].rearrange("o p n -> p (o n)"), actr[:, s % HR, :])\
                        .then_inc(s_hst[s % HR], 16)
                    if gates and s % 2:
                        sp.wait_ge(s_gadd, it * 4 + (s + 1))
                        sp.dma_start(gpd[:, :, bass.ds(it * 2 + s // 2, 1), :].rearrange("b p k n -> p b (k n)"),
                                     stage[:, s // 2, 0, :, :].rearrange("p (b j) t -> p b (j t)", b=NB))\
                            .then_inc(s_gst[s // 2], 16)

            with sp.Fori(0, A1 // 4) as it:
                first_product(it, 0, "u", False)
            with sp.Fori(0, TP // TOK // 4) as it:
                first_product(it, A1, "u", True)

            def load_gates(b, slot):
                sp.dma_start(gbp[:, slot].rearrange("p k j t -> p (k j t)"),
                             gpd[bass.ds(b, 1)].rearrange("o p k n -> p (o k n)")).then_inc(s_gl[slot], 16)

            def load_act(j, slot):
                sp.dma_start(hring[:, slot, :], hd[bass.ds(j, 1)].rearrange("o p n -> p (o n)")).then_inc(s_hl[slot], 16)

            for k in range(A3):
                m, s = NK - A3 + k, k % 4
                sp.wait_ge(s_lo, m + (NSP + 1))
                src = dr["u"][m + NRAW] if m + NRAW < NK else dr["v"][m + NRAW - NK]
                sp.dma_start(raw[:, s, :], src).then_inc(s_raw[s], 16)
                sp.wait_ge(s_act, m + (NTT + 1))
                sp.dma_start(hd[m], actr[:, s % HR, :]).then_inc(s_hst[s % HR], 16)
                if k == 0:
                    for i in range(HR):
                        sp.wait_ge(s_hst[i], 16 * (NK - A3) // HR)
                    for j in range(4):
                        load_act(j, j)
                elif k == 1:
                    for i in range(2):
                        sp.wait_ge(s_gst[i], 16 * (TP // GBLK) // 2)
                    load_gates(0, 0)
                elif k == 2:
                    sp.wait_ge(s_gadd, TP // TOK + 1)
                    load_gates(1, 1)
                else:
                    for j in H_AT.get(k, ()):
                        sp.wait_ge(s_w, j - 3)
                        load_act(j, j % 4)
            for s in range(HR):
                sp.wait_ge(s_hst[s], 16 * NK // HR)

            def second_product(b2, odd, i2, s, more_v=True, more_h=True):
                mm = b2 * 16 + (i2 * 4 + (odd * 8 + s))
                if more_v:
                    sp.wait_ge(s_lo, mm + (NSP + NK + 1))
                    sp.dma_start(raw[:, s, :], dr["v"][bass.ds(mm + NRAW, 1)].rearrange("o p n -> p (o n)"))\
                        .then_inc(s_raw[s], 16)
                if more_h:
                    sp.wait_ge(s_w, mm + (JB + 1))
                    load_act(mm + 12, s)

            with sp.Fori(0, NB // 2 - 1) as b2:
                for odd in range(2):
                    sp.wait_ge(s_w, b2 * 16 + JB * (odd + 1))
                    load_gates(b2 * 2 + (odd + 2), odd)
                    with sp.Fori(0, 2) as i2:
                        for s in range(4):
                            second_product(b2, odd, i2, s)
            for mm in range(NK - 16, NK - 4):
                second_product(NB // 2 - 1, mm % 16 // 8, mm % 8 // 4, mm % 4, True, mm + 12 < NK)
            sp.wait_ge(s_hs, 3 * (KD + 1))
            for k in range(KD):
                sp.wait_ge(s_h, 2 * KD + k + 1)
                sp.dma_start(out["y"][:, k], yo[:, k, :]).then_inc(s_out, 16)
            sp.wait_ge(s_out, 16 * KD)

        @block.gpsimd
        def _(pool):
            n = [0]

            def link(ins):
                n[0] += 1
                ins.then_inc(s_p, 1)
                pool.wait_ge(s_p, n[0])

            pool.memset(ones[:], 1.0)
            pool.memset(adaR[0:32 + 1 + TS, :], 0.0)
            pool.memset(ident[:], 0.0)
            pool.memset(XR[:, :, L:2 * L - 1, :], 0.0)
            pool.memset(XI[:, :, L:2 * L - 1, :], 0.0)
            pool.memset(Cbd[:], 0.0)
            pool.memset(U[:, :, NC:NC + 2 * TS], 0.0)
            pool.memset(S[:, :, :, 0:1], 0.0)
            link(pool.iota(iota[:], pattern=[[1, P]], base=0, channel_multiplier=0,
                           allow_small_or_imprecise_dtypes=True))
            pool.affine_select(out=ident[:], in_=ident[:], compare_op=ALU.not_equal, fill=1.0,
                               base=0, pattern=[[-1, P]], channel_multiplier=1).then_inc(s_const, 1)
            def split_lo(k, ring):
                n_ = SPLIT[k] if k < NSP else NPRE + k - NSP
                pool.wait_ge(s_hi, k + 1)
                pool.tensor_tensor(ring[:, k % 2, 1, :], raw[:, n_ % NRAW, :], ring[:, k % 2, 0, :].bitcast(F32),
                                   ALU.subtract).then_inc(s_lo, 1)

            def load_chunk_rows(i):
                if i < L:
                    dst, src = U[i * SQ:(i + 1) * SQ, :, 0:NC], ud[:, :, i, :]
                elif i == L:
                    dst, src = U[0:SQ, :, NC:NC + TS], usd
                else:
                    dst, src = U[P - SQ:P, :, NC + TS:NC + 2 * TS], usd
                pool.dma_start(dst, src.rearrange("g q c -> q g c")).then_inc(s_ul, 16)

            for w in range(3 * CT):
                split_lo(FSP["in"] + w, hlm)
                if 2 <= w < CT + 2:
                    t = w - 2
                    pool.wait_ge(s_uev, t + 1)
                    pool.dma_start(ud.rearrange("(t g) q i c -> t (g q) (i c)", t=CT)[t], uT[:, t, 0:TP]).then_inc(s_ush, 16)
                    pool.dma_start(usd.rearrange("(t g) q s -> t (g q) s", t=CT)[t], uT[:, t, TP:T]).then_inc(s_ush, 16)
                if w == CT + 3:
                    pool.wait_ge(s_ush, 16 * 2 * CT)
                    pool.wait_ge(s_const, 1)
                if w >= CT + 3:
                    for i in range(2 * (w - CT - 3), 2 * (w - CT - 3) + 2):
                        load_chunk_rows(i)
            pool.wait_ge(s_small, 16 * NSMALL)
            pool.wait_ge(s_win, 3 * CT)
            for t in range(CT):
                pool.tensor_scalar(dskip[:, t, :], ident[:], cvec[:, 3, t:t + 1], 1.0, ALU.mult, ALU.mult).then_inc(s_dg, 1)
            pool.wait_ge(s_hc, CT)
            pool.dma_start(out["conv_p"], hc[:, :, TP:TP + CW - 1]).then_inc(s_os, 16)
            for c in range(CT):
                pool.dma_start(out["conv_s"][:, c], stc[:, c, :, 1:CW]).then_inc(s_os, 16)
            pool.wait_ge(s_S, 2)
            pool.dma_start(out["ssm_p"], ssp[:]).then_inc(s_os, 16)
            pool.dma_start(out["ssm_s"], ssn[:]).then_inc(s_os, 16)
            for t in range(CT):
                pool.wait_ge(s_gsig, t + 1)
                pool.tensor_tensor(mixin[:, CT + t, :], yT[:, t, :], uT[:, t, :], ALU.mult).then_inc(s_hsm, 1)

            for k in range(8):
                split_lo(FSP["out"] + k, hlm)

            pool.wait_ge(s_os, 16 * (CT + 3))
            pool.wait_ge(s_x1, KD)
            pool.memset(keys[:], 0.0).then_inc(s_kz, 1)

            def low_part(s, m):
                pool.wait_ge(s_hi, m + (NSP + 1))
                pool.tensor_tensor(hl[:, s % 2, 1, :], raw[:, s, :], hl[:, s % 2, 0, :].bitcast(F32),
                                   ALU.subtract).then_inc(s_lo, 1)

            def add_gates(s, step, dst=None):
                t = slice(8 * (s % 2), 8 * (s % 2) + TOK)
                hi, lo = stage[:, s // 2, 0, :, t], stage[:, s // 2, 1, :, t]
                pool.wait_ge(s_gev, step * 4 + 10)
                pool.tensor_tensor(hi if dst is None else dst, hi, lo, ALU.add).then_inc(s_gadd, 1)

            for k in range(FSP["q"], NSP + 2):
                split_lo(k, hl)
            with pool.Fori(0, A1 // 4) as it:
                for s in range(4):
                    low_part((s + 2) % 4, it * 4 + (s + 2))
            with pool.Fori(0, TP // TOK // 4) as it:
                for s in range(4):
                    low_part((s + 2) % 4, it * 4 + (A1 + s + 2))
                    add_gates(s, it * 4 + s)
            low_part(2, NK - A3 + 2)
            add_gates(0, TP // TOK, stages)
            low_part(3, NK - A3 + 3)
            with pool.Fori((NK - A3 + 4) // 4, 2 * NK // 4) as it:
                for s in range(4):
                    low_part(s, it * 4 + s)

        @block.scalar
        def _(act):
            act.wait_ge(s_c, 16)
            act.activation(sil[:], cT[:], ACT.Silu).then_inc(s_sil, 1)
            act.wait_ge(s_trig_in, 1)
            act.activation(K[:, 12:14, :], K[:, 10:12, :], ACT.Sin).then_inc(s_trig, 1)

            def modulation_rows(pair):
                act.wait_ge(s_mod, PAIR * (pair + 1))
                after(act, s_adt, pair)
                if pair == 0:
                    act.wait_ge(s_const, 1)
                for c in range(2):
                    last = act.activation(adaR[32 * c:32 * c + 1 + TS, :], ps[32 * c:32 * c + 1 + TS, 6:8, :].rearrange(
                        "p a n -> p (a n)"), ACT.Copy)
                last.then_inc(s_ade, 1)

            def split_hi(k, ring):
                n_ = SPLIT[k] if k < NSP else NPRE + k - NSP
                act.wait_ge(s_raw[n_ % NRAW], 16 * (n_ // NRAW + 1))
                act.activation(ring[:, k % 2, 0, :], raw[:, n_ % NRAW, :], ACT.Copy).then_inc(s_hi, 1)

            def squares(norm, rows, count):
                for k in range(count):
                    if k >= 2:
                        act.wait_ge(s_squ, SQU_BEFORE[norm] + k - 1)
                    act.activation(sq[:, k % 2, :], rows[:, k, :], ACT.Square).then_inc(s_sq, 1)

            def root(norm):
                act.wait_ge(s_rec, RSTD[norm])
                act.activation(rstd[:], rstd[:], ACT.Sqrt).then_inc(s_rstd, 1)

            def shifts(norm, dst, first):
                for k in range(KD):
                    act.wait_ge(s_hs, APPLY[norm] * (KD + 1) + k + 2)
                    act.activation(dst[:, k, 0:TP], dst[:, k, 0:TP], ACT.Identity,
                                   bias=mods[:, first + k, 0:1]).then_inc(s_h, 1)

            act.wait_ge(s_xl, 16 * KD)
            squares("rms1", x, KD)
            root("rms1")
            modulation_rows(0)
            act.wait_ge(s_hs, 1)
            act.activation(rhi[:, :, TP:T], h1[:, :, TP:T], ACT.Copy).then_inc(s_h1s, 1)
            for k in range(KD):
                act.wait_ge(s_hs, k + 2)
                act.activation(rhi[:, k, 0:TP], h1[:, k, 0:TP], ACT.Identity,
                               bias=mods[:, SH1 + k, 0:1]).then_inc(s_h, 1)
                if k in (2, 5):
                    split_hi(FSP["in"] + k // 3, hlm)
            for t in range(CT):
                act.wait_ge(s_win, t + 1)
                split_hi(FSP["in"] + t + 2, hlm)
                for h, (a, b) in enumerate(HALVES):
                    last = act.activation(uT[:, t, a:b], ps[:, in_bank(t) + h, 0:b - a], ACT.Copy)
                last.then_inc(s_uev, 1)
            for t in range(CT):
                for w in (CT + 2 * t, CT + 2 * t + 1):
                    act.wait_ge(s_win, w + 1)
                    if w + 2 < 3 * CT:
                        split_hi(FSP["in"] + w + 2, hlm)
                after(act, s_hc, t)
                for h, (a, b) in enumerate(HALVES):
                    last = act.activation(sq[:, 0, a:b], ps[:, in_bank(CT + 2 * t + 1) + h, 0:b - a], ACT.Sigmoid)
                last.then_inc(s_sig, 1)
            for e in range(20):
                act.wait_ge(s_prep, e + 1)
                src = ps[:, 4 + e % 2, :]
                if e < 4:
                    dst, src = Kt[:, e, :], src[:, 0:MQ]
                elif e < 12:
                    dst = ET[:, (e - 4) // 4, 4 * (e % 4):4 * (e % 4) + 4, :].rearrange("p t n -> p (t n)")
                else:
                    n4, ih = divmod(e - 12, 2)
                    dst = Tm[:, 8 * n4:8 * n4 + 8, 64 * ih:64 * ih + 64].rearrange("p g (i q) -> p i g q", q=SQ)
                    src = src.rearrange("p (i g q) -> p i g q", i=4, g=8)
                act.activation(dst, src, ACT.Copy).then_inc(s_prepe, 1)
            act.wait_ge(s_V, 1)
            for a in range(2):
                for b in range(3):
                    t0, t1 = 6 * b, min(6 * b + 6, ST)
                    act.activation(V[:, a, t0:t1, :].rearrange("p t c -> p (t c)"),
                                   ps[:, 3 * a + b, 0:(t1 - t0) * (NC + 2 * TS)], ACT.Copy).then_inc(s_Ve, 1)
            modulation_rows(1)
            for e in range(2 * CT):
                b, g2 = divmod(e, 2)
                if g2 == 0 or b == 0:
                    act.wait_ge(s_Y, 1 + g2)
                act.activation(Ysb[:, b].rearrange("p i (g h q) -> p g h i q", h=2, q=SQ)[:, :, g2],
                               ps[0:NC + TS, 4 * g2 + b, :].rearrange("p (g i q) -> p g i q", g=4, i=L),
                               ACT.Copy).then_inc(s_Ye, 1)
            for t in range(CT):
                act.wait_ge(s_yt, t + 1)
                for h in range(2):
                    act.activation(yT[:, t, h * 256:(h + 1) * 256].rearrange("p (i c) -> p i c", i=4),
                                   ps[:, 4 * h + t, 0:4 * (NC + TS)].rearrange("p (i c) -> p i c", i=4)[:, :, 0:NC],
                                   ACT.Gelu_apprx_tanh)
                act.activation(yT[:, t, TP:T], ps[:, t, NC:NC + TS], ACT.Gelu_apprx_tanh).then_inc(s_z, 1)
            for t in range(CT):
                act.wait_ge(s_glu, t + 1)
                for h, (a, b) in enumerate(HALVES):
                    last = act.activation(uT[:, t, a:b], ps[:, 2 * (t % 2) + h, 0:b - a], ACT.Sigmoid)
                last.then_inc(s_gsig, 1)
            modulation_rows(2)
            act.wait_ge(s_cvd, 1)
            squares("conv", cv, CT)
            root("conv")
            act.wait_ge(s_cn, 1)
            for t in range(CT):
                act.activation(mixin[:, t, 0:TP].rearrange("p (i c) -> p i c", i=L), natural(cv[:, t, 0:TP]), ACT.Silu,
                               scale=cvec[:, 1, t:t + 1], bias=cvec[:, 2, t:t + 1])
                act.activation(mixin[:, t, TP:T], cv[:, t, TP:T], ACT.Silu,
                               scale=cvec[:, 1, t:t + 1], bias=cvec[:, 2, t:t + 1]).then_inc(s_hcm, 1)
            split_hi(FSP["out"], hlm)
            split_hi(FSP["out"] + 1, hlm)
            act.wait_ge(s_hsm, CT)
            act.activation(rhi[:, CT:KD, :], mixin[:, CT:KD, :], ACT.Copy).then_inc(s_rh, 1)
            act.wait_ge(s_hcm, CT)
            act.activation(rhi[:, 0:CT, :], mixin[:, 0:CT, :], ACT.Copy).then_inc(s_rh, 1)
            for k in range(KD):
                if k + 2 < KD:
                    act.wait_ge(s_mix, k + 1)
                    split_hi(FSP["out"] + k + 2, hlm)
                act.wait_ge(s_x1, k + 1)
                if k >= 2:
                    act.wait_ge(s_squ, SQU_BEFORE["rms2"] + k - 1)
                act.activation(sq[:, k % 2, :], x[:, k, :], ACT.Square).then_inc(s_sq, 1)
            root("rms2")
            act.wait_ge(s_hs, KD + 1 + 1)
            act.activation(h2[:, 0, :, TP:T], h2f[:, :, TP:T], ACT.Copy).then_inc(s_h2s, 1)
            for k in range(KD):
                act.wait_ge(s_hs, KD + 1 + k + 2)
                act.activation(h2[:, 0, k, 0:TP], h2f[:, k, 0:TP], ACT.Identity,
                               bias=mods[:, SH2 + k, 0:1]).then_inc(s_h, 1)

            split_hi(FSP["q"], hl)
            split_hi(FSP["q"] + 1, hl)
            modulation_rows(3)
            for k in range(KD):
                act.wait_ge(s_q, k + 1)
                split_hi(FSP["q"] + k + 2, hl)
                for h, (a, b) in enumerate(HALVES):
                    last = act.activation(qT[:, k, a:b], ps[:, 2 * (k % 2) + h, 0:b - a], ACT.Copy)
                last.then_inc(s_qe, 1)
            for t in range(NTT):
                act.wait_ge(s_sc, t + 1)
                for q in range(4):
                    last = act.activation(sc[0:TT, t, 4 * q:4 * q + 4, :].rearrange("p a n -> p (a n)"),
                                          ps[0:TT, 4 * (1 - t % 2) + q, :], ACT.Copy)
                last.then_inc(s_act, 1)

            NP4 = NPRE // 4

            def activations(s, it, first):
                m = it * 4 + (first + s)
                act.wait_ge(s_raw[(s + 2) % 4], (it + (NP4 + first // 4 + 1 + (s + 2) // 4)) * 16)
                act.wait_ge(s_pe, m + 1)
                act.activation(hl[:, s % 2, 0, :], raw[:, (s + 2) % 4, :], ACT.Copy).then_inc(s_hi, 1)
                after(act, s_hst[s % HR], it * 32 + (first // 2 + s // 2) * 16)
                for h, (a, b) in enumerate(HALVES):
                    last = act.activation(actr[:, s % HR, a:b], ps[:, 2 * (s % 2) + h, 0:b - a], ACT.Gelu_apprx_tanh)
                last.then_inc(s_act, 1)

            def copy_gates(s, it, banks):
                if s % 2 == 0 and 0 in banks:
                    after(act, s_gst[s // 2], it * 16)
                for q in banks:
                    act.wait_ge(s_tok, it * 32 + (8 * s + 2 * q + 2))
                    t0 = 8 * (s % 2) + 2 * q
                    act.activation(stage[:, s // 2, :, :, t0:t0 + 2].rearrange("p a j t -> p t a j"),
                                   ps[:, 4 + q, :].rearrange("p (t a j) -> p t a j", t=2, a=2),
                                   ACT.Copy).then_inc(s_gev, 1)

            for s in range(4):
                activations(s, 0, 0)
            with act.Fori(1, A1 // 4 - 1) as it:
                for s in range(4):
                    activations(s, it, 0)
            act.wait_ge(s_exi, 1)
            act.activation(selv[0:TT, :, 2, :], eq[0:TT].rearrange("p a b -> p (a b)")[:, 0:NTT * NSEL].rearrange(
                "p (t n) -> p t n", t=NTT), ACT.Exp).then_inc(s_exo, 1)
            for s in range(2):
                activations(s, A1 // 4 - 1, 0)
            act.wait_ge(s_selp, 1)
            for kind in range(3):
                act.activation(selT[:, kind, 0:4 * TT], ps[:, 4 + kind, 0:4 * TT], ACT.Copy).then_inc(s_gev, 1)
                act.activation(selT[:, kind, 4 * TT:T], ps[:, 7, kind * TT:(kind + 1) * TT], ACT.Copy).then_inc(s_gev, 1)
            act.wait_ge(s_gev, 6)
            act.activation(gp[:, 0, :], selT[:, 2, :], ACT.Copy).then_inc(s_gh, 1)
            for s in range(2, 4):
                activations(s, A1 // 4 - 1, 0)
            for s in range(4):
                copy_gates(s, 0, (0, 1, 2))
                activations(s, 0, A1)
                copy_gates(s, 0, (3,))
            with act.Fori(1, TP // TOK // 4) as it:
                for s in range(4):
                    copy_gates(s, it, (0, 1, 2))
                    activations(s, it, A1)
                    copy_gates(s, it, (3,))

            def weighted_hi(j):
                act.wait_ge(s_w, j + 1)
                act.activation(WH0[:, 0, j, :], wf[:, j % 2, :], ACT.Copy).then_inc(s_wh, 1)

            for k in range(A3):
                activations(k % 4, TP // TOK // 4 + k // 4, A1)
                if k == 0:
                    copy_gates(0, TP // TOK // 4, range(4))
                for j in W_AT.get(k, ()):
                    weighted_hi(j)

            def second(b2, odd, i2, s, more_v=True, more_w=True):
                mm = b2 * 16 + (i2 * 4 + (odd * 8 + s))
                if more_w:
                    act.wait_ge(s_w, mm + 9)
                    if s == 0:
                        act.wait_ge(s_pe, b2 * 16 + (NK + 8 * odd))
                    act.activation(WHL[1 - odd][:, 0, i2 * 4 + s, :], wf[:, s % 2, :], ACT.Copy).then_inc(s_wh, 1)
                if more_v:
                    act.wait_ge(s_raw[(s + 2) % 4], b2 * 64 + (i2 + (NP4 + NK // 4 + 2 * odd + 1 + (s + 2) // 4)) * 16)
                    act.wait_ge(s_pe, mm + (NK + 1))
                    act.activation(hl[:, s % 2, 0, :], raw[:, (s + 2) % 4, :], ACT.Copy).then_inc(s_hi, 1)

            with act.Fori(0, NB // 2 - 1) as b2:
                for odd in range(2):
                    for i2 in range(2):
                        for s in range(4):
                            second(b2, odd, i2, s)
            def final_squares(q):
                act.wait_ge(s_x1, NK + q + 1)
                if q >= 2:
                    act.wait_ge(s_squ, SQU_BEFORE["final"] + q - 1)
                act.activation(sq[:, q % 2, :], x[:, q, :], ACT.Square).then_inc(s_sq, 1)

            for mm in range(NK - 16, NK - 2):
                second(NB // 2 - 1, mm % 16 // 8, mm % 8 // 4, mm % 4, True, mm + 8 < NK)
                if mm > NK - 8:
                    final_squares(mm - (NK - 8) - 1)
            for q in range(KD - 3, KD):
                final_squares(q)
            root("final")
            shifts("final", yo, SHF)

        @block.vector
        def _(dve):
            n = [0]

            def link(ins):
                n[0] += 1
                ins.then_inc(s_v, 1)
                dve.wait_ge(s_v, n[0])

            def tt(o, a, b, op):
                link(dve.tensor_tensor(o, a, b, op))

            def cmul(o, a, b, t):
                dve.tensor_tensor(o[0], a[0], b[0], ALU.mult)
                tt(t, a[1], b[1], ALU.mult)
                tt(o[0], o[0], t, ALU.subtract)
                dve.tensor_tensor(o[1], a[0], b[1], ALU.mult)
                tt(t, a[1], b[0], ALU.mult)
                tt(o[1], o[1], t, ALU.add)

            def k(i):
                return K[:, i, :]

            def exp_exact(dst, src, t, r, p):
                link(dve.tensor_scalar(t, src, LOG2E, MAGIC, ALU.mult, ALU.add))
                link(dve.tensor_scalar(t, t, MAGIC, None, ALU.subtract))
                link(dve.tensor_scalar(t, t, 127.0, -126.0, ALU.min, ALU.max))
                link(dve.scalar_tensor_tensor(r, t, -LN2_HI, src, ALU.mult, ALU.add))
                link(dve.scalar_tensor_tensor(r, t, -LN2_LO, r, ALU.mult, ALU.add))
                link(dve.tensor_scalar(p, r, 1.0 / 5040, None, ALU.mult))
                for c in (1 / 720, 1 / 120, 1 / 24, 1 / 6, 0.5, 1.0):
                    link(dve.scalar_tensor_tensor(p, p, c, r, ALU.add, ALU.mult))
                link(dve.tensor_scalar(t, t, 127.0, None, ALU.add))
                link(dve.tensor_copy(ki[:], t))
                link(dve.tensor_scalar(ki[:], ki[:], 23, None, ALU.logical_shift_left))
                link(dve.scalar_tensor_tensor(dst, p, 1.0, ki[:].bitcast(F32), ALU.add, ALU.mult))

            dve.wait_ge(s_small, 16 * NSMALL)
            lr, li, ldt = par[:, 0, :], par[:, 1, :], par[:, 2, :]
            DT, X1, X8, MAG, MAG8, ANG = k(0), k(1), k(2), k(3), k(4), k(5)
            exp_exact(DT, ldt, k(6), k(7), k(8))
            tt(X1, lr, DT, ALU.mult)
            tt(ANG, li, DT, ALU.mult)
            link(dve.tensor_scalar(X8, X1, float(L), None, ALU.mult))
            exp_exact(MAG, X1, k(6), k(7), k(8))
            exp_exact(MAG8, X8, k(6), k(7), k(8))
            link(dve.tensor_scalar(k(6), ANG, INV2PI, MAGIC, ALU.mult, ALU.add))
            link(dve.tensor_scalar(k(6), k(6), MAGIC, None, ALU.subtract))
            link(dve.scalar_tensor_tensor(k(7), k(6), -TWO_PI_HI, ANG, ALU.mult, ALU.add))
            link(dve.scalar_tensor_tensor(k(10), k(6), -TWO_PI_LO, k(7), ALU.mult, ALU.add))
            link(dve.tensor_scalar(k(11), k(10), 0.5 * 3.141592653589793, None, ALU.add))
            link(dve.tensor_scalar(k(6), k(11), PI_IN, -2 * 3.141592653589793, ALU.is_gt, ALU.mult))
            tt(k(11), k(11), k(6), ALU.add)
            dve.tensor_scalar(K[:, 10:12, :], K[:, 10:12, :], PI_IN, -PI_IN, ALU.min, ALU.max).then_inc(s_trig_in, 1)
            dve.wait_ge(s_trig, 1)
            SIN, COS = k(12), k(13)
            dve.memset(PW[:, 0, :, 0:1], 1.0)
            dve.memset(PW[:, 1, :, 0:1], 0.0)
            tt(PW[:, 0, :, 1], MAG, COS, ALU.mult)
            tt(PW[:, 1, :, 1], MAG, SIN, ALU.mult)
            for m in (1, 2, 4):
                def wide(a):
                    return PW[:, a, :, m:m + 1].broadcast_to([P, ST, m])
                tmp = K[:, 14:14 + m, :].rearrange("p m t -> p t m")
                cmul([PW[:, a, :, m + 1:2 * m + 1] for a in (0, 1)], [wide(0), wide(1)],
                     [PW[:, a, :, 1:m + 1] for a in (0, 1)], tmp)
            for r in range(L + 1):
                last = dve.tensor_copy(PR[:, :, :, r], PW[:, :, :, L - r])
            link(last)
            AM, DEN, CR, CI = k(14), k(15), k(16), k(17)
            dve.tensor_scalar(AM, PW[:, 0, :, 1], -1.0, None, ALU.add)
            tt(DEN, lr, lr, ALU.mult)
            tt(k(18), li, li, ALU.mult)
            tt(DEN, DEN, k(18), ALU.add)
            link(dve.reciprocal(DEN, DEN))
            dve.tensor_tensor(CR, AM, lr, ALU.mult)
            tt(k(18), PW[:, 1, :, 1], li, ALU.mult)
            tt(CR, CR, k(18), ALU.add)
            dve.tensor_tensor(CI, PW[:, 1, :, 1], lr, ALU.mult)
            tt(k(18), AM, li, ALU.mult)
            tt(CI, CI, k(18), ALU.subtract)
            tt(CR, CR, DEN, ALU.mult)
            tt(CI, CI, DEN, ALU.mult)

            def per_state(a, n):
                return a.rearrange("p (t o) -> p t o", o=1).broadcast_to([P, ST, n])

            cmul([Bb[:, 0], Bb[:, 1]], [per_state(CR, SQ), per_state(CI, SQ)], [bm[:, 0], bm[:, 1]], xt[:, :, 0, :])
            def modulations(pair):
                dve.wait_ge(s_adt, pair + 1)
                cols = ps[:, 6, 0:KD * (32 + 1 + TS)].rearrange("p (q s) -> p q s", q=KD)
                for c in range(2):
                    f0 = (2 * pair + c) * KD
                    last = dve.tensor_tensor(mods[:, f0:f0 + KD, :], cols[:, :, 32 * c:32 * c + 1 + TS],
                                             bada[:, f0:f0 + KD].rearrange("p (f o) -> p f o", o=1).broadcast_to(
                                                 [P, KD, 1 + TS]), ALU.add)
                last.then_inc(s_mods, 1)
                dve.wait_ge(s_mods, pair + 1)

            def gain(i, first):
                g = ngain[:, i].rearrange("p (f o) -> p f o", o=1).broadcast_to([P, KD, 1 + TS])
                link(dve.scalar_tensor_tensor(gsc[:, i], mods[:, first:first + KD, :], 1.0, g, ALU.add, ALU.mult))

            def variance(norm, width):
                dve.wait_ge(s_stat, STAT[norm])
                for h, (a, b) in enumerate(HALVES):
                    last = dve.tensor_scalar(rstd[:, a:b], ps[:, 4 + h, 0:b - a], 1.0 / width, EPS, ALU.mult, ALU.add)
                link(last)
                dve.reciprocal(rstd[:], rstd[:]).then_inc(s_rec, 1)
                dve.wait_ge(s_rstd, RSTD[norm])

            def apply_norm(norm, dst, first):
                i = APPLY[norm]
                r = rstd[:, TP:T].rearrange("p (o s) -> p o s", o=1).broadcast_to([P, KD, TS])
                tt(smalls[:], x[:, :, TP:T], r, ALU.mult)
                tt(smalls[:], smalls[:], gsc[:, i, :, 1:1 + TS], ALU.mult)
                dve.tensor_tensor(dst[:, :, TP:T], smalls[:], mods[:, first:first + KD, 1:1 + TS], ALU.add)\
                    .then_inc(s_hs, 1)
                for q in range(KD):
                    dve.scalar_tensor_tensor(dst[:, q, 0:TP], x[:, q, 0:TP], gsc[:, i, q, 0:1], rstd[:, 0:TP],
                                             ALU.mult, ALU.mult).then_inc(s_hs, 1)

            variance("rms1", D)
            modulations(0)
            gain(0, SC1)
            apply_norm("rms1", h1, SH1)
            dve.wait_ge(s_h1s, 1)
            dve.tensor_tensor(h1lo[:, :, TP:T], h1[:, :, TP:T], rhi[:, :, TP:T].bitcast(F32), ALU.subtract)\
                .then_inc(s_h1l, 1)
            for q in range(KD):
                dve.wait_ge(s_h, q + 1)
                dve.scalar_tensor_tensor(h1lo[:, q, 0:TP], h1[:, q, 0:TP], mods[:, SH1 + q, 0:1],
                                         rhi[:, q, 0:TP].bitcast(F32), ALU.add, ALU.subtract).then_inc(s_h1l, 1)

            dve.wait_ge(s_const, 1)

            def powers(src, first):
                return [src[:, a, :, first:first + L].rearrange("p t (m o) -> p t m o", o=1).broadcast_to([P, ST, L, SQ])
                        for a in (0, 1)]

            def over(m4):
                return [m4[:, a].rearrange("p t (o q) -> p t o q", o=1).broadcast_to([P, ST, L, SQ]) for a in (0, 1)]

            cmul([XR[:, :, 0:L, :], XI[:, :, 0:L, :]], powers(PR, 1), over(Bb), xt)
            for g2 in range(2):
                rows = slice(64 * g2, 64 * g2 + 64)
                dve.tensor_copy(Cbd[rows, 0, :, g2, :], cm[rows, 0])
                dve.tensor_scalar(Cbd[rows, 1, :, g2, :], cm[rows, 1], -1.0, None, ALU.mult).then_inc(s_Xr, 1)
            cmul([FO[:, 0], FO[:, 1]], powers(PW, 1), over(cm), xt)
            dve.tensor_scalar(FO[:, 1], FO[:, 1], -1.0, None, ALU.mult).then_inc(s_Fr, 1)
            dve.memset(hc[:, :, 0:CW - 1], 0.0)

            def conv_rows(t):
                dve.wait_ge(s_win, CT + 2 * t + 2)
                dve.wait_ge(s_sig, t + 1)
                rows = natural(hc[:, t, CW - 1:CW - 1 + TP])
                for h in range(2):
                    dve.tensor_tensor(rows[:, 4 * h:4 * h + 4, :],
                                      ps[:, in_bank(CT + 2 * t) + h, 0:TP // 2].rearrange("p (i c) -> p i c", i=4),
                                      sq[:, 0, h * 256:h * 256 + 256].rearrange("p (i c) -> p i c", i=4), ALU.mult)
                dve.tensor_tensor(stc[:, t, :, CW - 1], ps[:, in_bank(CT + 2 * t) + 1, TP // 2:TP // 2 + TS], sq[:, 0, TP:T],
                                  ALU.mult).then_inc(s_hc, 1)

            conv_rows(0)
            cmul([k(20), k(21)], [COS, SIN], [COS, SIN], k(18))
            cmul([k(22), k(23)], [k(20), k(21)], [k(20), k(21)], k(18))
            cmul([k(20), k(21)], [k(22), k(23)], [k(22), k(23)], k(18))
            for i in range(5):
                q = (k(20 + 2 * i), k(21 + 2 * i))
                cmul([k(22 + 2 * i), k(23 + 2 * i)], q, q, k(18))
            for t in range(1, CT):
                conv_rows(t)
            dve.wait_ge(s_hc, CT)

            dve.wait_ge(s_prep, 12)
            dve.memset(R[:, 0, :, 0:1], 1.0)
            link(dve.memset(R[:, 1, :, 0:1], 0.0))
            for i in range(6):
                m = 1 << i
                q = [per_state(k(20 + 2 * i + a), m) for a in (0, 1)]
                cmul([R[:, a, :, m:2 * m] for a in (0, 1)], q, [R[:, a, :, 0:m] for a in (0, 1)], wt[:, :, 0:m])
            dve.wait_ge(s_Ve, 6)
            vr, vi = V[:, 0, :, 0:NC], V[:, 1, :, 0:NC]
            dve.tensor_tensor(W2[:, 0], vr, R[:, 0], ALU.mult)
            tt(wt[:], vi, R[:, 1], ALU.mult)
            tt(W2[:, 0], W2[:, 0], wt[:], ALU.add)
            dve.tensor_tensor(W2[:, 1], vi, R[:, 0], ALU.mult)
            tt(wt[:], vr, R[:, 1], ALU.mult)
            tt(W2[:, 1], W2[:, 1], wt[:], ALU.subtract)
            link(dve.tensor_copy(wt[:], per_state(MAG8, NC)))
            link(dve.memset(wt[:, :, 0:1], 0.0))
            wtf = wt[:, :, :].rearrange("p t c -> p (t c)")
            for a in range(2):
                link(dve.tensor_tensor_scan(W2f[:, a, :], wtf, W2f[:, a, :], 0.0, ALU.mult, ALU.add))
            dve.tensor_tensor(V[:, 0, :, 0:NC], W2[:, 0], R[:, 0], ALU.mult)
            tt(wt[:], W2[:, 1], R[:, 1], ALU.mult)
            dve.tensor_tensor(S[:, 0, :, 1:NC], V[:, 0, :, 0:NC - 1], wt[:, :, 0:NC - 1], ALU.subtract)
            tt(ssp[:, 0, :], V[:, 0, :, NC - 1], wt[:, :, NC - 1], ALU.subtract)
            dve.tensor_tensor(V[:, 1, :, 0:NC], W2[:, 0], R[:, 1], ALU.mult)
            tt(wt[:], W2[:, 1], R[:, 0], ALU.mult)
            tt(S[:, 1, :, 1:NC], V[:, 1, :, 0:NC - 1], wt[:, :, 0:NC - 1], ALU.add)
            dve.tensor_tensor(ssp[:, 1, :], V[:, 1, :, NC - 1], wt[:, :, NC - 1], ALU.add)
            dve.tensor_copy(S[:, :, :, NC:NC + TS], h0[:]).then_inc(s_S, 1)
            modulations(1)
            a1 = [PW[:, a, :, 1:2].broadcast_to([P, ST, TS]) for a in (0, 1)]
            cmul([ssn[:, 0], ssn[:, 1]], a1, [h0[:, 0], h0[:, 1]], wt[:, :, 0:TS])
            dve.tensor_tensor(ssn[:], ssn[:], V[:, :, :, NC + TS:NC + 2 * TS], ALU.add).then_inc(s_S, 1)

            for t in range(CT):
                dve.tensor_scalar(cv[:, t, 0:TP], hc[:, t, 0:TP], cw[:, t, 0:1], cvec[:, 0, t:t + 1],
                                  ALU.mult, ALU.add).then_inc(s_cv, 1)
            for w in range(1, CW):
                for t in range(CT):
                    dve.wait_ge(s_cv, CT * (w - 1) + t + 1)
                    dve.scalar_tensor_tensor(cv[:, t, 0:TP], hc[:, t, w:w + TP], cw[:, t, w:w + 1], cv[:, t, 0:TP],
                                             ALU.mult, ALU.add).then_inc(s_cv, 1)
            prod = wt[:, :, :].rearrange("p t c -> p (t c)")[:, 0:CT * TS * CW].rearrange(
                "p (t s w) -> p t s w", t=CT, s=TS)
            dve.wait_ge(s_S, 2)
            for t in range(CT):
                last = dve.tensor_tensor(prod[:, t], stc[:, t],
                                         cw[:, t, :].rearrange("p (o w) -> p o w", o=1).broadcast_to([P, TS, CW]), ALU.mult)
            link(last)
            link(dve.tensor_reduce(cv[:, :, TP:T], prod, AX.X, ALU.add))
            dve.tensor_tensor(cv[:, :, TP:T], cv[:, :, TP:T],
                              cvec[:, 0, :].rearrange("p (t o) -> p t o", o=1).broadcast_to([P, CT, TS]),
                              ALU.add).then_inc(s_cv, 1)

            modulations(2)
            gain(1, SC2)

            dve.wait_ge(s_stat, STAT["mean"])
            for h, (a, b) in enumerate(HALVES):
                mean = ps[:, 4 + h, 0:b - a].rearrange("p (o n) -> p o n", o=1).broadcast_to([P, CT, b - a])
                last = dve.scalar_tensor_tensor(cv[:, :, a:b], mean, -1.0 / CC, cv[:, :, a:b], ALU.mult, ALU.add)
            last.then_inc(s_cvd, 1)
            dve.wait_ge(s_cvd, 1)
            variance("conv", CC)
            dve.tensor_tensor(cv[:], cv[:], rstd[:].rearrange("p (o n) -> p o n", o=1).broadcast_to([P, CT, T]),
                              ALU.mult).then_inc(s_cn, 1)

            for k, c in enumerate((slice(CT, KD), slice(0, CT))):
                dve.wait_ge(s_rh, k + 1)
                dve.tensor_tensor(mixlo[:, c, :], mixin[:, c, :], rhi[:, c, :].bitcast(F32),
                                  ALU.subtract).then_inc(s_rl, 1)

            def residual(f, first_gate, done):
                q, gate, bank = x[:, f, :], mods[:, first_gate + f, :], 2 * (f % 2)
                dve.tensor_tensor(smalls[:, f, :], ps[:, bank + 1, 256:256 + TS], gate[:, 1:1 + TS],
                                  ALU.mult).then_inc(s_xs, 1)
                for h in range(2):
                    dve.scalar_tensor_tensor(q[:, h * 256:h * 256 + 256], ps[:, bank + h, 0:256], gate[:, 0:1],
                                             q[:, h * 256:h * 256 + 256], ALU.mult, ALU.add)
                dve.wait_ge(s_xs, done)
                dve.tensor_tensor(q[:, TP:T], q[:, TP:T], smalls[:, f, :], ALU.add).then_inc(s_x1, 1)

            for q in range(KD):
                dve.wait_ge(s_mix, q + 1)
                residual(q, G1, q + 1)
            variance("rms2", D)
            dve.wait_ge(s_os, 16 * (CT + 3))
            apply_norm("rms2", h2f, SH2)
            dve.wait_ge(s_h2s, 1)
            dve.tensor_tensor(h2[:, 1, :, TP:T], h2f[:, :, TP:T], h2[:, 0, :, TP:T].bitcast(F32), ALU.subtract)\
                .then_inc(s_h2l, 1)
            for q in range(KD):
                dve.wait_ge(s_h, KD + q + 1)
                dve.scalar_tensor_tensor(h2[:, 1, q, 0:TP], h2f[:, q, 0:TP], mods[:, SH2 + q, 0:1],
                                         h2[:, 0, q, 0:TP].bitcast(F32), ALU.add, ALU.subtract).then_inc(s_h2l, 1)
            modulations(3)
            gain(2, SCF)

            A = slice(0, TT)
            dve.wait_ge(s_h2l, KD + 1)
            dve.wait_ge(s_act, NTT)
            for t in range(NTT):
                def top16(vals, idx, src, width):
                    link(dve.max(vals[:, 0:8], src))
                    dve.max_index(idx[:, 0:8], vals[:, 0:8], src)
                    link(dve.match_replace(wk[A, 0:width], vals[:, 0:8], src, NEG))
                    link(dve.max(vals[:, 8:16], wk[A, 0:width]))
                    link(dve.max_index(idx[:, 8:16], vals[:, 8:16], wk[A, 0:width]))

                for h in range(HEADS):
                    for s in range(2):
                        top16(v16[A, h, s, :], i16[A, h, s, :], sc[A, t, 2 * h + s, :], NK)
                dve.tensor_copy(i16f[A], i16[A])
                for c0, a0, na, nb in ((0, 0, RC, TOPK), (RC * TOPK, RC, TOPK - RC, RC)):
                    last = dve.tensor_tensor(
                        cand[A, :, c0:c0 + na * nb].rearrange("p h (a b) -> p h a b", b=nb),
                        v16[A, :, 0, a0:a0 + na].rearrange("p h (a o) -> p h a o", o=1).broadcast_to([TT, HEADS, na, nb]),
                        v16[A, :, 1, 0:nb].rearrange("p h (o b) -> p h o b", o=1).broadcast_to([TT, HEADS, na, nb]), ALU.add)
                link(last)
                for h in range(HEADS):
                    top16(selv[A, t, 2, h * TOPK:(h + 1) * TOPK], pos[A, h * TOPK:(h + 1) * TOPK],
                          cand[A, h], NCAND)
                dve.tensor_scalar(rr[A, 0, :], pos[A, :], 4, None, ALU.logical_shift_right)
                dve.tensor_scalar(rr[A, 1, :], pos[A, :], 15, None, ALU.bitwise_and)
                dve.tensor_scalar(rr[A, 2, :], pos[A, :], 2, None, ALU.logical_shift_right)
                link(dve.tensor_scalar(rr[A, 3, :], pos[A, :], 3, None, ALU.bitwise_and))
                link(dve.tensor_copy(rf[A], rr[A]))
                dve.tensor_scalar(late[A, :], rf[A, 2, :], float(RC * TOPK // 4), None, ALU.is_ge)
                link(dve.tensor_scalar(rf[A, 2, :], rf[A, 2, :], float(RC * TOPK // 4 - RC), None, ALU.subtract))
                tt(rf[A, 2:4, :], rf[A, 2:4, :], rf[A, 0:2, :], ALU.subtract)
                tt(rf[A, 2:4, :], rf[A, 2:4, :], late[A, :].rearrange("p (o n) -> p o n", o=1).broadcast_to(
                    [TT, 2, NSEL]), ALU.mult)
                tt(rf[A, 0:2, :], rf[A, 0:2, :], rf[A, 2:4, :], ALU.add)
                for s in range(2):
                    tt(eq[A], rf[A, s, :].rearrange("p (n o) -> p n o", o=1).broadcast_to([TT, NSEL, TOPK]),
                       iota[A, 0:TOPK].rearrange("p (o r) -> p o r", o=1).broadcast_to([TT, NSEL, TOPK]), ALU.is_equal)
                    eq4 = eq[A].rearrange("p (h n) r -> p h n r", h=HEADS)
                    tt(eq4, eq4, i16f[A, :, s, :].rearrange("p h (o r) -> p h o r", o=1).broadcast_to(
                        [TT, HEADS, TOPK, TOPK]), ALU.mult)
                    link(dve.tensor_reduce(selv[A, t, s, :], eq[A], AX.X, ALU.add))
            sc4 = selv[A, :, 2, :].rearrange("p t (h n) -> p t h n", h=HEADS)
            ex = eq[A].rearrange("p a b -> p (a b)")[:, 0:NTT * NSEL].rearrange("p (t h n) -> p t h n", t=NTT, h=HEADS)
            dve.tensor_tensor(ex, sc4, selv[A, :, 2, :].rearrange("p t (h n) -> p t h n", h=HEADS)[:, :, :, 0:1]
                              .broadcast_to([TT, NTT, HEADS, TOPK]), ALU.subtract).then_inc(s_exi, 1)
            dve.wait_ge(s_exo, 1)
            sums = rs[A, 0, :].rearrange("p (t h) -> p t h", t=NTT)
            link(dve.tensor_reduce(sums, sc4, AX.X, ALU.add))
            link(dve.reciprocal(rs[A, 1, :], rs[A, 0, :]))
            dve.tensor_tensor(sc4, sc4, rs[A, 1, :].rearrange("p (t h o) -> p t h o", t=NTT, o=1).broadcast_to(
                [TT, NTT, HEADS, TOPK]), ALU.mult).then_inc(s_top, 1)

            dve.wait_ge(s_gh, 1)
            dve.tensor_tensor(gp[:, 1, :], selT[:, 2, :], gp[:, 0, :].bitcast(F32), ALU.subtract).then_inc(s_gh, 1)
            dve.wait_ge(s_gh, 2)
            gpf = gp[:, :, :].bitcast(F32)

            def one_hots(it, s):
                tok = it * 4 + s
                after(dve, s_tok, tok - 3)
                if isinstance(tok, int):
                    col = slice(tok, tok + 1)
                else:
                    col = bass.ds(tok, 1)
                dve.tensor_scalar(ohA[:, s, :], iota[:], selT[:, 0, col], None, ALU.is_equal)
                last = dve.scalar_tensor_tensor(
                    ohB[:, s], iota[:].rearrange("p (o n) -> p o n", o=1).broadcast_to([P, 2, P]), selT[:, 1, col],
                    gpf[:, :, col].broadcast_to([P, 2, P]), ALU.is_equal, ALU.mult)
                last.then_inc(s_oh, 1)

            for s in range(4):
                one_hots(0, s)
            with dve.Fori(1, T // 4) as it:
                for s in range(4):
                    one_hots(it, s)

            def weigh(jj, slot, hslot, gloads, hloads, j):
                dve.wait_ge(s_gl[slot], gloads)
                dve.wait_ge(s_hl[hslot], hloads)
                after(dve, s_wl, j - 1)
                w = wf[:, hslot % 2, :]
                h = hring[:, hslot, :]
                dve.tensor_tensor(w[:, 0:TP].rearrange("p (k t) -> p k t", t=GBLK),
                                  h[:, 0:TP].rearrange("p (k t) -> p k t", t=GBLK),
                                  gbp[:, slot, :, jj, :], ALU.mult)
                dve.tensor_tensor(w[:, TP:T], h[:, TP:T], stages[:, j, :] if isinstance(j, int) else
                                  stages[:, bass.ds(j, 1), :].rearrange("p o t -> p (o t)"), ALU.mult).then_inc(s_w, 1)

            def low(jj, slot, j):
                dve.wait_ge(s_wh, j + 1)
                dve.tensor_tensor(WHL[slot][:, 1, jj, :], wf[:, jj % 2, :], WHL[slot][:, 0, jj, :].bitcast(F32),
                                  ALU.subtract).then_inc(s_wl, 1)

            dve.wait_ge(s_gadd, TP // TOK + 1)
            for j in range(JB):
                weigh(j, 0, j % 4, 16, 16 * (j // 4 + 1), j)
                if j:
                    low(j - 1, 0, j - 1)
            low(JB - 1, 0, JB - 1)

            def add_out(q, steps):
                dve.wait_ge(s_pe, steps)
                residual(q, G2, steps + (KD - NK))

            def second(b2, odd, jj, first, more_w=True):
                j = b2 * 16 + (odd * 8 + jj + 8)
                if more_w:
                    weigh(jj, 1 - odd, jj % 4, b2 * 16 + (16 if odd == 0 else 32),
                          (b2 * 4 + (2 * odd + 2 + jj // 4 + 1)) * 16, j)
                if not first:
                    add_out((jj - 1) % 8, b2 * 16 + (NK + odd * 8 + jj))
                if more_w:
                    low(jj, 1 - odd, j)

            for odd in range(2):
                for jj in range(JB):
                    second(0, odd, jj, odd == 0 and jj == 0)
            last_b2 = NB // 2 - 1
            with dve.Fori(1, last_b2) as b2:
                for odd in range(2):
                    for jj in range(JB):
                        second(b2, odd, jj, False)
            for odd in range(2):
                for jj in range(JB):
                    second(last_b2, odd, jj, False, odd == 0)
            add_out(KD - 1, 2 * NK)
            variance("final", D)
            apply_norm("final", yo, SHF)

        @block.tensor
        def _(pe):
            def tile(n_):
                pe.wait_ge(s_raw[n_ % NRAW], 16 * (n_ // NRAW + 1))

            def modulation_rows(pair, tiles=range(PAIR)):
                for i in tiles:
                    n_ = STREAM.index(("ada", PAIR * pair + i))
                    c, q = divmod(i, KD)
                    tile(n_)
                    if i == 0:
                        after(pe, s_mods, pair)
                    for h in range(2):
                        last = pe.matmul(ps[32 * c:32 * c + 1 + TS, 6 + h, :], sil[:, q, :],
                                         raw[:, n_ % NRAW, h * 512:(h + 1) * 512], start=q == 0, stop=q == KD - 1)
                    last.then_inc(s_mod, 1)

            def modulation_columns(pair):
                pe.wait_ge(s_ade, pair + 1)
                w = 32 + 1 + TS
                for q in range(KD):
                    last = pe.transpose(ps[:, 6, q * w:(q + 1) * w], adaR[0:w, q * P:(q + 1) * P], ident[0:w, 0:w])
                last.then_inc(s_adt, 1)

            def dense(n_, rows, count, bank, sem_):
                tile(n_)
                for q in range(count):
                    for h, (a, b) in enumerate(HALVES):
                        last = pe.matmul(ps[:, bank + h, 0:b - a], raw[:, n_ % NRAW, q * P:(q + 1) * P], rows[:, q, a:b],
                                         start=q == 0, stop=q == count - 1)
                last.then_inc(sem_, 1)

            PASSES = ((0, 0), (0, 1), (1, 0))

            def sum_squares(norm, q):
                pe.wait_ge(s_sq, SQ_BEFORE[norm] + q + 1)
                for h, (a, b) in enumerate(HALVES):
                    last = pe.matmul(ps[:, 4 + h, 0:b - a], ones[:], sq[:, q % 2, a:b], start=q == 0, stop=q == KD - 1)
                last.then_inc(s_squ if q < KD - 1 else s_stat, 1)

            def split_dense(kind, ring, rows, taken, sem_):
                for t in range(3 * CT if kind == "in" else KD):
                    k = FSP[kind] + t
                    pe.wait_ge(s_lo, k + 1)
                    if kind == "in":
                        if 3 <= t < 7:
                            pe.wait_ge(s_uev, t - 2)
                        elif t >= 7:
                            pe.wait_ge(s_hc, (t - 5) // 2)
                    elif t >= 2:
                        pe.wait_ge(taken, t - 1)
                    if kind == "out" and t >= 3:
                        sum_squares("rms2", t - 3)
                    bank = in_bank(t) if kind == "in" else 2 * (t % 2)
                    for i, q in enumerate(K_ORDER[kind]):
                        if kind == "out" and t == 0 and i % CT == 0:
                            pe.wait_ge(s_rl, i // CT + 1)
                        if kind != "out" and t == 0:
                            pe.wait_ge(s_h1l if kind == "in" else s_h2l, i + 2)
                        for w, r in PASSES:
                            for h, (a, b) in enumerate(HALVES):
                                last = pe.matmul(ps[:, bank + h, 0:b - a], ring[:, k % 2, w, q * P:(q + 1) * P],
                                                 rows[r][:, q, a:b], start=i == 0 and (w, r) == (0, 0),
                                                 stop=i == KD - 1 and (w, r) == (1, 0))
                    last.then_inc(sem_, 1)

            K_ORDER = {"out": (4, 5, 6, 7, 0, 1, 2, 3), "q": range(KD), "in": range(KD)}

            def column_sums(rows_of, count, ready, summed):
                for q in range(count):
                    if ready is not None:
                        pe.wait_ge(s_sq, ready + q + 1)
                    r = rows_of(q)
                    for h, (a, b) in enumerate(HALVES):
                        last = pe.matmul(ps[:, 4 + h, 0:b - a], ones[:], r[:, a:b], start=q == 0, stop=q == count - 1)
                    if q < count - 1 and summed:
                        last.then_inc(s_squ, 1)
                last.then_inc(s_stat, 1)

            def sq_rows(q):
                return sq[:, q % 2, :]

            pe.wait_ge(s_sil, 1)
            modulation_rows(0, range(KD))
            pe.wait_ge(s_const, 1)
            column_sums(sq_rows, KD, SQ_BEFORE["rms1"], True)
            modulation_rows(0, range(KD, PAIR))
            modulation_columns(0)
            modulation_rows(1, range(EARLY))
            split_dense("in", hlm, (rhi, h1lo), None, s_win)
            pe.wait_ge(s_Xr, 2)
            pe.wait_ge(s_hc, CT - 1)
            X = (XR, XI)
            for e in range(20):
                if e >= 2:
                    pe.wait_ge(s_prepe, e - 1)
                bank = 4 + e % 2
                if e < 4:
                    for j in range(4):
                        for a in range(2):
                            last = pe.matmul(ps[32 * j:32 * j + 32, bank, 0:MQ],
                                             Cbd[:, a, 4 * e + j].rearrange("p g q -> p (g q)"),
                                             X[a][:, 4 * e + j].rearrange("p m q -> p (m q)"), start=a == 0, stop=a == 1)
                elif e < 12:
                    for j in range(4):
                        last = pe.transpose(ps[:, bank, j * P:(j + 1) * P],
                                            X[(e - 4) // 4][:, 4 * (e % 4) + j, 0:L, :].rearrange("p m q -> p (m q)"), ident[:])
                else:
                    n4, ih = divmod(e - 12, 2)
                    for j in range(4):
                        m = L - 1 - (4 * ih + j)
                        last = pe.transpose(ps[:, bank, j * P:(j + 1) * P], Kt[:, n4, m * SQ:m * SQ + P], ident[:])
                last.then_inc(s_prep, 1)
            pe.wait_ge(s_prepe, 20)
            pe.wait_ge(s_hc, CT)
            pe.wait_ge(s_ul, 16 * (L + 2))
            for t in range(ST):
                for g in range(2):
                    for a in range(2):
                        c = (t % 6) * (NC + 2 * TS)
                        last = pe.matmul(ps[64 * g:64 * g + 64, 3 * a + t // 6, c:c + NC + 2 * TS],
                                         ET[:, a, t, 64 * g:64 * g + 64], U[:, 2 * t + g, :], start=True, stop=True)
            last.then_inc(s_V, 1)
            modulation_rows(1, range(EARLY, PAIR))
            modulation_columns(1)
            pe.wait_ge(s_S, 1)
            pe.wait_ge(s_Fr, 1)
            pe.wait_ge(s_Ve, 6)
            for g in range(2):
                rows = slice(64 * g, 64 * g + 64)
                if g == 1:
                    pe.wait_ge(s_mods, 2)
                for t in range(ST):
                    o = ps[0:NC + TS, 4 * g + t // 4, (t % 4) * P:(t % 4 + 1) * P]
                    pe.matmul(o, U[:, 2 * t + g, 0:NC + TS], Tm[:, 2 * t + g, :], start=True, stop=False)
                    for a in range(2):
                        last = pe.matmul(o, S[rows, a, t], FO[rows, a, t].rearrange("p i q -> p (i q)"),
                                         start=False, stop=a == 1)
                last.then_inc(s_Y, 1)
            pe.wait_ge(s_dg, CT)
            for t in range(CT):
                pe.wait_ge(s_Ye, 2 * t + 2)
                for h in range(2):
                    o = ps[:, 4 * h + t, 0:4 * (NC + TS)].rearrange("p (i c) -> p i c", i=4)
                    if h == 0:
                        pe.matmul(o[:, 0, NC:NC + TS], dskip[:, t, :], uT[:, t, TP:T], start=True, stop=False)
                        pe.matmul(o[:, 0, NC:NC + TS], Ysb[:, t, 0, :], ident[0:NC + TS, NC:NC + TS], start=False, stop=True)
                    pe.matmul(o[:, :, 0:NC], dskip[:, t, :], uT[:, t, h * 256:(h + 1) * 256], start=True, stop=False)
                    for i in range(4):
                        last = pe.matmul(o[:, i, 0:NC], Ysb[0:NC, t, 4 * h + i, :], ident[0:NC, 0:NC],
                                         start=False, stop=i == 3)
                last.then_inc(s_yt, 1)
            pe.wait_ge(s_z, CT)
            for w in range(CT):
                if w >= 2:
                    pe.wait_ge(s_gsig, w - 1)
                dense(FIRST["glu"] + w, yT, CT, 2 * (w % 2), s_glu)
            modulation_rows(2)
            modulation_columns(2)
            pe.wait_ge(s_cv, CT * CW + 1)
            column_sums(lambda q: cv[:, q, :], CT, None, False)
            column_sums(sq_rows, CT, SQ_BEFORE["conv"], True)
            modulation_rows(3, range(LATE))
            split_dense("out", hlm, (rhi, mixlo), s_x1, s_mix)
            for q in range(KD - 3, KD):
                sum_squares("rms2", q)
            modulation_rows(3, range(LATE, PAIR))
            split_dense("q", hl, (h2[:, 0], h2[:, 1]), s_qe, s_q)
            modulation_columns(3)
            pe.wait_ge(s_keys, 32)
            pe.wait_ge(s_qe, KD)
            pe.wait_ge(s_mods, 4)
            for t in range(NTT):
                if t >= 2:
                    pe.wait_ge(s_act, t - 1)
                for h in range(HEADS):
                    last = pe.matmul(ps[0:TT, 4 * (1 - t % 2) + h // 2, (h % 2) * 2 * NK:(h % 2 + 1) * 2 * NK],
                                     qT[:, h, t * TT:(t + 1) * TT], keys[:, h].rearrange("p s n -> p (s n)"),
                                     start=True, stop=True)
                last.then_inc(s_sc, 1)

            def token(step, w, tok):
                if w % 2 == 0:
                    pe.wait_ge(s_gev, step * 4 + (3 + w // 2))
                pe.wait_ge(s_oh, tok + 1)
                pe.matmul(ps[:, 4 + w // 2, (w % 2) * 2 * NK:(w % 2 + 1) * 2 * NK], ohA[:, w % 4, :],
                          ohB[:, w % 4].rearrange("p a n -> p (a n)"), start=True, stop=True).then_inc(s_tok, 1)

            def first_product(s, m, step=None):
                pe.wait_ge(s_lo, m + (NSP + 1))
                pe.wait_ge(s_act, m + (NTT - 1))
                for q in range(KD):
                    for w, r in PASSES:
                        for h, (a, b) in enumerate(HALVES):
                            last = pe.matmul(ps[:, 2 * s + h, 0:b - a], hl[:, s, w, q * P:(q + 1) * P], h2[:, r, q, a:b],
                                             start=q == 0 and (w, r) == (0, 0), stop=q == KD - 1 and (w, r) == (1, 0))
                    if step is not None and q < KD - 1:
                        token(step, q, step * TOK + q)
                last.then_inc(s_pe, 1)
                if step is not None:
                    token(step, TOK - 1, step * TOK + TOK - 1)

            with pe.Fori(0, A1 // 2 - 1) as it:
                for s in range(2):
                    first_product(s, it * 2 + s)
            pe.wait_ge(s_top, 1)
            pe.wait_ge(s_act, NTT)
            for kind in range(3):
                for t in range(NTT):
                    o = ps[:, 4 + kind, t * TT:(t + 1) * TT] if t < 4 else ps[:, 7, kind * TT:(kind + 1) * TT]
                    last = pe.transpose(o, selv[0:TT, t, kind, :], ident[0:TT, 0:TT])
            last.then_inc(s_selp, 1)
            for m in range(A1 - 2, A1):
                first_product(m % 2, m)
            with pe.Fori(0, TP // TOK // 2) as it:
                for s in range(2):
                    first_product(s, it * 2 + (A1 + s), it * 2 + s)
            first_product(0, NK - A3, TP // TOK)
            for m in range(NK - A3 + 1, NK):
                first_product(m % 2, m)

            def second_product(b2, odd, s, mm):
                pe.wait_ge(s_wl, b2 * 16 + 8 * (odd + 1))
                pe.wait_ge(s_lo, mm + (NSP + NK + 1))
                pe.wait_ge(s_x1, mm + (KD - 1))
                for j in range(JB):
                    for w, r in PASSES:
                        for h, (a, b) in enumerate(HALVES):
                            last = pe.matmul(ps[:, 2 * s + h, 0:b - a], hl[:, s, w, j * P:(j + 1) * P],
                                             WHL[odd][:, r, j, a:b],
                                             start=j == 0 and (w, r) == (0, 0), stop=j == JB - 1 and (w, r) == (1, 0))
                last.then_inc(s_pe, 1)

            pe.wait_ge(s_act, NTT + NK)
            with pe.Fori(0, NB // 2 - 1) as b2:
                for odd in range(2):
                    with pe.Fori(0, JB // 2) as i2:
                        for s in range(2):
                            second_product(b2, odd, s, b2 * 16 + i2 * 2 + (odd * 8 + s))
            with pe.Fori(0, JB // 2) as i2:
                for s in range(2):
                    second_product(NB // 2 - 1, 0, s, i2 * 2 + (NK - 16 + s))
            for q in range(KD):
                if q >= 3:
                    sum_squares("final", q - 3)
                second_product(NB // 2 - 1, 1, q % 2, NK - 8 + q)
            for q in range(KD - 3, KD):
                sum_squares("final", q)


_OUTS = {"y": (P, KD, T), "conv_p": (P, CT, CW - 1), "conv_s": (P, CT, TS, CW - 1),
         "ssm_p": (P, 2, ST), "ssm_s": (P, 2, ST, TS)}


def layout(i):
    import numpy as np

    def cols(prompt, sample):
        chunked = prompt.reshape(NC, L, D).transpose(1, 0, 2).reshape(TP, D)
        return np.concatenate([chunked, sample], 0).T.reshape(KD, P, T).transpose(1, 0, 2)

    def tiles(w):
        k, n = w.shape
        return w.reshape(k // P, P, n // P, P).transpose(2, 1, 0, 3).reshape(n // P, P, k)

    def slabs(w):
        k, n = w.shape
        return w.reshape(k // P, P, n // RAW, RAW).transpose(2, 0, 1, 3).reshape(-1, P, RAW)

    def per_partition(v):
        return v.reshape(-1, P).T

    def states(v):
        return v.reshape(ST, P, -1).transpose(1, 0, 2)

    a = {
        "x": cols(i["x_prompt"][0], i["x_sample"][:, 0]),
        "cT": np.concatenate([i["c_prompt"], i["c_sample"]], 0).T.reshape(KD, P, 1 + TS).transpose(1, 0, 2),
        "par": np.stack([per_partition(i["ssm_lambda_re"][0].reshape(-1)), per_partition(i["ssm_lambda_im"][0].reshape(-1)),
                         per_partition(np.repeat(i["ssm_log_dt"][0], SN))], 1),
        "bm": np.stack([states(i["ssm_b_re"][0]), states(i["ssm_b_im"][0])], 1),
        "cm": np.stack([states(i["ssm_c_re"][0].transpose(0, 2, 1)), states(i["ssm_c_im"][0].transpose(0, 2, 1))], 1),
        "h0": np.stack([states(i[n][0].reshape(TS, SG * SN).T) for n in ("state_ssm_re", "state_ssm_im")], 1),
        "stc": i["state_conv"][0].transpose(2, 0, 1).reshape(CT, P, TS, CW - 1).transpose(1, 0, 2, 3),
        "cw": i["conv_w"][0].T.reshape(CT, P, CW).transpose(1, 0, 2),
        "cvec": np.stack([per_partition(i[n][0]) for n in ("conv_b", "conv_ln_g", "conv_ln_b", "ssm_d")], 1),
        "bada": np.concatenate([per_partition(i["b_ada"][0]), per_partition(i["b_ada_final"])], 1),
        "ngain": np.stack([per_partition(v) for v in (i["norm1_g"][0], i["norm2_g"][0], i["final_norm_g"])], 1),
        "w_ada": np.concatenate([slabs(i["w_ada"][0]), slabs(i["w_ada_final"])], 0),
        "w_in": tiles(i["w_in"][0]),
        "w_glu": tiles(i["ssm_w_glu"][0]),
        "w_out": tiles(i["w_out"][0]),
        "w_q": tiles(i["peer_w_q"][0]),
        "keys": i["peer_keys"][0].transpose(1, 3, 0, 2).reshape(P, HEADS, NK),
        "u": i["peer_u"][0].reshape(P, NK, KD, P).transpose(1, 3, 2, 0).reshape(NK, P, RAW),
        "v": i["peer_v"][0].reshape(P, NB, JB, KD, P).transpose(1, 3, 0, 2, 4).reshape(NB * KD, P, RAW),
    }
    return {n: np.ascontiguousarray(v) for n, v in a.items()}


def kernel(**inputs):
    import numpy as np
    import concourse.bacc as bacc
    from concourse.bass_utils import run_bass_kernel_spmd

    inputs = {n: np.asarray(v) for n, v in inputs.items()}
    nc = bacc.Bacc("TRN2", target_bir_lowering=False, num_devices=1)
    arrays = layout(inputs)
    dr = {n: nc.dram_tensor(f"in_{n}", a.shape, F32, kind="ExternalInput").ap() for n, a in arrays.items()}
    out = {n: nc.dram_tensor(f"out_{n}", s, F32, kind="ExternalOutput").ap() for n, s in _OUTS.items()}
    build(nc, dr, out)
    r = run_bass_kernel_spmd(nc, [{f"in_{n}": a for n, a in arrays.items()}], core_ids=[0]).results[0]
    y = r["out_y"].transpose(1, 0, 2).reshape(D, T).T
    y_prompt = y[:TP].reshape(L, NC, D).transpose(1, 0, 2).reshape(1, TP, D)
    conv_p = r["out_conv_p"].transpose(2, 1, 0).reshape(1, 1, CW - 1, CC)
    conv_s = r["out_conv_s"].transpose(2, 3, 1, 0).reshape(1, TS, CW - 1, CC)
    ssm_p = r["out_ssm_p"].transpose(1, 2, 0).reshape(2, 1, 1, SG, SN)
    ssm_s = r["out_ssm_s"].transpose(1, 3, 2, 0).reshape(2, 1, TS, SG, SN)
    c = np.ascontiguousarray
    return (c(y_prompt), c(y[TP:].reshape(TS, 1, D)), c(conv_p), c(conv_s), c(ssm_p[0]), c(ssm_p[1]), c(ssm_s[0]), c(ssm_s[1]))
```
